# Optimizing a Trainium2 kernel written in Bass

```python
import math
import jax, jax.numpy as jnp
from jax import lax
import numpy as np

D_MODEL = 1024
BATCH = 1
SEQ = 512
DEPTH = 1

CHUNK = 64
PLE_DIM = 256
POOL_WIDTH = D_MODEL // 4
POOL_GROUPS = 4
POOL_GROUP_DIM = POOL_WIDTH // POOL_GROUPS
POOL_WINDOWS = (2, 4, 8, 16)
ATTN_HEAD_DIM = 64
ATTN_HEADS = (3 * D_MODEL // 8) // ATTN_HEAD_DIM
ATTN_WIDTH = ATTN_HEADS * ATTN_HEAD_DIM
N_PREV_CHUNKS = 8
BAND_CHUNKS = N_PREV_CHUNKS + 1
REL_CLIP = 128
SSM_WIDTH = D_MODEL - POOL_WIDTH - ATTN_WIDTH
SSM_GROUP_DIM = 16
SSM_GROUPS = SSM_WIDTH // SSM_GROUP_DIM
SSM_STATE = 64
MIX_WIDTH = POOL_WIDTH + ATTN_WIDTH + SSM_WIDTH
IN_PROJ_WIDTH = POOL_WIDTH + 3 * ATTN_WIDTH + SSM_WIDTH
N_EXPERTS = 16
N_EXPERT_GROUPS = 4
EXPERTS_PER_GROUP = N_EXPERTS // N_EXPERT_GROUPS
TOP_K = 2
D_EXPERT = D_MODEL // 4
DN_ALPHA = (2 * DEPTH) ** 0.25
DN_BETA = (8 * DEPTH) ** -0.25
NORM_EPS = 1e-5

kernel_name = 'hybrid_pool_chunkattn_s5_grouped_moe'

def layer_norm(x, g, b):
    xf = x.astype(jnp.float32)
    mu = jnp.mean(xf, axis=-1, keepdims=True)
    xc = xf - mu
    var = jnp.mean(xc * xc, axis=-1, keepdims=True)
    y = xc * lax.rsqrt(var + NORM_EPS) * g.astype(jnp.float32) + b.astype(jnp.float32)
    return y.astype(x.dtype)

def rms_norm(x, g):
    xf = x.astype(jnp.float32)
    y = xf * lax.rsqrt(jnp.mean(xf * xf, axis=-1, keepdims=True) + NORM_EPS) * g.astype(jnp.float32)
    return y.astype(x.dtype)

def pool_mixer(u, w_pool, pool_scale):
    b, l, _ = u.shape
    ug = u.reshape(b, l, POOL_GROUPS, POOL_GROUP_DIM).astype(jnp.float32)
    cs = jnp.concatenate([jnp.zeros_like(ug[:, :1]), jnp.cumsum(ug, axis=1)], axis=1)
    pos = jnp.arange(l)
    outs = []
    for g, w in enumerate(POOL_WINDOWS):
        lo = jnp.maximum(pos + 1 - w, 0)
        cnt = jnp.minimum(pos + 1, w).astype(jnp.float32)
        mean = (cs[:, 1:, g] - cs[:, lo, g]) / cnt[None, :, None]
        outs.append(mean - ug[:, :, g])
    d = jnp.stack(outs, axis=2).astype(u.dtype)
    y = jnp.einsum('blgc,gce->blge', d, w_pool)
    return y.reshape(b, l, POOL_WIDTH) * pool_scale

def rel_bias_matrix(rel_bias):
    qi = jnp.arange(CHUNK)[:, None]
    kk = jnp.arange(BAND_CHUNKS * CHUNK)[None, :]
    rel = N_PREV_CHUNKS * CHUNK + qi - kk
    idx = jnp.clip(rel, -REL_CLIP, REL_CLIP) + REL_CLIP
    return rel_bias[:, idx]

def chunk_band(t, nc):
    tp = jnp.pad(t, ((0, 0), (N_PREV_CHUNKS, 0), (0, 0), (0, 0), (0, 0)))
    return jnp.concatenate([tp[:, j:j + nc] for j in range(BAND_CHUNKS)], axis=2)

def chunk_attention(q, k, v, rel_bias):
    b, l, _ = q.shape
    nc = l // CHUNK
    shp = (b, nc, CHUNK, ATTN_HEADS, ATTN_HEAD_DIM)
    q = q.reshape(shp)
    kb = chunk_band(k.reshape(shp), nc)
    vb = chunk_band(v.reshape(shp), nc)
    s = jnp.einsum('bnqhd,bnkhd->bnhqk', q, kb).astype(jnp.float32) * (ATTN_HEAD_DIM ** -0.5)
    s = s + rel_bias_matrix(rel_bias).astype(jnp.float32)[None, None]
    key_chunk = jnp.arange(nc)[:, None] - N_PREV_CHUNKS + jnp.arange(BAND_CHUNKS * CHUNK)[None, :] // CHUNK
    s = jnp.where((key_chunk >= 0)[None, :, None, None, :], s, -jnp.inf)
    pr = jax.nn.softmax(s, axis=-1).astype(vb.dtype)
    o = jnp.einsum('bnhqk,bnkhd->bnqhd', pr, vb)
    return o.reshape(b, l, ATTN_WIDTH)

def _complex_affine_combine(e1, e2):
    a1r, a1i, b1r, b1i = e1
    a2r, a2i, b2r, b2i = e2
    return (a2r * a1r - a2i * a1i,
            a2r * a1i + a2i * a1r,
            a2r * b1r - a2i * b1i + b2r,
            a2r * b1i + a2i * b1r + b2i)

def s5_mixer(u, a_re, a_im, log_dt, b_re, b_im, c_re, c_im, d_skip, w_glu, b_glu):
    f32 = jnp.float32
    bsz, l, _ = u.shape
    ug = u.reshape(bsz, l, SSM_GROUPS, SSM_GROUP_DIM).astype(f32)
    dt = jnp.exp(log_dt.astype(f32))[:, None]
    ar = a_re.astype(f32)
    ai = a_im.astype(f32)
    mag = jnp.exp(ar * dt)
    abar_re = mag * jnp.cos(ai * dt)
    abar_im = mag * jnp.sin(ai * dt)
    den = ar * ar + ai * ai
    nr = abar_re - 1.0
    ni = abar_im
    coef_re = ((nr * ar + ni * ai) / den)[..., None]
    coef_im = ((ni * ar - nr * ai) / den)[..., None]
    br = b_re.astype(f32)
    bi = b_im.astype(f32)
    bbar_re = coef_re * br - coef_im * bi
    bbar_im = coef_re * bi + coef_im * br
    bu_re = jnp.einsum('blgh,gph->blgp', ug, bbar_re)
    bu_im = jnp.einsum('blgh,gph->blgp', ug, bbar_im)
    shape = bu_re.shape
    elems = (jnp.broadcast_to(abar_re, shape), jnp.broadcast_to(abar_im, shape), bu_re, bu_im)
    _, _, s_re, s_im = lax.associative_scan(_complex_affine_combine, elems, axis=1)
    y = (jnp.einsum('blgp,ghp->blgh', s_re, c_re.astype(f32))
         - jnp.einsum('blgp,ghp->blgh', s_im, c_im.astype(f32)))
    y = y + d_skip.astype(f32).reshape(SSM_GROUPS, SSM_GROUP_DIM) * ug
    y = jax.nn.gelu(y.reshape(bsz, l, SSM_WIDTH)).astype(u.dtype)
    return y * jax.nn.sigmoid(y @ w_glu + b_glu)

def route(h, w_router, router_bias):
    scores = jax.nn.sigmoid((h @ w_router).astype(jnp.float32))
    biased = scores + router_bias.astype(jnp.float32)
    grouped = biased.reshape(*biased.shape[:-1], N_EXPERT_GROUPS, EXPERTS_PER_GROUP)
    group_score = lax.top_k(grouped, TOP_K)[0].sum(-1)
    top_group = jnp.argmax(group_score, axis=-1)
    expert_group = jnp.arange(N_EXPERTS) // EXPERTS_PER_GROUP
    in_group = expert_group == top_group[..., None]
    masked = jnp.where(in_group, biased, -jnp.inf)
    _, idx = lax.top_k(masked, TOP_K)
    w = jnp.take_along_axis(scores, idx, axis=-1)
    w = w / jnp.sum(w, axis=-1, keepdims=True)
    combine = jnp.sum(jax.nn.one_hot(idx, N_EXPERTS, dtype=jnp.float32) * w[..., None], axis=-2)
    return combine

def moe(h, combine, w_gate, w_up, w_down):
    out = jnp.zeros_like(h)
    for e in range(N_EXPERTS):
        a = jax.nn.silu(h @ w_gate[e]) * (h @ w_up[e])
        out = out + combine[..., e:e + 1].astype(h.dtype) * (a @ w_down[e])
    return out

def setup_inputs(seed: int = 0) -> dict:
    key = jax.random.key(seed)
    ks = jax.random.split(key, 32)
    f32 = jnp.float32
    nrm = lambda k, shape, s: jax.random.normal(k, shape, f32) * s
    L = DEPTH
    return {
        'x': nrm(ks[0], (BATCH, SEQ, D_MODEL), 1.0),
        'p': nrm(ks[1], (DEPTH, BATCH, SEQ, PLE_DIM), 1.0),
        'w_in': nrm(ks[2], (L, D_MODEL, IN_PROJ_WIDTH), D_MODEL ** -0.5),
        'w_out': nrm(ks[3], (L, MIX_WIDTH, D_MODEL), DN_BETA * MIX_WIDTH ** -0.5),
        'w_pool': nrm(ks[4], (L, POOL_GROUPS, POOL_GROUP_DIM, POOL_GROUP_DIM), POOL_GROUP_DIM ** -0.5),
        'pool_scale': 1.0 + nrm(ks[5], (L, POOL_WIDTH), 0.1),
        'rel_bias': nrm(ks[6], (L, ATTN_HEADS, 2 * REL_CLIP + 1), 0.1),
        'ssm_a_re': -0.5 + nrm(ks[7], (L, SSM_GROUPS, SSM_STATE), 0.01),
        'ssm_a_im': math.pi * jnp.arange(SSM_STATE, dtype=f32)[None, None, :] + nrm(ks[8], (L, SSM_GROUPS, SSM_STATE), 0.01),
        'ssm_log_dt': jax.random.uniform(ks[9], (L, SSM_GROUPS), f32, math.log(1e-3), math.log(1e-1)),
        'ssm_b_re': nrm(ks[10], (L, SSM_GROUPS, SSM_STATE, SSM_GROUP_DIM), (2 * SSM_GROUP_DIM) ** -0.5),
        'ssm_b_im': nrm(ks[11], (L, SSM_GROUPS, SSM_STATE, SSM_GROUP_DIM), (2 * SSM_GROUP_DIM) ** -0.5),
        'ssm_c_re': nrm(ks[12], (L, SSM_GROUPS, SSM_GROUP_DIM, SSM_STATE), (2 * SSM_STATE) ** -0.5),
        'ssm_c_im': nrm(ks[13], (L, SSM_GROUPS, SSM_GROUP_DIM, SSM_STATE), (2 * SSM_STATE) ** -0.5),
        'ssm_d': nrm(ks[14], (L, SSM_WIDTH), 1.0),
        'w_glu': nrm(ks[15], (L, SSM_WIDTH, SSM_WIDTH), SSM_WIDTH ** -0.5),
        'b_glu': nrm(ks[16], (L, SSM_WIDTH), 0.02),
        'g_pool': 1.0 + nrm(ks[17], (L, POOL_WIDTH), 0.05),
        'g_attn': 1.0 + nrm(ks[18], (L, ATTN_WIDTH), 0.05),
        'g_ssm': 1.0 + nrm(ks[19], (L, SSM_WIDTH), 0.05),
        'ln1_g': 1.0 + nrm(ks[20], (L, D_MODEL), 0.05),
        'ln1_b': nrm(ks[21], (L, D_MODEL), 0.02),
        'ln2_g': 1.0 + nrm(ks[22], (L, D_MODEL), 0.05),
        'ln2_b': nrm(ks[23], (L, D_MODEL), 0.02),
        'w_router': nrm(ks[24], (D_MODEL, N_EXPERTS), D_MODEL ** -0.5),
        'router_bias': nrm(ks[25], (N_EXPERTS,), 0.01),
        'w_exp_gate': nrm(ks[26], (L, N_EXPERTS, D_MODEL, D_EXPERT), D_MODEL ** -0.5),
        'w_exp_up': nrm(ks[27], (L, N_EXPERTS, D_MODEL, D_EXPERT), D_MODEL ** -0.5),
        'w_exp_down': nrm(ks[28], (L, N_EXPERTS, D_EXPERT, D_MODEL), DN_BETA * D_EXPERT ** -0.5),
        'w_ple_gate': nrm(ks[29], (L, D_MODEL, D_MODEL), D_MODEL ** -0.5),
        'w_ple_proj': nrm(ks[30], (L, PLE_DIM, D_MODEL), DN_BETA * PLE_DIM ** -0.5),
    }

def reference(x, p, w_in, w_out, w_pool, pool_scale, rel_bias, ssm_a_re, ssm_a_im, ssm_log_dt,
              ssm_b_re, ssm_b_im, ssm_c_re, ssm_c_im, ssm_d, w_glu, b_glu, g_pool, g_attn, g_ssm,
              ln1_g, ln1_b, ln2_g, ln2_b, w_router, router_bias, w_exp_gate, w_exp_up, w_exp_down,
              w_ple_gate, w_ple_proj):
    splits = [POOL_WIDTH, POOL_WIDTH + ATTN_WIDTH, POOL_WIDTH + 2 * ATTN_WIDTH, POOL_WIDTH + 3 * ATTN_WIDTH]
    for i in range(DEPTH):
        z = x @ w_in[i]
        u_pool, q, k, v, u_ssm = jnp.split(z, splits, axis=-1)
        y_pool = pool_mixer(u_pool, w_pool[i], pool_scale[i])
        y_attn = chunk_attention(q, k, v, rel_bias[i])
        y_ssm = s5_mixer(u_ssm, ssm_a_re[i], ssm_a_im[i], ssm_log_dt[i], ssm_b_re[i], ssm_b_im[i],
                         ssm_c_re[i], ssm_c_im[i], ssm_d[i], w_glu[i], b_glu[i])
        heads = jnp.concatenate([rms_norm(y_pool, g_pool[i]), rms_norm(y_attn, g_attn[i]),
                                 rms_norm(y_ssm, g_ssm[i])], axis=-1)
        h = layer_norm(DN_ALPHA * x + heads @ w_out[i], ln1_g[i], ln1_b[i])
        combine = route(h, w_router, router_bias)
        ffn = moe(h, combine, w_exp_gate[i], w_exp_up[i], w_exp_down[i])
        ple = jax.nn.sigmoid(h @ w_ple_gate[i]) * (p[i] @ w_ple_proj[i])
        x = layer_norm(DN_ALPHA * h + ffn + ple, ln2_g[i], ln2_b[i])
    return x


_drawn_inputs = setup_inputs


def setup_inputs(seed=0):
    import zlib

    import numpy as np

    out = dict(_drawn_inputs(seed))
    spreads = {}
    factors = {}
    for name, (base, spread) in spreads.items():
        noise = np.random.default_rng([zlib.crc32(name.encode()), seed]).standard_normal(out[name].shape)
        drawn = base * np.exp(spread * noise) if base else spread * noise
        out[name] = __import__('jax').numpy.asarray(drawn.astype(out[name].dtype))
    for name, factor in factors.items():
        out[name] = (out[name] * factor).astype(out[name].dtype)
    return out
```

```python
from contextlib import ExitStack

import numpy as np

import concourse.bass as bass
from concourse import mybir

F32 = mybir.dt.float32
I32 = mybir.dt.int32
ALU = mybir.AluOpType
ACT = mybir.ActivationFunctionType
AX = mybir.AxisListType

P = 128
D = 1024
T = 512
NT = T // P
KD = D // P
POOL_W, ATT_W, SSM_W = 256, 384, 384
IN_W = POOL_W + 3 * ATT_W + SSM_W
HEADS, HD = 6, 64
REL = 128
G, GD, NS = 24, 16, 64
CH = 8
NC = T // CH
Q = G // 2
NE, DE = 16, 256
EG, EPG = 4, 4
PLE = 256
ALPHA = 2.0 ** 0.25
EPS = 1e-5
NEG = -1.0e30
BIG = 3.0e38
CAP = P
OVER = 7
SLOT_TILES = NE + OVER
PAD = 4096
ROUND = 1.5 * 2.0 ** 23
PI2_A = 6.28125
PI2_B = 0.00193500518798828125
PI2_C = float(2 * np.pi - PI2_A - PI2_B)
PI_SAFE = 3.1415925

NG = Q + G
C_ARE, C_AIM, C_LDT = 0, NG, 2 * NG
C_BRE = 3 * NG
C_BIM = C_BRE + NG * GD
C_CA = C_BIM + NG * GD
C_CB = C_CA + G * GD
SSM_COLS = C_CB + G * GD
V_D, V_BG, V_GAIN, V_PS, V_RB, V_RC = 0, 3, 6, 14, 16, 32
VEC_COLS = 38

SCORE_AT = {0: (0, 0, 0), 2: (0, 128, 128), 3: (1, 0, 512), 1: (2, 0, 1024)}
WO_AT = (0, 2, 4, 2)
PT_AT = {0: 0, 1: 512, 3: 896, 2: 1024}
PT_UNITS = [((0,), 0, 512), ((1, 3), 512, 512), ((2,), 1024, 256)]


def trunk(nc, io, out):
    with ExitStack() as ctx:
        def sb(name, shape, dt=F32):
            return ctx.enter_context(nc.sbuf_tensor(name, shape, dt))

        def sem(name):
            return ctx.enter_context(nc.semaphore(name))

        RA = sb("region_a", [P, 14336])
        RB = sb("region_b", [P, 8192])
        RC = sb("region_c", [P, 9600])
        RE = sb("region_e", [P, 4096])
        RF = sb("region_f", [P, 4096])
        RG = sb("region_g", [P, 4096])
        RH = sb("region_h", [P, 7680])
        ident = sb("ident", [P, P])
        ones = sb("ones", [P, P])
        tri = sb("tri", [P, P])
        vec = sb("vec", [P, VEC_COLS])
        w_rt = sb("w_rt", [P, KD, NE])
        w_pl = sb("w_pl", [P, 2, P])
        ln_st = sb("ln_st", [P, NT, 12])
        ln_mv = sb("ln_mv", [P, NT, 2])
        ln_rs = sb("ln_rs", [P, NT, 2])
        att_mx = sb("att_mx", [P, 2, 4])
        att_sm = sb("att_sm", [P, 2, 4])

        O_SSM, O_Q, O_K, O_V, O_PL = 0, KD * 384, KD * 768, KD * 1152, KD * 1536
        w_ssm = RA[:, O_SSM:O_SSM + KD * 384].rearrange("p (k n) -> p k n", k=KD)
        w_q = RA[:, O_Q:O_Q + KD * 384].rearrange("p (k n) -> p k n", k=KD)
        w_k = RA[:, O_K:O_K + KD * 384].rearrange("p (k n) -> p k n", k=KD)
        w_v = RA[:, O_V:O_V + KD * 384].rearrange("p (k n) -> p k n", k=KD)
        w_up = RA[:, O_PL:O_PL + KD * 256].rearrange("p (k n) -> p k n", k=KD)
        prob = RA[:, 0:2560].rearrange("p (r n) -> p r n", r=2)
        probT = RA[:, 2560:5120].rearrange("p (r n) -> p r n", r=2)
        w_glu = RA[:, 5120:6272].rearrange("p (k n) -> p k n", k=3)
        rcnt = RA[:, 6272:7296].rearrange("p (k n) -> p k n", k=2)
        s_in = RA[:, 7296:8832].rearrange("p (g c) -> p g c", g=G)
        x_rot = RA[:, 8832:10368].rearrange("p (r n) -> p r n", r=2)
        y_ch = RA[:, 8832:10368].rearrange("p (g c) -> p g c", g=G)
        sgl = RA[:, 8832:10368].rearrange("p (m t) -> p m t", m=3)
        x_tmp = RA[:, 10368:11904].rearrange("p (r n) -> p r n", r=2)
        yT = RA[:, 10368:11904].rearrange("p (m t) -> p m t", m=3)
        pl_s = RA[:, 12288:14336].rearrange("p (r m t) -> p r m t", r=2, m=2)
        rstdB = RA[:, 12288:13824].rearrange("p (g t) -> p g t", g=3)
        par = RB[:, 0:SSM_COLS]
        bb = RB[:, 2028:3180].rearrange("p (r g h) -> p r g h", r=2, g=NG)
        b_st = RB[:, 3180:3564].rearrange("p (g h) -> p g h", g=G)
        tmp = RB[:, 3564:7020]
        pw = RB[:, 7020:7668].rearrange("p (r g l) -> p r g l", r=2, g=NG)
        sm = RB[:, 7668:8192]
        w_o = RB[:, :].rearrange("p (k n) -> p k n", k=KD)
        bx = RC[:, 0:3072].rearrange("p (r q j h) -> p r q j h", r=2, q=Q, j=CH)
        kern = RC[0:GD, 0:3072].rearrange("p (g l h) -> p g l h", g=G, l=CH)
        bxT = RC[:, 3072:6144].rearrange("p (r q s) -> p r q s", r=2, q=Q)
        cp = RC[:, 6144:9600].rearrange("p (g l h) -> p g l h", g=G, l=CH + 1)
        w_pg = RC[:, 0:8192].rearrange("p (k n) -> p k n", k=KD)
        rt = RC[:, 8192:9600]
        act_e = RC[:, 6144:7680].rearrange("p (r s n) -> p r s n", r=2, s=3)
        xT = RE[:, :].rearrange("p (k t) -> p k t", k=KD)
        hdT = RE[:, :].rearrange("p (k t) -> p k t", k=KD)
        hg = RE[:, :].rearrange("p (r n) -> p r n", r=4)
        rbias = RF[:, 0:1536].rearrange("p (h n) -> p h n", h=HEADS)
        rot = RF[:, 1536:3096].rearrange("p (r q c) -> p r q c", r=2, q=Q)
        decay = RF[:, 3096:3864]
        xh = RF[:, :].rearrange("p (t d) -> p t d", t=NT)
        qT = RG[:, 0:1536].rearrange("p (m t) -> p m t", m=3)
        kT = RG[:, 1536:3072].rearrange("p (m t) -> p m t", m=3)
        plT = RG[:, 3072:4096].rearrange("p (m t) -> p m t", m=2)
        hT = RG[:, :].rearrange("p (k t) -> p k t", k=KD)
        hgT = RG[:, 0:2048].rearrange("p (r k s) -> p r k s", r=2, k=KD)
        y_e = [RG[:, 2048:3072], RG[:, 3072:4096], RB[:, 6144:7168], RB[:, 7168:8192]]
        uT = RH[:, 0:1536].rearrange("p (m t) -> p m t", m=3)
        uch = RH[:, 1536:3072].rearrange("p (g c) -> p g c", g=G)
        m0 = RH[:, 3072:6144].rearrange("p (g l h) -> p g l h", g=G, l=CH)
        vN = RH[:, 6144:7680].rearrange("p (t n) -> p t n", t=NT)
        w_pp = RH[:, 0:2048].rearrange("p (k n) -> p k n", k=2)
        pT = RH[:, 2048:3072].rearrange("p (k t) -> p k t", k=2)
        lng = RH[:, 3072:4096]
        lnb = RH[:, 4096:5120]
        ple_t = RH[:, 5120:6144]
        sq2 = RH[:, 6144:7168].rearrange("p (r n) -> p r n", r=2)
        ebuf = [RA[:, 0:6144], RA[:, 6144:12288], RB[:, 0:6144], RC[:, 0:6144]]

        bank = [ctx.enter_context(nc.psum_tensor(f"bank{i}", [P, 512], F32)) for i in range(8)]

        def dram(name, shape, dt=F32):
            return nc.dram_tensor(name, shape, dt, kind="Internal").ap()
        u_d = dram("u_scratch", (SSM_W, T))
        y_d = dram("y_scratch", (SSM_W, T))
        h_d = dram("h_scratch", (T, D))
        inv_d = dram("slot_scratch", (SLOT_TILES * P, 1), I32)
        ye_d = dram("expert_scratch", (2 * T, D))

        dt_, expo, ang, turns, angr, sinf, sinh = (
            sm[:, lo:lo + w] for lo, w in ((0, 36), (36, 48), (84, 48), (132, 48), (180, 48), (228, 48), (276, 48)))
        u8 = sm[:, 324:348].rearrange("p (r q) -> p r q", r=2)
        mag8 = sm[:, 348:360]
        r_s = rt[:, 0:NT * NE]
        r_sel = rt[:, 1024:1024 + NT * NE].rearrange("p (t e) -> p t e", t=NT)
        eps_t = sb("eps_t", [P, 1])

        io_t = sb("io_t", [P, 2 * NT], I32)
        pad_t = sb("pad_t", [P, SLOT_TILES], I32)
        slot_i = sb("slot_i", [P, 2 * NT], I32)
        inv_t = sb("inv_t", [P, SLOT_TILES], I32)
        tok_t = sb("tok_t", [P, SLOT_TILES], I32)
        cur_t = sb("cur_t", [P, 2], I32)
        over_i = sb("over_i", [1, 8], I32)
        e_off = sb("e_off", [P, NE])
        io_o = sb("io_o", [P, OVER])
        wgt = sb("wgt", [P, 2, NT])

        S = {n: sem(n) for n in (
            "xT_in0 xT_in1 wssm_in wqk_in wv_in wup_in small_in par_in rb_in wpl_in wrt_in wglu_in rc_in "
            "wo_in wpg_in wpp_in pT_in ln_in xh_in "
            "const_set dve_step act_step gp_step uT_done qk_done pool_in_done v_done bx_ready bxT_done "
            "cp_ready kern_done rot_ready xrot_done "
            "u_out u_back m0_in s_ready s_moved y_evac y_out y_back yin_ready gelu_done glu_sig ssm_done "
            "pool_ready pool_mixed pe_u pe_qk pe_pool pe_v pe_bxT pe_kern pe_x pe_s pe_pt pe_pv pe_pm pe_y "
            "pe_glu s_evac p_exp p_norm pt_evac pv_evac sq_done pe_sq rms_sqrt rms_ready heads_ready pe_wo "
            "ang trig sel_ready o_c1 z_ready ln_sqrt h_ready pe_hT hT_evac h_out0 h_out1 h_out2 h_out3 pe_rt sig_rt pe_cnt slots_ready inv_set inv_put "
            "inv_back tok_ready pe_pg pe_pp ple_sig ple_done "
            "e_in0 e_in1 e_in2 e_in3 hg_in0 hg_in1 hg_in2 hg_in3 ye_out0 ye_out1 ye_out2 ye_out3 pe_hgT hgT_evac pe_gu silu_done a_ready "
            "pe_aT aT_evac pe_dn ye_evac moe_done "
            "o_col o_in o_hg o_t o_te o_gu o_si o_a o_at o_ae o_dn o_ye o_out o_round_sp o_round_gp o_round_dv "
            "yk0_in0 yk0_in1 yk0_in2 yk0_in3 yk1_in0 yk1_in1 yk1_in2 yk1_in3 z2_ready ln2_sqrt ln2_in rs2_ready xhat_done gain_done o_g out_st").split()}

        block = ctx.enter_context(nc.Block())

        w_in_v = io["w_in"].rearrange("(p k) n -> p k n", k=KD)
        eg_v = io["w_exp_gate"].rearrange("e (p k) n -> e p (k n)", k=KD)
        eu_v = io["w_exp_up"].rearrange("e (p k) n -> e p (k n)", k=KD)
        ed_v = io["w_exp_down"].rearrange("e (p k) n -> e p (k n)", k=2)

        @block.sync
        def _(sp):
            def load(dst, src, signal):
                sp.dma_start(dst, src).then_inc(S[signal], 16)

            xv = io["xT"].rearrange("(p k) t -> p k t", k=KD)
            load(xT[:, 0:4, :], xv[:, 0:4, :], "xT_in0")
            load(w_ssm, w_in_v[:, :, POOL_W + 3 * ATT_W:IN_W], "wssm_in")
            load(xT[:, 4:8, :], xv[:, 4:8, :], "xT_in1")
            load(par, io["ssm_par"], "par_in")
            load(w_q, w_in_v[:, :, POOL_W:POOL_W + ATT_W], "wqk_in")
            load(w_k, w_in_v[:, :, POOL_W + ATT_W:POOL_W + 2 * ATT_W], "wqk_in")
            load(w_up, w_in_v[:, :, 0:POOL_W], "wup_in")
            load(w_v, w_in_v[:, :, POOL_W + 2 * ATT_W:POOL_W + 3 * ATT_W], "wv_in")
            load(rbias, io["rel_tab"], "rb_in")
            sp.wait_ge(S["pe_v"], NT)
            sp.wait_ge(S["pe_pool"], 2)
            load(rcnt, io["rcnt"], "rc_in")
            load(w_glu, io["w_glu"].rearrange("(k p) n -> p k n", p=P), "wglu_in")
            sp.wait_ge(S["pe_kern"], 6)
            sp.wait_ge(S["rot_ready"], 1)
            sp.wait_ge(S["cp_ready"], 1)
            load(w_o, io["w_out"].rearrange("(k p) n -> p k n", p=P), "wo_in")
            sp.wait_ge(S["m0_in"], 16 * CH)
            sp.wait_ge(S["pe_y"], 3)
            load(w_pg, io["w_ple_gate"].rearrange("(p k) n -> p k n", k=KD), "wpg_in")
            sp.wait_ge(S["yin_ready"], 3)
            load(w_pp, io["w_ple_proj"].rearrange("(k p) n -> p k n", p=P), "wpp_in")
            load(pT, io["pT"].rearrange("(k p) t -> p k t", p=P), "pT_in")
            load(lng, io["ln"][0:1, :].partition_broadcast(P), "ln_in")
            load(lnb, io["ln"][1:2, :].partition_broadcast(P), "ln_in")
            sp.wait_ge(S["s_evac"], HEADS)
            load(xh, io["x"].rearrange("(t p) d -> p t d", p=P), "xh_in")
            sp.wait_ge(S["pe_pv"], HEADS)
            sp.wait_ge(S["ssm_done"], 3)

            def load_expert(b, e, first=False):
                sp.dma_start(ebuf[b][:, 0:2048], eg_v[e]).then_inc(S[f"e_in{b}"], 16)
                sp.dma_start(ebuf[b][:, 2048:4096], eu_v[e]).then_inc(S[f"e_in{b}"], 16)
                sp.dma_start(ebuf[b][:, 4096:6144], ed_v[e]).then_inc(S[f"e_in{b}"], 16)

            load_expert(0, 0)
            load_expert(1, 1)
            for t in range(NT):
                sp.wait_ge(S["h_ready"], t + 1)
                sp.dma_start(h_d[t * P:(t + 1) * P, :], xh[:, t, :]).then_inc(S[f"h_out{t}"], 16)
            load(lng, io["ln"][2:3, :].partition_broadcast(P), "ln2_in")
            load(lnb, io["ln"][3:4, :].partition_broadcast(P), "ln2_in")
            sp.wait_ge(S["pe_wo"], 2 * NT)
            load_expert(2, 2)
            sp.wait_ge(S["pe_pg"], 2 * NT)
            load_expert(3, 3)
            with sp.Fori(0, 3) as blk:
                for b in range(4):
                    sp.wait_ge(S["pe_dn"], 4 * blk + b + 1)
                    e = blk * 4 + (4 + b)
                    sp.dma_start(ebuf[b][:, 0:2048], eg_v[bass.ds(e, 1)].rearrange("o p n -> p (o n)")).then_inc(S[f"e_in{b}"], 16)
                    sp.dma_start(ebuf[b][:, 2048:4096], eu_v[bass.ds(e, 1)].rearrange("o p n -> p (o n)")).then_inc(S[f"e_in{b}"], 16)
                    sp.dma_start(ebuf[b][:, 4096:6144], ed_v[bass.ds(e, 1)].rearrange("o p n -> p (o n)")).then_inc(S[f"e_in{b}"], 16)
            sp.wait_ge(S["tok_ready"], 1)
            n_over = sp.value_load(over_i[0:1, 0:1], min_val=0, max_val=OVER)
            sp.wait_ge(S["pe_dn"], NE)
            with sp.Fori(0, OVER) as o:
                with sp.If(o < n_over):
                    e = sp.value_load(over_i[0:1, bass.ds(o + 1, 1)], min_val=0, max_val=NE - 1)
                    sp.wait_ge(S["o_col"], o + 1)
                    sp.dma_start(ebuf[0][:, 0:2048], eg_v[bass.ds(e, 1)].rearrange("o p n -> p (o n)")).then_inc(S["o_in"], 16)
                    sp.dma_start(ebuf[0][:, 2048:4096], eu_v[bass.ds(e, 1)].rearrange("o p n -> p (o n)")).then_inc(S["o_in"], 16)
                    sp.dma_start(ebuf[0][:, 4096:6144], ed_v[bass.ds(e, 1)].rearrange("o p n -> p (o n)")).then_inc(S["o_in"], 16)
                    sp.wait_ge(S["o_out"], 16 * (o + 1))
                    sp.sem_inc(S["o_round_sp"], 1)
            sp.wait_ge(S["moe_done"], 1)
            yv = ye_d.rearrange("(t p k) d -> t k p d", p=P, k=2)
            for t in range(NT):
                for k in range(2):
                    sp.dma_start(RA[:, (2 * t + k) * D:(2 * t + k + 1) * D], yv[t, k]).then_inc(S[f"yk{k}_in{t}"], 16)
            for t in range(NT):
                sp.wait_ge(S["o_g"], t + 1)
                sp.dma_start(out[t * P:(t + 1) * P, :], xh[:, t, :]).then_inc(S["out_st"], 16)
            sp.wait_ge(S["out_st"], 16 * NT)

        @block.gpsimd
        def _(gp):
            n = [0]

            def link(ins):
                n[0] += 1
                ins.then_inc(S["gp_step"], 1)
                gp.wait_ge(S["gp_step"], n[0])

            g = nc.gpsimd
            link(g.memset(ident[:], 0.0))
            link(g.memset(ones[:], 1.0))
            link(g.affine_select(out=ident[:], in_=ident[:], compare_op=ALU.not_equal, fill=1.0, base=0,
                                 pattern=[[-1, P]], channel_multiplier=1))
            link(g.affine_select(out=tri[:], in_=ones[:], compare_op=ALU.is_gt, fill=0.0, base=0,
                                 pattern=[[1, P]], channel_multiplier=-1))
            link(g.memset(w_pl[:], 0.0))
            link(g.memset(m0, 0.0))
            link(g.iota(io_t[:].rearrange("p (t k) -> p t k", k=2), pattern=[[2 * P, NT], [1, 2]], base=0, channel_multiplier=2))
            link(g.iota(pad_t[:], pattern=[[0, SLOT_TILES]], base=PAD, channel_multiplier=0))
            link(g.iota(e_off[:], pattern=[[CAP, NE]], base=0, channel_multiplier=0, allow_small_or_imprecise_dtypes=True))
            g.iota(io_o[:], pattern=[[1, OVER]], base=0, channel_multiplier=0,
                   allow_small_or_imprecise_dtypes=True).then_inc(S["const_set"], 1)
            gp.wait_ge(S["const_set"], 1)
            for i in range(4):
                h, m = i % 2, i // 2
                gp.dma_start(w_pl[64 * h:64 * h + 64, m, 64 * h:64 * h + 64], io["w_pool"][i]).then_inc(S["wpl_in"], 16)
            gp.dma_start(inv_d.rearrange("(p c) o -> p (c o)", p=P), pad_t[:]).then_inc(S["inv_set"], 16)
            gp.wait_ge(S["rb_in"], 16)
            link(g.memset(rbias[0:64, :, 192:256], NEG))

            gp.wait_ge(S["bx_ready"], 1)
            tmp_g = decay
            link(g.memset(rot[:, 0, :, 0:1], 1.0))
            link(g.memset(rot[:, 1, :, 0:1], 0.0))
            link(g.tensor_copy(rot[:, 0, :, 1:2], u8[:, 0, :].unsqueeze(2)))
            link(g.tensor_copy(rot[:, 1, :, 1:2], u8[:, 1, :].unsqueeze(2)))
            m = 1
            while m < NC:
                shape = [P, Q, m]
                t = tmp_g[:, 0:Q * m].rearrange("p (q c) -> p q c", q=Q)
                ar, ai = rot[:, 0, :, 1:m + 1], rot[:, 1, :, 1:m + 1]
                br = rot[:, 0, :, m:m + 1].broadcast_to(shape)
                bi = rot[:, 1, :, m:m + 1].broadcast_to(shape)
                orr, oi = rot[:, 0, :, m + 1:2 * m + 1], rot[:, 1, :, m + 1:2 * m + 1]
                link(g.tensor_tensor(t, ai, bi, ALU.mult))
                link(g.tensor_tensor(orr, ar, br, ALU.mult))
                link(g.tensor_tensor(orr, orr, t, ALU.subtract))
                link(g.tensor_tensor(t, ar, bi, ALU.mult))
                link(g.tensor_tensor(oi, ai, br, ALU.mult))
                link(g.tensor_tensor(oi, oi, t, ALU.add))
                m *= 2
            dec = decay.rearrange("p (q c) -> p q c", q=Q)
            link(g.tensor_copy(dec, mag8[:].unsqueeze(2).broadcast_to([P, Q, NC])))
            g.memset(dec[:, :, 0:1], 0.0).then_inc(S["rot_ready"], 1)
            gp.wait_ge(S["rot_ready"], 1)

            gp.wait_ge(S["kern_done"], 6)
            for j in range(CH):
                gp.dma_start(m0[GD * j:GD * (j + 1), :, j:CH, :], kern[:, :, 0:CH - j, :]).then_inc(S["m0_in"], 16)

            gp.wait_ge(S["pool_in_done"], 2)
            gp.wait_ge(S["pe_v"], NT)
            a, b2 = pl_s[:, 0], pl_s[:, 1]

            def add_shift(o, i, w, lo, ms):
                link(g.tensor_copy(o[lo:P, ms, 0:w], i[lo:P, ms, 0:w]))
                link(g.tensor_tensor(o[lo:P, ms, w:T], i[lo:P, ms, w:T], i[lo:P, ms, 0:T - w], ALU.add))

            both, second = slice(0, 2), slice(1, 2)
            add_shift(a, plT, 1, 0, both)
            add_shift(b2, a, 2, 0, second)
            add_shift(b2, a, 2, 64, slice(0, 1))
            link(g.tensor_copy(a[64:P, 0:1], b2[64:P, 0:1]))
            add_shift(a, b2, 4, 0, second)
            link(g.tensor_copy(b2[64:P, 1:2], a[64:P, 1:2]))
            add_shift(a, b2, 8, 64, second)
            gp.wait_ge(S["rc_in"], 16)
            link(g.tensor_tensor(a, a, rcnt, ALU.mult))
            g.tensor_tensor(a, a, plT, ALU.subtract).then_inc(S["pool_ready"], 1)

            gp.wait_ge(S["s_ready"], 1)
            sv = s_in.rearrange("p (q r) c -> p q r c", r=2)
            for r in range(2):
                for par_ in range(2):
                    gp.dma_start(sv[64 * r:64 * r + 64, :, par_, :],
                                 x_tmp[64 * par_:64 * par_ + 64, r, :].rearrange("p (q c) -> p q c", q=Q)).then_inc(S["s_moved"], 16)

            gp.wait_ge(S["pe_wo"], 2 * NT)
            link(g.memset(RE[:, :], 0.0))
            gp.wait_ge(S["slots_ready"], 1)
            gp.wait_ge(S["inv_set"], 16)
            for i in range(NT):
                for k in range(2):
                    gp.indirect_dma_start(
                        out=inv_d, out_offset=bass.IndirectOffsetOnAxis(ap=slot_i[:, 2 * i + k:2 * i + k + 1], axis=0),
                        in_=io_t[:, 2 * i + k:2 * i + k + 1], in_offset=None,
                        bounds_check=SLOT_TILES * P - 1, oob_is_err=False).then_inc(S["inv_put"], 16)
            gp.wait_ge(S["inv_put"], 16 * 2 * NT)
            gp.dma_start(inv_t[:], inv_d.rearrange("(c p) o -> p (c o)", p=P), allow_slow_non_contiguous=True).then_inc(S["inv_back"], 16)

            def gather(dst, idx, signal):
                gp.indirect_dma_start(out=dst, out_offset=None, in_=h_d,
                                      in_offset=bass.IndirectOffsetOnAxis(ap=idx, axis=0),
                                      bounds_check=T - 1, oob_is_err=False).then_inc(S[signal], 16)

            def scatter(idx, src, signal):
                gp.indirect_dma_start(out=ye_d, out_offset=bass.IndirectOffsetOnAxis(ap=idx, axis=0),
                                      in_=src, in_offset=None,
                                      bounds_check=2 * T - 1, oob_is_err=False).then_inc(S[signal], 16)

            gp.wait_ge(S["tok_ready"], 1)
            for t in range(NT):
                gp.wait_ge(S[f"h_out{t}"], 16)
            for e in range(4):
                gather(hg[:, e, :], tok_t[:, e:e + 1], f"hg_in{e}")
            for e in range(NE):
                if e + 4 < NE:
                    gp.wait_ge(S["pe_hgT"], e + 1)
                    gather(hg[:, e % 4, :], tok_t[:, e + 4:e + 5], f"hg_in{e % 4}")
                gp.wait_ge(S["ye_evac"], e + 1)
                scatter(inv_t[:, e:e + 1], y_e[e % 4], f"ye_out{e % 4}")
            for b in range(4):
                gp.wait_ge(S[f"ye_out{b}"], 16 * NE // 4)
            n_over = gp.value_load(over_i[0:1, 0:1], min_val=0, max_val=OVER)
            with gp.Fori(0, OVER) as o:
                with gp.If(o < n_over):
                    gp.wait_ge(S["o_col"], o + 1)
                    gp.sem_inc(S["o_round_gp"], 1)
                    gather(hg[:, 0, :], cur_t[:, 0:1], "o_hg")
                    gp.wait_ge(S["o_ye"], 2 * o + 2)
                    gp.sem_inc(S["o_round_gp"], 1)
                    scatter(cur_t[:, 1:2], y_e[0], "o_out")
                    gp.wait_ge(S["o_out"], 16 * (o + 1))
                    gp.sem_inc(S["o_round_gp"], 1)
            gp.sem_inc(S["moe_done"], 1)
            gp.wait_ge(S["ln2_in"], 32)
            for t in range(NT - 1):
                gp.wait_ge(S["gain_done"], t + 1)
                g.tensor_tensor(xh[:, t, :], xh[:, t, :], lnb, ALU.add).then_inc(S["o_g"], 1)

        @block.scalar
        def _(ac):
            a = nc.scalar
            n = [0]

            def link(ins):
                n[0] += 1
                ins.then_inc(S["act_step"], 1)
                ac.wait_ge(S["act_step"], n[0])

            ac.dma_start(vec[:], io["vec"]).then_inc(S["small_in"], 16)
            ac.dma_start(w_rt[:], io["w_router"].rearrange("(p k) n -> p k n", k=KD)).then_inc(S["wrt_in"], 16)

            ac.wait_ge(S["small_in"], 16)
            ac.wait_ge(S["par_in"], 16)
            link(a.activation(par[64:P, C_CA:C_CB], par[64:P, C_CA:C_CB], ACT.Copy, scale=-1.0))
            link(a.activation(par[:, C_CB:SSM_COLS], par[:, C_CB:SSM_COLS], ACT.Copy, scale=-1.0))
            link(a.activation(dt_[:], par[:, C_LDT:C_LDT + NG], ACT.Exp))
            ac.wait_ge(S["ang"], 1)
            link(a.activation(expo[:], expo[:], ACT.Exp))
            link(a.activation(sinf[:], angr[:], ACT.Sin))
            a.activation(sinh[:], angr[:], ACT.Sin, scale=0.5).then_inc(S["trig"], 1)
            for m in range(3):
                ac.wait_ge(S["pe_u"], m + 1)
                a.activation(uT[:, m, :].rearrange("p (j c) -> p j c", j=CH),
                             bank[m][:].rearrange("p (c j) -> p j c", j=CH), ACT.Copy).then_inc(S["uT_done"], 1)
                ac.wait_ge(S["uT_done"], m + 1)
                ac.dma_start(u_d[m * P:(m + 1) * P, :], uT[:, m, :]).then_inc(S["u_out"], 16)
            for m in range(6):
                ac.wait_ge(S["pe_qk"], m + 1)
                dst = (qT if m % 2 == 0 else kT)[:, m // 2, :]
                a.activation(dst, bank[(3 + m) % 8][:], ACT.Copy).then_inc(S["qk_done"], 1)
                if m == 0:
                    ac.wait_ge(S["u_out"], 48)
                    for j in range(CH):
                        ac.dma_start(uch[GD * j:GD * (j + 1), :, :],
                                     u_d.rearrange("(g h) (j c) -> j h g c", h=GD, j=CH)[j]).then_inc(S["u_back"], 16)
            for m in range(2):
                ac.wait_ge(S["pe_pool"], m + 1)
                a.activation(plT[:, m, :], bank[1 + m][:], ACT.Copy).then_inc(S["pool_in_done"], 1)
            for t in range(NT):
                ac.wait_ge(S["pe_v"], t + 1)
                a.activation(vN[:, t, :], bank[[4, 6, 0, 2][t]][:, 0:ATT_W], ACT.Copy).then_inc(S["v_done"], 1)
            for m in range(6):
                ac.wait_ge(S["pe_kern"], m + 1)
                a.activation(kern[:, 4 * m:4 * m + 4], bank[(5 + m) % 8][0:GD, :].rearrange("p (g l h) -> p g l h", g=4, l=CH),
                             ACT.Copy).then_inc(S["kern_done"], 1)

            def exps(h):
                ac.wait_ge(S["s_evac"], h + 1)
                for i in range(NT):
                    o, w = SCORE_AT[i][2], (i + 1) * P
                    blk = prob[:, h % 2, o:o + w]
                    last = a.activation(blk, blk, ACT.Exp, bias=att_mx[:, h % 2, i:i + 1],
                                        accum_out=att_sm[:, h % 2, i:i + 1])
                    if i < NT - 1:
                        link(last)
                last.then_inc(S["p_exp"], 1)

            def pt_copy(h):
                for u, (_, o, w) in enumerate(PT_UNITS):
                    k = 3 * h + u
                    ac.wait_ge(S["pe_pt"], k + 1)
                    if u == 0 and h >= 2:
                        ac.wait_ge(S["pe_pv"], h - 1)
                    a.activation(probT[:, h % 2, o:o + w], bank[3 + k % 2][:, 0:w], ACT.Copy).then_inc(S["pt_evac"], 1)

            def pv_copy(pair):
                ac.wait_ge(S["pe_pv"], 2 * pair + 2)
                a.activation(hdT[:, 2 + pair, :], bank[5 + pair % 2][:], ACT.Copy).then_inc(S["pv_evac"], 1)

            exps(0)
            for m in range(2):
                ac.wait_ge(S["pe_pm"], m + 1)
                a.activation(hdT[:, m, :], bank[7 - m][:], ACT.Copy, scale=vec[:, V_PS + m:V_PS + m + 1]).then_inc(S["pool_mixed"], 1)
            exps(1)
            pt_copy(0)
            exps(2)
            pt_copy(1)
            pv_copy(0)
            for m in range(3):
                ac.wait_ge(S["pe_y"], m + 1)
                a.activation(y_ch[:, 8 * m:8 * m + 8, :], bank[7 - m % 2][:].rearrange("p (g c) -> p g c", g=8),
                             ACT.Copy).then_inc(S["y_evac"], 1)
            ac.wait_ge(S["y_evac"], 3)
            for j in range(CH):
                ac.dma_start(y_d.rearrange("(g h) (j c) -> j h g c", h=GD, j=CH)[j],
                             y_ch[GD * j:GD * (j + 1), :, :]).then_inc(S["y_out"], 16)
            exps(3)
            pt_copy(2)
            ac.wait_ge(S["y_out"], 16 * CH)
            ac.wait_ge(S["s_moved"], 64)
            ac.dma_start(yT, y_d.rearrange("(m p) t -> p m t", p=P)).then_inc(S["y_back"], 16)
            exps(4)
            pt_copy(3)
            pv_copy(1)
            exps(5)
            for m in range(3):
                ac.wait_ge(S["yin_ready"], m + 1)
                a.activation(hdT[:, 5 + m, :].rearrange("p (c j) -> p c j", j=CH),
                             yT[:, m, :].rearrange("p (j c) -> p c j", j=CH), ACT.Gelu_apprx_tanh).then_inc(S["gelu_done"], 1)
            pt_copy(4)
            for m in range(3):
                ac.wait_ge(S["pe_glu"], m + 1)
                a.activation(sgl[:, m, :], bank[7 - m % 2][:], ACT.Sigmoid, bias=vec[:, V_BG + m:V_BG + m + 1]).then_inc(S["glu_sig"], 1)
            pt_copy(5)
            pv_copy(2)
            ac.wait_ge(S["pv_evac"], 3)
            ac.wait_ge(S["pool_mixed"], 2)
            for k, m in enumerate([0, 1, 5, 6, 7, 2, 3, 4]):
                if m >= 5:
                    ac.wait_ge(S["ssm_done"], m - 4)
                if k >= 2:
                    ac.wait_ge(S["pe_sq"], k - 1)
                a.activation(sq2[:, k % 2, :], hdT[:, m, :], ACT.Square).then_inc(S["sq_done"], 1)
            for g in range(3):
                ac.wait_ge(S["pe_sq"], [2, 5, 8][g])
                a.activation(rstdB[:, g, :], bank[[7, 6, 0][g]][:], ACT.Sqrt, bias=eps_t[:],
                             scale=[1.0 / POOL_W, 1.0 / SSM_W, 1.0 / ATT_W][g]).then_inc(S["rms_sqrt"], 1)
            def hT_copy(t):
                for u in range(2):
                    ac.wait_ge(S["pe_hT"], 2 * t + u + 1)
                    a.activation(hT[:, 4 * u:4 * u + 4, t * P:(t + 1) * P], bank[u][:].rearrange("p (k t) -> p k t", k=4),
                                 ACT.Copy).then_inc(S["hT_evac"], 1)

            def ple_gate(k):
                ac.wait_ge(S["pe_pg"], k + 1)
                if k >= 2:
                    ac.wait_ge(S["ple_done"], k - 1)
                a.activation(ple_t[:, (k % 2) * 512:(k % 2) * 512 + 512], bank[6 + k % 2][:], ACT.Sigmoid).then_inc(S["ple_sig"], 1)

            for t in range(NT):
                ac.wait_ge(S["z_ready"], t + 1)
                a.activation(ln_rs[:, t, 0:1], ln_mv[:, t, 1:2], ACT.Sqrt, bias=eps_t[:]).then_inc(S["ln_sqrt"], 1)
                if t >= 1:
                    hT_copy(t - 1)
            ple_gate(0)
            ple_gate(1)
            hT_copy(NT - 1)
            ac.wait_ge(S["pe_rt"], 1)
            a.activation(r_s, bank[2][:, 0:NT * NE], ACT.Sigmoid).then_inc(S["sig_rt"], 1)
            for k in range(2, 2 * NT):
                ple_gate(k)

            def hgT_copy(e, r):
                ac.wait_ge(S["pe_hgT"], e + 1)
                for u in range(2):
                    a.activation(hgT[:, r, 4 * u:4 * u + 4, :], bank[u][:].rearrange("p (k s) -> p k s", k=4),
                                 ACT.Copy).then_inc(S["hgT_evac"], 1)

            def expert(e, r, last=False):
                ac.wait_ge(S["pe_gu"], e + 1)
                a.activation(act_e[:, r, 0, :], bank[2 + r][:, 0:DE], ACT.Silu).then_inc(S["silu_done"], 1)
                if not last:
                    hgT_copy(e + 1, 1 - r)
                ac.wait_ge(S["pe_aT"], e + 1)
                a.activation(act_e[:, r, 2, :], bank[4 + r][:, 0:DE], ACT.Copy).then_inc(S["aT_evac"], 1)

            ac.wait_ge(S["pe_pg"], 2 * NT)
            hgT_copy(0, 0)
            with ac.Fori(0, NE // 2 - 1) as blk:
                for r in range(2):
                    expert(2 * blk + r, r)
            expert(NE - 2, 0)
            expert(NE - 1, 1, last=True)
            n_over = ac.value_load(over_i[0:1, 0:1], min_val=0, max_val=OVER)
            with ac.Fori(0, OVER) as o:
                with ac.If(o < n_over):
                    ac.wait_ge(S["o_t"], o + 1)
                    for u in range(2):
                        a.activation(hgT[:, 0, 4 * u:4 * u + 4, :], bank[u][:].rearrange("p (k s) -> p k s", k=4),
                                     ACT.Copy).then_inc(S["o_te"], 1)
                    ac.wait_ge(S["o_gu"], o + 1)
                    a.activation(act_e[:, 0, 0, :], bank[2][:, 0:DE], ACT.Silu).then_inc(S["o_si"], 1)
                    ac.wait_ge(S["o_at"], o + 1)
                    a.activation(act_e[:, 0, 2, :], bank[4][:, 0:DE], ACT.Copy).then_inc(S["o_ae"], 1)
            for t in range(NT):
                ac.wait_ge(S["z2_ready"], t + 1)
                a.activation(ln_rs[:, t, 0:1], ln_mv[:, t, 1:2], ACT.Sqrt, bias=eps_t[:]).then_inc(S["ln2_sqrt"], 1)
                ac.wait_ge(S["rs2_ready"], t + 1)
                a.activation(xh[:, t, :], xh[:, t, :], ACT.Identity, bias=ln_mv[:, t, 0:1], scale=ln_rs[:, t, 1:2]).then_inc(S["xhat_done"], 1)

        @block.tensor
        def _(pe):
            mm = nc.tensor.matmul
            pe.wait_ge(S["const_set"], 1)

            def project(bank_i, w, m, signal):
                for k in range(KD):
                    if k == 4:
                        pe.wait_ge(S["xT_in1"], 16)
                    last = mm(bank[bank_i][:], w[:, k, m * P:(m + 1) * P], xT[:, k, :], start=(k == 0), stop=(k == KD - 1))
                last.then_inc(S[signal], 1)

            pe.wait_ge(S["xT_in0"], 16)
            pe.wait_ge(S["wssm_in"], 16)
            for m in range(3):
                project(m, w_ssm, m, "pe_u")
            pe.wait_ge(S["wqk_in"], 32)
            for m in range(6):
                if m == 5:
                    pe.wait_ge(S["uT_done"], 1)
                project((3 + m) % 8, w_q if m % 2 == 0 else w_k, m // 2, "pe_qk")
            pe.wait_ge(S["wup_in"], 16)
            for m in range(2):
                pe.wait_ge(S["uT_done"], m + 2)
                project(1 + m, w_up, m, "pe_pool")
            pe.wait_ge(S["wv_in"], 16)

            def v_tile(t, bank_i):
                for k in range(KD):
                    last = mm(bank[bank_i][:, 0:ATT_W], xT[:, k, t * P:(t + 1) * P], w_v[:, k, :], start=(k == 0), stop=(k == KD - 1))
                last.then_inc(S["pe_v"], 1)

            def bx_turn(n, bank_i):
                for i in range(4):
                    r, q = n // 3, 4 * (n % 3) + i
                    last = nc.tensor.transpose(bank[bank_i][:, i * P:(i + 1) * P], bx[:, r, q].rearrange("p j h -> p (j h)"), ident[:])
                last.then_inc(S["pe_bxT"], 1)

            pe.wait_ge(S["qk_done"], 2)
            v_tile(0, 4)
            pe.wait_ge(S["bx_ready"], 2)
            bx_turn(0, 3)
            pe.wait_ge(S["qk_done"], 4)
            bx_turn(1, 5)
            v_tile(1, 6)
            pe.wait_ge(S["qk_done"], 6)
            bx_turn(2, 7)
            v_tile(2, 0)
            pe.wait_ge(S["pool_in_done"], 2)
            bx_turn(3, 1)
            v_tile(3, 2)
            pe.wait_ge(S["bxT_done"], 1)
            bx_turn(4, 3)
            pe.wait_ge(S["v_done"], 1)
            bx_turn(5, 4)

            pe.wait_ge(S["cp_ready"], 1)
            for n, (signal, count) in enumerate([("bxT_done", 2), ("v_done", 2), ("bxT_done", 3), ("v_done", 3), ("bxT_done", 4), ("v_done", 4)]):
                pe.wait_ge(S[signal], count)
                for i in range(4):
                    g = 4 * n + i
                    last = mm(bank[(5 + n) % 8][0:GD, i * P:(i + 1) * P], b_st[:, g, :],
                              cp[:, g, 0:CH, :].rearrange("p l h -> p (l h)"), start=True, stop=True)
                last.then_inc(S["pe_kern"], 1)

            pe.wait_ge(S["bxT_done"], 6)
            pe.wait_ge(S["kern_done"], 2)
            pe.wait_ge(S["u_back"], 16 * CH)
            for r in range(2):
                for q in range(Q):
                    for h in range(2):
                        b = 3 + 2 * r + q // 6
                        last = mm(bank[b][64 * h:64 * h + 64, (q % 6) * NC:(q % 6 + 1) * NC], bxT[:, r, q, 64 * h:64 * h + 64],
                                  uch[:, 2 * q + h, :], start=True, stop=True)
            last.then_inc(S["pe_x"], 1)

            def scores(h):
                if h == 0:
                    pe.wait_ge(S["kern_done"], 6)
                else:
                    pe.wait_ge(S["s_evac"], h)
                rows = slice(64 * (h % 2), 64 * (h % 2) + 64)
                for i in (0, 2, 3, 1):
                    b, c, _ = SCORE_AT[i]
                    w = (i + 1) * P
                    last = mm(bank[b][:, c:c + w], qT[rows, h // 2, i * P:(i + 1) * P], kT[rows, h // 2, 0:w], start=True, stop=True)
                last.then_inc(S["pe_s"], 1)

            def turn_probs(h):
                pe.wait_ge(S["p_norm"], h + 1)
                for u, (tiles, _, _) in enumerate(PT_UNITS):
                    k = 3 * h + u
                    if k >= 2:
                        pe.wait_ge(S["pt_evac"], k - 1)
                    elif k == 0:
                        pe.wait_ge(S["xrot_done"], 1)
                    c = 0
                    for j in tiles:
                        for i in range(j, NT):
                            o = SCORE_AT[i][2] + j * P
                            last = nc.tensor.transpose(bank[3 + k % 2][:, c:c + P], prob[:, h % 2, o:o + P], ident[:])
                            c += P
                    last.then_inc(S["pe_pt"], 1)

            def weigh_values(h):
                pair = h // 2
                pe.wait_ge(S["pt_evac"], 3 * h + 3)
                if h == 4:
                    pe.wait_ge(S["pv_evac"], 1)
                if h == 2:
                    pe.wait_ge(S["y_evac"], 3)
                rows = slice(64 * (h % 2), 64 * (h % 2) + 64)
                for j in range(NT):
                    o = PT_AT[j]
                    last = mm(bank[5 + pair % 2][rows, j * P:T], vN[:, j, h * HD:(h + 1) * HD],
                              probT[:, h % 2, o:o + T - j * P], start=(j == 0), stop=(j == NT - 1))
                last.then_inc(S["pe_pv"], 1)

            pe.wait_ge(S["qk_done"], 6)
            pe.wait_ge(S["v_done"], 4)
            scores(0)
            scores(1)
            pe.wait_ge(S["pool_ready"], 1)
            pe.wait_ge(S["wpl_in"], 64)
            pe.wait_ge(S["xrot_done"], 1)
            for m in range(2):
                mm(bank[7 - m][:], w_pl[:, m, :], pl_s[:, 0, m, :], start=True, stop=True).then_inc(S["pe_pm"], 1)
            turn_probs(0)
            scores(2)
            weigh_values(0)
            turn_probs(1)
            scores(3)
            weigh_values(1)
            pe.wait_ge(S["pool_mixed"], 2)
            pe.wait_ge(S["s_moved"], 64)
            pe.wait_ge(S["m0_in"], 16 * CH)
            for m in range(3):
                if m == 2:
                    pe.wait_ge(S["y_evac"], 1)
                for i in range(8):
                    g = 8 * m + i
                    dst = bank[7 - m % 2][:, i * NC:(i + 1) * NC]
                    mm(dst, m0[:, g].rearrange("p l h -> p (l h)"), uch[:, g, :], start=True, stop=False)
                    last = mm(dst, cp[:, g, 1:CH + 1, :].rearrange("p l h -> p (l h)"), s_in[:, g, :], start=False, stop=True)
                last.then_inc(S["pe_y"], 1)
            turn_probs(2)
            scores(4)
            weigh_values(2)
            turn_probs(3)
            scores(5)
            weigh_values(3)
            turn_probs(4)
            pe.wait_ge(S["gelu_done"], 3)
            pe.wait_ge(S["wglu_in"], 16)
            pe.wait_ge(S["pv_evac"], 2)
            for m in range(3):
                if m == 2:
                    pe.wait_ge(S["glu_sig"], 1)
                for k in range(3):
                    last = mm(bank[7 - m % 2][:], w_glu[:, k, m * P:(m + 1) * P], hdT[:, 5 + k, :], start=(k == 0), stop=(k == 2))
                last.then_inc(S["pe_glu"], 1)
            weigh_values(4)
            turn_probs(5)
            weigh_values(5)
            pe.wait_ge(S["glu_sig"], 3)
            k = 0
            for g, tiles in enumerate([2, 3, 3]):
                for i in range(tiles):
                    pe.wait_ge(S["sq_done"], k + 1)
                    mm(bank[[7, 6, 0][g]][:], ones[:], sq2[:, k % 2, :], start=(i == 0), stop=(i == tiles - 1)).then_inc(S["pe_sq"], 1)
                    k += 1
            pe.wait_ge(S["wo_in"], 16)
            pe.wait_ge(S["rms_sqrt"], 3)
            pe.wait_ge(S["pv_evac"], 3)
            def out_proj(t):
                if t == 3:
                    pe.wait_ge(S["z_ready"], 2)
                for half in range(2):
                    for i, k in enumerate([0, 1, 5, 6, 7, 2, 3, 4]):
                        if t == 0 and half == 0:
                            pe.wait_ge(S["heads_ready"], i + 1)
                        last = mm(bank[WO_AT[t] + half][:], hdT[:, k, t * P:(t + 1) * P], w_o[:, k, half * 512:half * 512 + 512], start=(i == 0), stop=(i == KD - 1))
                    last.then_inc(S["pe_wo"], 1)

            def turn_h(t):
                pe.wait_ge(S["h_ready"], t + 1)
                for u in range(2):
                    if t:
                        pe.wait_ge(S["hT_evac"], 2 * t - 1 + u)
                    for i in range(4):
                        last = nc.tensor.transpose(bank[u][:, i * P:(i + 1) * P], xh[:, t, 4 * u + i:D:KD], ident[:])
                    last.then_inc(S["pe_hT"], 1)

            def ple(k):
                t, half = k // 2, k % 2
                if k >= 2:
                    pe.wait_ge(S["ple_done"], k - 1)
                cols = slice(half * 512, half * 512 + 512)
                for c in range(KD):
                    last = mm(bank[6 + k % 2][:], hT[:, c, t * P:(t + 1) * P], w_pg[:, c, cols], start=(c == 0), stop=(c == KD - 1))
                last.then_inc(S["pe_pg"], 1)
                for c in range(2):
                    last = mm(bank[4 + k % 2][:], pT[:, c, t * P:(t + 1) * P], w_pp[:, c, cols], start=(c == 0), stop=(c == 1))
                last.then_inc(S["pe_pp"], 1)

            out_proj(0)
            for t in range(1, NT):
                out_proj(t)
                turn_h(t - 1)
            pe.wait_ge(S["wpg_in"], 16)
            pe.wait_ge(S["wpp_in"], 16)
            pe.wait_ge(S["pT_in"], 16)
            pe.wait_ge(S["hT_evac"], 2)
            ple(0)
            ple(1)
            turn_h(NT - 1)
            pe.wait_ge(S["hT_evac"], 2 * NT)
            pe.wait_ge(S["wrt_in"], 16)
            for t in range(NT):
                for k in range(KD):
                    last = mm(bank[2][:, t * NE:(t + 1) * NE], hT[:, k, t * P:(t + 1) * P], w_rt[:, k, :], start=(k == 0), stop=(k == KD - 1))
            last.then_inc(S["pe_rt"], 1)
            ple(2)
            pe.wait_ge(S["sel_ready"], 1)
            for t in range(NT):
                for s in range(t + 1):
                    mm(bank[3][:, t * NE:(t + 1) * NE], (tri if s == t else ones)[:], r_sel[:, s, :], start=(s == 0), stop=(s == t))
            for s in range(NT):
                last = mm(bank[3][:, NT * NE:(NT + 1) * NE], ones[:], r_sel[:, s, :], start=(s == 0), stop=(s == NT - 1))
            last.then_inc(S["pe_cnt"], 1)
            for k in range(3, 2 * NT):
                ple(k)

            def turn_tokens(r):
                for k in range(KD):
                    last = nc.tensor.transpose(bank[k // 4][:, (k % 4) * P:(k % 4 + 1) * P], hg[:, r, k:D:KD], ident[:])
                return last

            def gate_up(b, r):
                w = ebuf[b][:, 0:4096].rearrange("p (u k n) -> p k u n", u=2, k=KD)
                for k in range(KD):
                    last = mm(bank[2 + r][:].rearrange("p (u n) -> p u n", u=2), hgT[:, r, k, :], w[:, k], start=(k == 0), stop=(k == KD - 1))
                return last

            def turn_act(r):
                for k in range(2):
                    last = nc.tensor.transpose(bank[4 + r][:, k * P:(k + 1) * P], act_e[:, r, 1, k:DE:2], ident[:])
                return last

            def down(b, r):
                w = ebuf[b][:, 4096:6144].rearrange("p (k n) -> p k n", k=2)
                for half in range(2):
                    for k in range(2):
                        last = mm(bank[6 + half][:], act_e[:, r, 2, k * P:(k + 1) * P], w[:, k, half * 512:half * 512 + 512],
                                  start=(k == 0), stop=(k == 1))
                return last

            def tokens_of(r, uses):
                pe.wait_ge(S[f"hg_in{r}"], 16 * uses)
                turn_tokens(r).then_inc(S["pe_hgT"], 1)

            def expert(e, b, loads, first=False, last=False):
                r = b % 2
                pe.wait_ge(S[f"e_in{b}"], 48 * loads)
                pe.wait_ge(S["hgT_evac"], 2 * e + 2)
                if not first:
                    pe.wait_ge(S["a_ready"], e)
                gate_up(b, r).then_inc(S["pe_gu"], 1)
                if not last:
                    tokens_of((b + 1) % 4, loads if b < 3 else loads + 1)
                if not first:
                    pe.wait_ge(S["aT_evac"], e)
                    if isinstance(e, int) and e == 1:
                        pe.wait_ge(S["ple_done"], 2 * NT)
                    else:
                        pe.wait_ge(S["ye_evac"], e - 1)
                    down((b + 3) % 4, 1 - r).then_inc(S["pe_dn"], 1)
                pe.wait_ge(S["a_ready"], e + 1)
                turn_act(r).then_inc(S["pe_aT"], 1)

            pe.wait_ge(S["pe_pg"], 2 * NT)
            tokens_of(0, 1)
            pe.wait_ge(S["ple_done"], 2 * NT)
            for e in range(4):
                expert(e, e, 1, first=(e == 0))
            with pe.Fori(1, NE // 4 - 1) as blk:
                for b in range(4):
                    expert(4 * blk + b, b, blk + 1)
            for e in range(NE - 4, NE):
                expert(e, e % 4, NE // 4, last=(e == NE - 1))
            pe.wait_ge(S["aT_evac"], NE)
            pe.wait_ge(S["ye_evac"], NE - 1)
            down(3, 1).then_inc(S["pe_dn"], 1)
            n_over = pe.value_load(over_i[0:1, 0:1], min_val=0, max_val=OVER)
            pe.wait_ge(S["ye_evac"], NE)
            with pe.Fori(0, OVER) as o:
                with pe.If(o < n_over):
                    pe.wait_ge(S["o_hg"], 16 * (o + 1))
                    turn_tokens(0).then_inc(S["o_t"], 1)
                    pe.wait_ge(S["o_te"], 2 * (o + 1))
                    pe.wait_ge(S["o_in"], 48 * (o + 1))
                    gate_up(0, 0).then_inc(S["o_gu"], 1)
                    pe.wait_ge(S["o_a"], o + 1)
                    turn_act(0).then_inc(S["o_at"], 1)
                    pe.wait_ge(S["o_ae"], o + 1)
                    down(0, 0).then_inc(S["o_dn"], 1)

        @block.vector
        def _(dv):
            v = nc.vector
            tt, ts, stt = v.tensor_tensor, v.tensor_scalar, v.scalar_tensor_tensor
            n = [0]

            def link(ins):
                n[0] += 1
                ins.then_inc(S["dve_step"], 1)
                dv.wait_ge(S["dve_step"], n[0])

            def cmul(o_r, o_i, a_r, a_i, b_r, b_i, t):
                link(tt(t, a_i, b_i, ALU.mult))
                link(tt(o_r, a_r, b_r, ALU.mult))
                link(tt(o_r, o_r, t, ALU.subtract))
                link(tt(t, a_r, b_i, ALU.mult))
                link(tt(o_i, a_i, b_r, ALU.mult))
                link(tt(o_i, o_i, t, ALU.add))

            link(v.memset(eps_t[:], EPS))
            dv.wait_ge(S["par_in"], 16)
            dv.wait_ge(S["act_step"], 3)
            are, aim = par[:, C_ARE:C_ARE + NG], par[:, C_AIM:C_AIM + NG]
            link(tt(expo[:, 0:NG], are, dt_[:], ALU.mult))
            link(tt(ang[:, 0:NG], aim, dt_[:], ALU.mult))
            link(ts(expo[:, NG:NG + Q], expo[:, 0:Q], float(CH), None, ALU.mult))
            link(ts(ang[:, NG:NG + Q], ang[:, 0:Q], float(CH), None, ALU.mult))
            link(ts(turns[:], ang[:], 1.0 / (2 * np.pi), ROUND, ALU.mult, ALU.add))
            link(ts(turns[:], turns[:], -ROUND, None, ALU.add))
            for part in (PI2_A, PI2_B, PI2_C):
                link(stt(ang[:], turns[:], -part, ang[:], ALU.mult, ALU.add))
            ts(angr[:], ang[:], PI_SAFE, -PI_SAFE, ALU.min, ALU.max).then_inc(S["ang"], 1)
            dv.wait_ge(S["trig"], 1)
            link(tt(sinh[:], sinh[:], sinh[:], ALU.mult))
            link(ts(sinh[:], sinh[:], -2.0, 1.0, ALU.mult, ALU.add))
            link(v.tensor_copy(u8[:, 0, :], sinh[:, NG:NG + Q]))
            link(v.tensor_copy(u8[:, 1, :], sinf[:, NG:NG + Q]))
            v.tensor_copy(mag8[:], expo[:, NG:NG + Q]).then_inc(S["bx_ready"], 1)
            dv.wait_ge(S["bx_ready"], 1)
            pr, pi = pw[:, 0], pw[:, 1]
            link(v.memset(pr[:, :, 0:1], 1.0))
            link(v.memset(pi[:, :, 0:1], 0.0))
            link(tt(pr[:, :, 1], expo[:, 0:NG], sinh[:, 0:NG], ALU.mult))
            link(tt(pi[:, :, 1], expo[:, 0:NG], sinf[:, 0:NG], ALU.mult))
            nr, c1, c2, c3 = (sm[:, k * NG:(k + 1) * NG] for k in range(10, 14))
            link(ts(nr, pr[:, :, 1], -1.0, None, ALU.add))
            link(tt(c1, are, are, ALU.mult))
            link(tt(c2, aim, aim, ALU.mult))
            link(tt(c1, c1, c2, ALU.add))
            link(v.reciprocal(c1, c1))
            link(tt(c2, nr, are, ALU.mult))
            link(tt(c3, pi[:, :, 1], aim, ALU.mult))
            link(tt(c2, c2, c3, ALU.add))
            link(tt(c2, c2, c1, ALU.mult))
            link(tt(c3, pi[:, :, 1], are, ALU.mult))
            link(tt(nr, nr, aim, ALU.mult))
            link(tt(c3, c3, nr, ALU.subtract))
            link(tt(c3, c3, c1, ALU.mult))
            wide = [P, NG, GD]
            b_re = par[:, C_BRE:C_BIM].rearrange("p (g h) -> p g h", g=NG)
            b_im = par[:, C_BIM:C_CA].rearrange("p (g h) -> p g h", g=NG)
            t3 = tmp[:, 0:NG * GD].rearrange("p (g h) -> p g h", g=NG)
            cmul(bb[:, 0], bb[:, 1], b_re, b_im, c2.unsqueeze(2).broadcast_to(wide), c3.unsqueeze(2).broadcast_to(wide), t3)
            link(v.tensor_copy(b_st[0:64], bb[0:64, 0, Q:NG, :]))
            link(v.tensor_copy(b_st[64:P], bb[64:P, 1, Q:NG, :]))
            for lo, hi, by in ((2, 3, 1), (3, 5, 2), (5, 9, 4)):
                w = hi - lo
                t2 = tmp[:, 0:NG * w].rearrange("p (g l) -> p g l", g=NG)
                a_r, a_i = pr[:, :, lo - by:hi - by], pi[:, :, lo - by:hi - by]
                s_ = [P, NG, w]
                cmul(pr[:, :, lo:hi], pi[:, :, lo:hi], a_r, a_i,
                     pr[:, :, by:by + 1].broadcast_to(s_), pi[:, :, by:by + 1].broadcast_to(s_), t2)
            t4 = tmp[:, 0:Q * GD].rearrange("p (q h) -> p q h", q=Q)
            for j in range(CH):
                s_ = [P, Q, GD]
                l = CH - 1 - j
                cmul(bx[:, 0, :, j, :], bx[:, 1, :, j, :], bb[:, 0, 0:Q, :], bb[:, 1, 0:Q, :],
                     pr[:, 0:Q, l:l + 1].broadcast_to(s_), pi[:, 0:Q, l:l + 1].broadcast_to(s_), t4)
            v.engine_nop().then_inc(S["bx_ready"], 1)
            t5 = tmp[:, 0:3456].rearrange("p (g l h) -> p g l h", g=G, l=CH + 1)
            s_ = [P, G, CH + 1, GD]
            d1 = par[:, C_CA:C_CB].rearrange("p (g h) -> p g h", g=G).unsqueeze(2).broadcast_to(s_)
            d2 = par[:, C_CB:SSM_COLS].rearrange("p (g h) -> p g h", g=G).unsqueeze(2).broadcast_to(s_)
            link(tt(cp, d1, pr[:, Q:NG, :].unsqueeze(3).broadcast_to(s_), ALU.mult))
            link(tt(t5, d2, pi[:, Q:NG, :].unsqueeze(3).broadcast_to(s_), ALU.mult))
            tt(cp, cp, t5, ALU.add).then_inc(S["cp_ready"], 1)
            for k in range(6):
                dv.wait_ge(S["pe_bxT"], k + 1)
                r, q = k // 3, 4 * (k % 3)
                v.tensor_copy(bxT[:, r, q:q + 4, :], bank[[3, 5, 7, 1, 3, 4][k]][:].rearrange("p (q s) -> p q s", q=4)).then_inc(S["bxT_done"], 1)

            dv.wait_ge(S["pe_x"], 1)
            dv.wait_ge(S["rot_ready"], 1)
            half = Q // 2 * NC
            cosv, sinv = rot[:, 0, :, 0:NC], rot[:, 1, :, 0:NC]

            def qc(ap):
                return ap.rearrange("p (q c) -> p q c", c=NC)
            for u in range(2):
                xr, xi = qc(bank[3 + u][:, 0:half]), qc(bank[5 + u][:, 0:half])
                cs, sn = cosv[:, 6 * u:6 * u + 6], sinv[:, 6 * u:6 * u + 6]
                cols = slice(u * half, (u + 1) * half)
                o_r, o_i = qc(x_rot[:, 0, cols]), qc(x_rot[:, 1, cols])
                t_r, t_i = qc(x_tmp[:, 0, cols]), qc(x_tmp[:, 1, cols])
                link(tt(o_r, xr, cs, ALU.mult))
                link(tt(t_r, xi, sn, ALU.mult))
                link(tt(o_i, xi, cs, ALU.mult))
                last = tt(t_i, xr, sn, ALU.mult)
                if u == 0:
                    link(last)
            last.then_inc(S["xrot_done"], 1)
            dv.wait_ge(S["xrot_done"], 1)
            link(tt(x_rot[:, 0, :], x_rot[:, 0, :], x_tmp[:, 0, :], ALU.add))
            link(tt(x_rot[:, 1, :], x_rot[:, 1, :], x_tmp[:, 1, :], ALU.subtract))
            for r in range(2):
                link(v.tensor_tensor_scan(x_rot[:, r, :], decay, x_rot[:, r, :], 0.0, ALU.mult, ALU.add))
            c0, c1_ = slice(0, NC - 1), slice(1, NC)
            s_r, s_i = qc(x_tmp[:, 0, :]), qc(x_tmp[:, 1, :])
            r_r, r_i = qc(x_rot[:, 0, :]), qc(x_rot[:, 1, :])
            tq = s_in.rearrange("p g c -> p (g c)")[:, 0:Q * NC].rearrange("p (q c) -> p q c", c=NC)
            link(v.memset(s_r[:, :, 0:1], 0.0))
            link(v.memset(s_i[:, :, 0:1], 0.0))
            link(tt(s_r[:, :, c1_], r_r[:, :, c0], cosv[:, :, c0], ALU.mult))
            link(tt(tq[:, :, c1_], r_i[:, :, c0], sinv[:, :, c0], ALU.mult))
            link(tt(s_r[:, :, c1_], s_r[:, :, c1_], tq[:, :, c1_], ALU.subtract))
            link(tt(s_i[:, :, c1_], r_i[:, :, c0], cosv[:, :, c0], ALU.mult))
            link(tt(tq[:, :, c1_], r_r[:, :, c0], sinv[:, :, c0], ALU.mult))
            tt(s_i[:, :, c1_], s_i[:, :, c1_], tq[:, :, c1_], ALU.add).then_inc(S["s_ready"], 1)

            def bias_max(h):
                dv.wait_ge(S["pe_s"], h + 1)
                if h == 0:
                    dv.wait_ge(S["rb_in"], 16)
                    dv.wait_ge(S["rot_ready"], 1)
                    dv.wait_ge(S["small_in"], 16)
                    dv.wait_ge(S["s_ready"], 1)
                if h >= 2:
                    dv.wait_ge(S["pe_pt"], 3 * h - 3)
                for i in range(NT):
                    b, c, o = SCORE_AT[i]
                    old = max(i - 1, 0) * P
                    near = (i + 1) * P - old
                    if old:
                        link(ts(prob[:, h % 2, o:o + old], bank[b][:, c:c + old], HD ** -0.5,
                                vec[:, V_RC + h:V_RC + h + 1], ALU.mult, ALU.add))
                    link(stt(prob[:, h % 2, o + old:o + old + near], bank[b][:, c + old:c + old + near], HD ** -0.5,
                             rbias[:, h, 256 - near:256], ALU.mult, ALU.add))
                for i in range(NT):
                    o, w = SCORE_AT[i][2], (i + 1) * P
                    last = v.tensor_reduce(att_mx[:, h % 2, i:i + 1], prob[:, h % 2, o:o + w], AX.X, ALU.max, negate=True)
                    if i < NT - 1:
                        link(last)
                last.then_inc(S["s_evac"], 1)

            def normalise(h):
                dv.wait_ge(S["p_exp"], h + 1)
                link(v.reciprocal(att_sm[:, h % 2, :], att_sm[:, h % 2, :]))
                for i in range(NT):
                    o, w = SCORE_AT[i][2], (i + 1) * P
                    last = ts(prob[:, h % 2, o:o + w], prob[:, h % 2, o:o + w], att_sm[:, h % 2, i:i + 1], None, ALU.mult)
                    if i < NT - 1:
                        link(last)
                last.then_inc(S["p_norm"], 1)

            bias_max(0)
            for h in range(HEADS):
                if h + 1 < HEADS:
                    bias_max(h + 1)
                normalise(h)
                if h == 3:
                    dv.wait_ge(S["y_back"], 16)
                    for m in range(3):
                        stt(yT[:, m, :], uT[:, m, :], vec[:, V_D + m:V_D + m + 1], yT[:, m, :], ALU.mult, ALU.add).then_inc(S["yin_ready"], 1)
            for m in range(3):
                dv.wait_ge(S["glu_sig"], m + 1)
                dv.wait_ge(S["pe_glu"], 3)
                tt(hdT[:, 5 + m, :], hdT[:, 5 + m, :], sgl[:, m, :], ALU.mult).then_inc(S["ssm_done"], 1)
            k = 0
            for g, tiles in enumerate([(0, 1), (5, 6, 7), (2, 3, 4)]):
                dv.wait_ge(S["rms_sqrt"], g + 1)
                dv.wait_ge(S["sq_done"], 8)
                link(v.reciprocal(rstdB[:, g, :], rstdB[:, g, :]))
                for m in tiles:
                    stt(hdT[:, m, :], hdT[:, m, :], vec[:, V_GAIN + m:V_GAIN + m + 1], rstdB[:, g, :], ALU.mult, ALU.mult).then_inc(S["heads_ready"], 1)
            dv.wait_ge(S["xh_in"], 16)
            dv.wait_ge(S["ln_in"], 32)

            def normalise_rows(t, signal, sqrt_signal, count):
                link(v.reciprocal(ln_rs[:, t, 1:2], ln_rs[:, t, 0:1]))
                link(ts(xh[:, t, :], xh[:, t, :], ln_mv[:, t, 0:1], ln_rs[:, t, 1:2], ALU.subtract, ALU.mult))
                link(tt(xh[:, t, :], xh[:, t, :], lng, ALU.mult))
                tt(xh[:, t, :], xh[:, t, :], lnb, ALU.add).then_inc(S[signal], 1)

            for t in range(NT):
                for half_ in range(2):
                    k = 2 * t + half_
                    dv.wait_ge(S["pe_wo"], k + 1)
                    cols = slice(half_ * 512, half_ * 512 + 512)
                    link(stt(xh[:, t, cols], xh[:, t, cols], ALPHA, bank[WO_AT[t] + half_][:], ALU.mult, ALU.add))
                    link(v.bn_stats(ln_st[:, t, 6 * half_:6 * half_ + 6], xh[:, t, cols]))
                v.bn_aggr(ln_mv[:, t, :], ln_st[:, t, :]).then_inc(S["z_ready"], 1)
                dv.wait_ge(S["ln_sqrt"], t + 1)
                normalise_rows(t, "h_ready", "ln_sqrt", t + 1)

            def ple_sum(k):
                t, half_ = k // 2, k % 2
                dv.wait_ge(S["ple_sig"], k + 1)
                dv.wait_ge(S["pe_pp"], k + 1)
                if half_ == 0:
                    dv.wait_ge(S["pe_hT"], 2 * t + 2)
                    dv.wait_ge(S[f"h_out{t}"], 16)
                cols = slice(half_ * 512, half_ * 512 + 512)
                link(tt(ple_t[:, cols], ple_t[:, cols], bank[4 + k % 2][:], ALU.mult))
                stt(xh[:, t, cols], xh[:, t, cols], ALPHA, ple_t[:, cols], ALU.mult, ALU.add).then_inc(S["ple_done"], 1)
            ple_sum(0)
            ple_sum(1)

            W3 = [P, NT, NE]

            def view(k, n_=NT * NE):
                return rt[:, 64 * k:64 * k + n_]
            b_s = view(1).rearrange("p (t e) -> p t e", t=NT)
            pairs = rt[:, 128:128 + NT * EG * 6].rearrange("p (t g c) -> p t g c", t=NT, g=EG)
            gs = rt[:, 224:240].rearrange("p (t g) -> p t g", t=NT)
            key = rt[:, 240:256].rearrange("p (t g) -> p t g", t=NT)
            ingr = rt[:, 256:272].rearrange("p (t g) -> p t g", t=NT)
            m4 = rt[:, 272:276]
            m4b = rt[:, 276:280]
            wsum = rt[:, 280:284]
            msk = view(5).rearrange("p (t e) -> p t e", t=NT)
            tie = view(6).rearrange("p (t e) -> p t e", t=NT)
            sel = [view(7).rearrange("p (t e) -> p t e", t=NT), view(8).rearrange("p (t e) -> p t e", t=NT)]
            slot = view(9).rearrange("p (t e) -> p t e", t=NT)
            low = view(10).rearrange("p (t e) -> p t e", t=NT)
            tc = view(11).rearrange("p (t e) -> p t e", t=NT)
            dv.wait_ge(S["sig_rt"], 1)
            s_v = r_s.rearrange("p (t e) -> p t e", t=NT)
            link(tt(b_s, s_v, vec[:, V_RB:V_RB + NE].unsqueeze(1).broadcast_to(W3), ALU.add))
            bg = view(1).rearrange("p (t g c) -> p t g c", t=NT, g=EG)
            link(tt(pairs[:, :, :, 0:3], bg[:, :, :, 0:3], bg[:, :, :, 1:4], ALU.add))
            link(tt(pairs[:, :, :, 3:5], bg[:, :, :, 0:2], bg[:, :, :, 2:4], ALU.add))
            link(tt(pairs[:, :, :, 5:6], bg[:, :, :, 0:1], bg[:, :, :, 3:4], ALU.add))
            link(v.tensor_reduce(gs, pairs, AX.X, ALU.max))

            def first_max(out_, in_, mx, keyb, order, width):
                s__ = [P, NT, width]
                link(v.tensor_reduce(mx, in_, AX.X, ALU.max))
                link(tt(keyb, in_, mx.unsqueeze(2).broadcast_to(s__), ALU.is_equal))
                link(tt(keyb, keyb, order, ALU.mult))
                link(v.tensor_reduce(mx, keyb, AX.X, ALU.max))
                link(tt(out_, keyb, mx.unsqueeze(2).broadcast_to(s__), ALU.is_equal))

            link(ts(tc[:, 0, :], e_off[:], -1.0, float(NE * CAP), ALU.mult, ALU.add))
            link(v.tensor_copy(low, tc[:, 0:1, :].broadcast_to(W3)))
            first_max(ingr, gs, m4, key, low[:, :, 0:EG], EG)
            ig4 = ingr.unsqueeze(3).broadcast_to([P, NT, EG, EPG])
            mk4 = view(5).rearrange("p (t g c) -> p t g c", t=NT, g=EG)
            link(tt(mk4, bg, ig4, ALU.mult))
            link(ts(ingr, ingr, BIG, -BIG, ALU.mult, ALU.add))
            link(tt(mk4, mk4, ig4, ALU.add))
            for k in range(2):
                first_max(sel[k], msk, m4, tie, low, NE)
                link(tt(tie, s_v, sel[k], ALU.mult))
                link(v.tensor_reduce(wgt[:, k, :], tie, AX.X, ALU.add))
                if k == 0:
                    link(ts(tie, sel[0], -BIG, None, ALU.mult))
                    link(tt(msk, msk, tie, ALU.add))
            link(tt(wsum, wgt[:, 0, :], wgt[:, 1, :], ALU.add))
            link(v.reciprocal(wsum, wsum))
            for k in range(2):
                link(tt(wgt[:, k, :], wgt[:, k, :], wsum, ALU.mult))
            tt(r_sel, sel[0], sel[1], ALU.add).then_inc(S["sel_ready"], 1)
            dv.wait_ge(S["pe_cnt"], 1)
            cnt, more, cum, base = (rt[:, 768 + 16 * k:784 + 16 * k] for k in range(4))
            link(v.tensor_copy(cnt, bank[3][:, NT * NE:(NT + 1) * NE]))
            link(ts(more, cnt, float(CAP), None, ALU.is_gt))
            for k in (2, 3):
                link(stt(more, cnt, float(CAP * k), more, ALU.is_gt, ALU.add))
            link(v.tensor_tensor_scan(cum, ones[:, 0:NE], more, 0.0, ALU.mult, ALU.add))
            link(tt(base, cum, more, ALU.subtract))
            link(ts(base, base, float(CAP), float((NE - 1) * CAP), ALU.mult, ALU.add))
            link(v.tensor_copy(slot, bank[3][:, 0:NT * NE].rearrange("p (t e) -> p t e", t=NT)))
            link(ts(low, slot, float(CAP), None, ALU.is_lt))
            link(tt(cnt, e_off[:], base, ALU.subtract))
            link(tt(low, low, cnt.unsqueeze(1).broadcast_to(W3), ALU.mult))
            link(tt(slot, slot, low, ALU.add))
            link(tt(slot, slot, base.unsqueeze(1).broadcast_to(W3), ALU.add))
            for k in range(2):
                link(tt(tie, slot, sel[k], ALU.mult))
                link(v.tensor_reduce(m4b, tie, AX.X, ALU.add))
                last = v.tensor_copy(slot_i[:].rearrange("p (t k) -> p t k", k=2)[:, :, k], m4b)
                if k == 0:
                    link(last)
            last.then_inc(S["slots_ready"], 1)
            dv.wait_ge(S["slots_ready"], 1)
            le = rt[:, 832:832 + OVER * NE].rearrange("p (o e) -> p o e", o=OVER)
            ov = rt[:, 960:968]
            link(tt(le, cum.unsqueeze(1).broadcast_to([P, OVER, NE]), io_o[:].unsqueeze(2).broadcast_to([P, OVER, NE]), ALU.is_le))
            link(v.tensor_reduce(ov[:, 1:8], le, AX.X, ALU.add))
            link(v.tensor_copy(ov[:, 0:1], cum[:, NE - 1:NE]))
            link(ts(ov[:, 1:8], ov[:, 1:8], float(NE - 1), None, ALU.min))
            link(v.tensor_copy(over_i[:], ov[0:1, :]))

            for k in range(2, 4):
                ple_sum(k)
            dv.wait_ge(S["inv_back"], 16)
            ts(tok_t[:], inv_t[:], 1, None, ALU.arith_shift_right).then_inc(S["tok_ready"], 1)
            for k in range(4, 2 * NT):
                ple_sum(k)

            def y_copy(e, b, uses):
                dv.wait_ge(S["pe_dn"], e + 1)
                if not isinstance(uses, int) or uses > 1:
                    dv.wait_ge(S[f"ye_out{b}"], 16 * (uses - 1))
                v.tensor_copy(y_e[b][:, 0:512], bank[6][:])
                v.tensor_copy(y_e[b][:, 512:1024], bank[7][:]).then_inc(S["ye_evac"], 1)

            def gate_times_up(e, r):
                dv.wait_ge(S["silu_done"], e + 1)
                if not isinstance(e, int) or e >= 2:
                    dv.wait_ge(S["pe_aT"], e - 1)
                tt(act_e[:, r, 1, :], act_e[:, r, 0, :], bank[2 + r][:, DE:2 * DE], ALU.mult).then_inc(S["a_ready"], 1)

            gate_times_up(0, 0)
            for e in range(4):
                gate_times_up(e + 1, (e + 1) % 2)
                y_copy(e, e, 1)
            with dv.Fori(1, NE // 4 - 1) as blk:
                for b in range(4):
                    gate_times_up(4 * blk + (b + 1), (b + 1) % 2)
                    y_copy(4 * blk + b, b, blk + 1)
            for e in range(NE - 4, NE):
                if e + 1 < NE:
                    gate_times_up(e + 1, (e + 1) % 2)
                y_copy(e, e % 4, NE // 4)
            n_over = dv.value_load(over_i[0:1, 0:1], min_val=0, max_val=OVER)
            dv.wait_ge(S["ye_out0"], 16 * NE // 4)
            with dv.Fori(0, OVER) as o:
                with dv.If(o < n_over):
                    v.tensor_copy(cur_t[:, 0:1], tok_t[:, bass.ds(o + NE, 1)]).then_inc(S["o_c1"], 1)
                    v.tensor_copy(cur_t[:, 1:2], inv_t[:, bass.ds(o + NE, 1)]).then_inc(S["o_col"], 1)
                    dv.wait_ge(S["o_si"], o + 1)
                    tt(act_e[:, 0, 1, :], act_e[:, 0, 0, :], bank[2][:, DE:2 * DE], ALU.mult).then_inc(S["o_a"], 1)
                    dv.wait_ge(S["o_dn"], o + 1)
                    v.tensor_copy(y_e[0][:, 0:512], bank[6][:]).then_inc(S["o_ye"], 1)
                    v.tensor_copy(y_e[0][:, 512:1024], bank[7][:]).then_inc(S["o_ye"], 1)
                    dv.wait_ge(S["o_out"], 16 * (o + 1))
                    dv.sem_inc(S["o_round_dv"], 1)

            dv.wait_ge(S["ln2_in"], 32)

            def combine(t):
                for k in range(2):
                    dv.wait_ge(S[f"yk{k}_in{t}"], 16)
                    yk = RA[:, (2 * t + k) * D:(2 * t + k + 1) * D]
                    link(stt(xh[:, t, :], yk, wgt[:, k, t:t + 1], xh[:, t, :], ALU.mult, ALU.add))
                for half_ in range(2):
                    link(v.bn_stats(ln_st[:, t, 6 * half_:6 * half_ + 6], xh[:, t, half_ * 512:half_ * 512 + 512]))
                v.bn_aggr(ln_mv[:, t, :], ln_st[:, t, :]).then_inc(S["z2_ready"], 1)

            def scale_rows(t):
                dv.wait_ge(S["ln2_sqrt"], t + 1)
                link(v.reciprocal(ln_rs[:, t, 1:2], ln_rs[:, t, 0:1]))
                stt(ln_mv[:, t, 0:1], ln_mv[:, t, 0:1], -1.0, ln_rs[:, t, 1:2], ALU.mult, ALU.mult).then_inc(S["rs2_ready"], 1)

            def gain(t):
                dv.wait_ge(S["xhat_done"], t + 1)
                return tt(xh[:, t, :], xh[:, t, :], lng, ALU.mult)

            combine(0)
            for t in range(1, NT):
                scale_rows(t - 1)
                combine(t)
                gain(t - 1).then_inc(S["gain_done"], 1)
            scale_rows(NT - 1)
            link(gain(NT - 1))
            dv.wait_ge(S["o_g"], NT - 1)
            tt(xh[:, NT - 1, :], xh[:, NT - 1, :], lnb, ALU.add).then_inc(S["o_g"], 1)


def _lay_out(inputs):
    a = {k: np.asarray(v) for k, v in inputs.items()}

    def pair(v):
        w = v.reshape(Q, 2, NS, -1).transpose(1, 2, 0, 3)
        return w.reshape(P, Q, -1)

    def stacked(re, im):
        w = np.stack([re, im]).reshape(2, G, NS, -1).transpose(0, 2, 1, 3)
        return w.reshape(P, G, -1)

    def both(v):
        return np.concatenate([pair(v), stacked(v, v)], axis=1).reshape(P, -1)

    ldt = np.repeat(a["ssm_log_dt"][0][:, None], NS, axis=1)
    c_re, c_im = (a[k][0].transpose(0, 2, 1) for k in ("ssm_c_re", "ssm_c_im"))
    par = np.concatenate([both(a["ssm_a_re"][0]), both(a["ssm_a_im"][0]), both(ldt), both(a["ssm_b_re"][0]), both(a["ssm_b_im"][0]),
                          stacked(c_re, c_im).reshape(P, -1), stacked(c_im, c_re).reshape(P, -1)], axis=1)

    def cols(v):
        return v.reshape(-1, P).T

    gains = np.concatenate([a["g_pool"][0], a["g_attn"][0], a["g_ssm"][0]])
    vec = np.concatenate([cols(a["ssm_d"][0]), cols(a["b_glu"][0]), cols(gains), cols(a["pool_scale"][0]),
                          np.repeat(a["router_bias"][None], P, axis=0), np.repeat(a["rel_bias"][0][:, -1][None], P, axis=0)], axis=1)
    rel = np.arange(P)[:, None] + P - np.arange(2 * P)[None, :]
    tab = a["rel_bias"][0][:, np.clip(rel, -REL, REL) + REL]
    windows = np.repeat([2, 4, 8, 16], 64).reshape(2, P).T[:, :, None]
    rcnt = (1.0 / np.minimum(np.arange(T) + 1, windows)).astype(np.float32)
    return {
        "xT": a["x"][0].T, "x": a["x"][0], "pT": a["p"][0, 0].T, "w_in": a["w_in"][0], "w_out": a["w_out"][0],
        "w_pool": a["w_pool"][0], "rel_tab": tab.transpose(1, 0, 2), "ssm_par": par, "vec": vec, "rcnt": rcnt,
        "w_glu": a["w_glu"][0], "w_router": a["w_router"],
        "ln": np.stack([a["ln1_g"][0], a["ln1_b"][0], a["ln2_g"][0], a["ln2_b"][0]]),
        "w_exp_gate": a["w_exp_gate"][0], "w_exp_up": a["w_exp_up"][0], "w_exp_down": a["w_exp_down"][0],
        "w_ple_gate": a["w_ple_gate"][0], "w_ple_proj": a["w_ple_proj"][0],
    }


def kernel(**inputs):
    import concourse.bacc as bacc
    from concourse.bass_utils import run_bass_kernel_spmd

    nc = bacc.Bacc("TRN2", target_bir_lowering=False, num_devices=1)
    arrays = {k: np.ascontiguousarray(v) for k, v in _lay_out(inputs).items()}
    io = {k: nc.dram_tensor("in_" + k, v.shape, mybir.dt.from_np(v.dtype), kind="ExternalInput").ap() for k, v in arrays.items()}
    out = nc.dram_tensor("out", (T, D), F32, kind="ExternalOutput").ap()
    trunk(nc, io, out)
    r = run_bass_kernel_spmd(nc, [{"in_" + k: v for k, v in arrays.items()}], core_ids=[0])
    return r.results[0]["out"].reshape(1, T, D)
```

```python
from contextlib import ExitStack

import numpy as np

import concourse.bass as bass
from concourse import mybir

F32 = mybir.dt.float32
I32 = mybir.dt.int32
ALU = mybir.AluOpType
ACT = mybir.ActivationFunctionType
AX = mybir.AxisListType

P = 128
D = 1024
T = 512
NT = T // P
KD = D // P
POOL_W, ATT_W, SSM_W = 256, 384, 384
IN_W = POOL_W + 3 * ATT_W + SSM_W
HEADS, HD = 6, 64
REL = 128
G, GD, NS = 24, 16, 64
CH = 8
NC = T // CH
Q = G // 2
NE, DE = 16, 256
EG, EPG = 4, 4
PLE = 256
ALPHA = 2.0 ** 0.25
EPS = 1e-5
NEG = -1.0e30
BIG = 3.0e38
CAP = P
OVER = 7
SLOT_TILES = NE + OVER
PAD = 4096
ROUND = 1.5 * 2.0 ** 23
PI2_A = 6.28125
PI2_B = 0.00193500518798828125
PI2_C = float(2 * np.pi - PI2_A - PI2_B)
PI_SAFE = 3.1415925

NG = Q + G
C_ARE, C_AIM, C_LDT = 0, NG, 2 * NG
C_BRE = 3 * NG
C_BIM = C_BRE + NG * GD
C_CA = C_BIM + NG * GD
C_CB = C_CA + G * GD
SSM_COLS = C_CB + G * GD
V_D, V_BG, V_GAIN, V_PS, V_RB, V_RC = 0, 3, 6, 14, 16, 32
VEC_COLS = 38

FIRST_K = (0, 1, 2, 4, KD)
SCORE_AT = {0: (0, 0, 0), 2: (0, 128, 128), 3: (1, 0, 512), 1: (2, 0, 1024)}
MIX_AT = ((0, 1), (5, 6, 7), (2, 3, 4))
WO_AT = ((2, 6, 1), (7, 0, 3))
PG_AT, PP_AT = (2, 7), (1, 0)
B_ROUTER, B_COUNT = 6, 3
B_TOK, B_GU, B_ACT, B_DN = (4, 5), (3, 6), (7, 0), (1, 2)
PT_AT = {0: 0, 1: 512, 3: 896, 2: 1024}
PT_UNITS = [((0,), 0, 512), ((1, 3), 512, 512), ((2,), 1024, 256)]


def trunk(nc, io, out):
    with ExitStack() as ctx:
        def sb(name, shape, dt=F32):
            return ctx.enter_context(nc.sbuf_tensor(name, shape, dt))

        def sem(name):
            return ctx.enter_context(nc.semaphore(name))

        RA = sb("region_a", [P, 14336])
        RB = sb("region_b", [P, 8192])
        RC = sb("region_c", [P, 9600])
        RE = sb("region_e", [P, 4096])
        RF = sb("region_f", [P, 4096])
        RG = sb("region_g", [P, 4096])
        RH = sb("region_h", [P, 7680])
        ident = sb("ident", [P, P])
        ones = sb("ones", [P, P])
        tri = sb("tri", [P, P])
        vec = sb("vec", [P, VEC_COLS])
        w_rt = sb("w_rt", [P, KD, NE])
        w_pl = sb("w_pl", [P, 2, P])
        ln_st = sb("ln_st", [P, NT, 12])
        ln_mv = sb("ln_mv", [P, NT, 2])
        ln_rs = sb("ln_rs", [P, NT, 2])
        att_mx = sb("att_mx", [P, 3, 4])
        att_sm = sb("att_sm", [P, 3, 4])
        rms_r = sb("rms_r", [P, 3, NT])

        O_SSM, O_Q, O_K, O_V, O_PL = 0, KD * 384, KD * 768, KD * 1152, KD * 1536
        w_ssm = RA[:, O_SSM:O_SSM + KD * 384].rearrange("p (k n) -> p k n", k=KD)
        w_q = RA[:, O_Q:O_Q + KD * 384].rearrange("p (k n) -> p k n", k=KD)
        w_k = RA[:, O_K:O_K + KD * 384].rearrange("p (k n) -> p k n", k=KD)
        w_v = RA[:, O_V:O_V + KD * 384].rearrange("p (k n) -> p k n", k=KD)
        w_up = RA[:, O_PL:O_PL + KD * 256].rearrange("p (k n) -> p k n", k=KD)
        prob = RA[:, 0:3840].rearrange("p (r n) -> p r n", r=3)
        probT = RA[:, 3840:6400].rearrange("p (r n) -> p r n", r=2)
        x_rot = RA[:, 2304:3840].rearrange("p (r n) -> p r n", r=2)
        x_tmp = RA[:, 3840:5376].rearrange("p (r n) -> p r n", r=2)
        s_in = RA[:, 6400:7936].rearrange("p (g c) -> p g c", g=G)
        y_ch = RA[:, 7936:9472].rearrange("p (g c) -> p g c", g=G)
        sgl = RA[:, 7936:9472].rearrange("p (m t) -> p m t", m=3)
        yT = RA[:, 9472:11008].rearrange("p (m t) -> p m t", m=3)
        w_glu = RA[:, 11008:12160].rearrange("p (k n) -> p k n", k=3)
        ssum = RA[:, 12288:13824].rearrange("p (g t) -> p g t", g=3)
        par = RB[:, 0:SSM_COLS]
        bb = RB[:, 2028:3180].rearrange("p (r g h) -> p r g h", r=2, g=NG)
        b_st = RB[:, 3180:3564].rearrange("p (g h) -> p g h", g=G)
        tmp = RB[:, 3564:7020]
        pw = RB[:, 7020:7668].rearrange("p (r g l) -> p r g l", r=2, g=NG)
        sm = RB[:, 7668:8192]
        pl_s = RB[:, 3564:5612].rearrange("p (r m t) -> p r m t", r=2, m=2)
        rcnt = RB[:, 5612:6636].rearrange("p (k n) -> p k n", k=2)
        w_o = RB[:, :].rearrange("p (k n) -> p k n", k=KD)
        bx = RC[:, 0:3072].rearrange("p (r q j h) -> p r q j h", r=2, q=Q, j=CH)
        kern = RC[0:GD, 0:3072].rearrange("p (g l h) -> p g l h", g=G, l=CH)
        bxT = RC[:, 3072:6144].rearrange("p (r q s) -> p r q s", r=2, q=Q)
        cp = RC[:, 6144:9600].rearrange("p (g l h) -> p g l h", g=G, l=CH + 1)
        w_pg = RC[:, 0:8192].rearrange("p (k n) -> p k n", k=KD)
        rt = RC[:, 8192:9600]
        act_e = RC[:, 6144:7680].rearrange("p (r s n) -> p r s n", r=2, s=3)
        xT = RE[:, :].rearrange("p (k t) -> p k t", k=KD)
        hdT = RE[:, :].rearrange("p (k t) -> p k t", k=KD)
        hg = RE[:, :].rearrange("p (r n) -> p r n", r=4)
        rbias = RF[:, 0:1536].rearrange("p (h n) -> p h n", h=HEADS)
        rot = RF[:, 1536:3096].rearrange("p (r q c) -> p r q c", r=2, q=Q)
        decay = RF[:, 3096:3864]
        xh = RF[:, :].rearrange("p (t d) -> p t d", t=NT)
        qT = RG[:, 0:1536].rearrange("p (m t) -> p m t", m=3)
        kT = RG[:, 1536:3072].rearrange("p (m t) -> p m t", m=3)
        plT = RG[:, 3072:4096].rearrange("p (m t) -> p m t", m=2)
        hT = RG[:, :].rearrange("p (k t) -> p k t", k=KD)
        hgT = RG[:, 0:2048].rearrange("p (r k s) -> p r k s", r=2, k=KD)
        y_e = [RG[:, 2048:3072], RG[:, 3072:4096], RB[:, 6144:7168], RB[:, 7168:8192]]
        uT = RH[:, 0:1536].rearrange("p (m t) -> p m t", m=3)
        uch = RH[:, 1536:3072].rearrange("p (g c) -> p g c", g=G)
        m0 = RH[:, 3072:6144].rearrange("p (g l h) -> p g l h", g=G, l=CH)
        vN = RH[:, 6144:7680].rearrange("p (t n) -> p t n", t=NT)
        w_pp = RH[:, 0:2048].rearrange("p (k n) -> p k n", k=2)
        pT = RH[:, 2048:3072].rearrange("p (k t) -> p k t", k=2)
        lng = RH[:, 3072:4096]
        lnb = RH[:, 4096:5120]
        ple_t = RH[:, 5120:6144]
        rtT = RH[0:NE, 6144:6144 + T]
        sq2 = RH[:, 5120:6144].rearrange("p (r n) -> p r n", r=2)
        ebuf = [RA[:, 0:6144], RA[:, 6144:12288], RB[:, 0:6144], RC[:, 0:6144]]

        bank = [ctx.enter_context(nc.psum_tensor(f"bank{i}", [P, 512], F32)) for i in range(8)]

        def dram(name, shape, dt=F32):
            return nc.dram_tensor(name, shape, dt, kind="Internal").ap()
        u_d = dram("u_scratch", (SSM_W, T))
        y_d = dram("y_scratch", (SSM_W, T))
        h_d = dram("h_scratch", (T, D))
        inv_d = dram("slot_scratch", (SLOT_TILES * P, 1), I32)
        ye_d = dram("expert_scratch", (2 * T, D))

        dt_, expo, ang, turns, angr, sinf, sinh = (
            sm[:, lo:lo + w] for lo, w in ((0, 36), (36, 48), (84, 48), (132, 48), (180, 48), (228, 48), (276, 48)))
        u8 = sm[:, 324:348].rearrange("p (r q) -> p r q", r=2)
        mag8 = sm[:, 348:360]
        r_s = rt[:, 0:NT * NE]
        r_sel = rt[:, 1024:1024 + NT * NE].rearrange("p (t e) -> p t e", t=NT)
        eps_t = sb("eps_t", [P, 1])

        io_t = sb("io_t", [P, 2 * NT], I32)
        pad_t = sb("pad_t", [P, SLOT_TILES], I32)
        slot_i = sb("slot_i", [P, 2 * NT], I32)
        inv_t = sb("inv_t", [P, SLOT_TILES], I32)
        tok_t = sb("tok_t", [P, SLOT_TILES], I32)
        cur_t = sb("cur_t", [P, 2], I32)
        over_i = sb("over_i", [1, 8], I32)
        e_off = sb("e_off", [P, NE])
        io_o = sb("io_o", [P, OVER])
        wgt = sb("wgt", [P, 2, NT])

        S = {n: sem(n) for n in (
            "x_in0 x_in1 x_in2 x_in3 wqk_in wv_in wup_in small_in par_in rb_in wpl_in wrt_in wglu_in rc_in "
            "wo_in wpg_in wpp_in pT_in ln_in xh_in "
            "const_set dve_step act_step gp_step uT_done qk_done pool_in_done v_done bx_ready bxT_done "
            "cp_ready kern_done rot_ready xrot_done "
            "u_out u_back m0_in s_ready s_moved y_evac y_out y_back yin_ready gelu_done glu_sig ssm_done "
            "pool_ready pool_mixed pe_u pe_qk pe_pool pe_v pe_bxT pe_kern pe_x pe_s pe_pt pe_pv pe_pm pe_y "
            "pe_glu s_read s_max p_exp p_norm pt_evac pv_evac sq_done sq_added pe_sq rms_sqrt rms_ready wo_scaled x_scaled wo_read pe_wo "
            "ang trig rt_by_token sel_ready o_c1 z_ready ln_sqrt h_ready pe_hT hT_evac h_out0 h_out1 h_out2 h_out3 pe_rt sig_rt pe_cnt slots_ready inv_set inv_put "
            "inv_back tok_ready pe_pg pe_pp ple_sig ple_done "
            "e_in0 e_in1 e_in2 e_in3 hg_in0 hg_in1 hg_in2 hg_in3 ye_out0 ye_out1 ye_out2 ye_out3 pe_hgT hgT_evac pe_gu silu_done a_ready "
            "pe_aT aT_evac pe_dn ye_evac moe_done "
            "o_col o_in o_hg o_t o_te o_gu o_si o_a o_at o_ae o_dn o_ye o_out o_round_sp o_round_gp o_round_dv "
            "yk0_in0 yk0_in1 yk0_in2 yk0_in3 yk1_in0 yk1_in1 yk1_in2 yk1_in3 z2_ready ln2_sqrt ln2_in rs2_ready var2_done xhat_done o_pool o_dve out_st").split()}

        block = ctx.enter_context(nc.Block())

        w_in_v = io["w_in"].rearrange("(p k) n -> p k n", k=KD)
        eg_v = io["w_exp_gate"].rearrange("e (p k) n -> e p (k n)", k=KD)
        eu_v = io["w_exp_up"].rearrange("e (p k) n -> e p (k n)", k=KD)
        ed_v = io["w_exp_down"].rearrange("e (p k) n -> e p (k n)", k=2)

        @block.sync
        def _(sp):
            def load(dst, src, signal):
                sp.dma_start(dst, src).then_inc(S[signal], 16)

            xv = io["xT"].rearrange("(p k) t -> p k t", k=KD)
            for i in range(4):
                ks = slice(FIRST_K[i], FIRST_K[i + 1])
                load(xT[:, ks, :], xv[:, ks, :], f"x_in{i}")
                load(w_ssm[:, ks, :], w_in_v[:, ks, POOL_W + 3 * ATT_W:IN_W], f"x_in{i}")
            load(par, io["ssm_par"], "par_in")
            load(w_q, w_in_v[:, :, POOL_W:POOL_W + ATT_W], "wqk_in")
            load(w_k, w_in_v[:, :, POOL_W + ATT_W:POOL_W + 2 * ATT_W], "wqk_in")
            load(w_up, w_in_v[:, :, 0:POOL_W], "wup_in")
            load(w_v, w_in_v[:, :, POOL_W + 2 * ATT_W:POOL_W + 3 * ATT_W], "wv_in")
            load(rbias, io["rel_tab"], "rb_in")
            sp.wait_ge(S["cp_ready"], 1)
            load(rcnt, io["rcnt"], "rc_in")
            sp.wait_ge(S["const_set"], 1)
            sp.wait_ge(S["kern_done"], 6)
            for j in range(CH):
                sp.dma_start(m0[GD * j:GD * (j + 1), :, j:CH, :], kern[:, :, 0:CH - j, :]).then_inc(S["m0_in"], 16)
            sp.wait_ge(S["s_ready"], 1)
            sv = s_in.rearrange("p (q r) c -> p q r c", r=2)
            for r in range(2):
                for par_ in range(2):
                    sp.dma_start(sv[64 * r:64 * r + 64, :, par_, :],
                                 x_tmp[64 * par_:64 * par_ + 64, r, :].rearrange("p (q c) -> p q c", q=Q)).then_inc(S["s_moved"], 16)
            sp.wait_ge(S["pe_v"], NT)
            load(w_glu, io["w_glu"].rearrange("(k p) n -> p k n", p=P), "wglu_in")
            sp.wait_ge(S["rot_ready"], 1)
            sp.wait_ge(S["pe_pm"], 2)
            load(w_o, io["w_out"].rearrange("(k p) n -> p k n", p=P), "wo_in")
            sp.wait_ge(S["y_evac"], 3)
            for j in range(CH):
                sp.dma_start(y_d.rearrange("(g h) (j c) -> j h g c", h=GD, j=CH)[j],
                             y_ch[GD * j:GD * (j + 1), :, :]).then_inc(S["y_out"], 16)
            sp.wait_ge(S["y_out"], 16 * CH)
            load(yT, y_d.rearrange("(m p) t -> p m t", p=P), "y_back")
            load(w_pg, io["w_ple_gate"].rearrange("(p k) n -> p k n", k=KD), "wpg_in")
            load(lng, io["ln"][0:1, :].partition_broadcast(P), "ln_in")
            load(lnb, io["ln"][1:2, :].partition_broadcast(P), "ln_in")
            sp.wait_ge(S["yin_ready"], 3)
            load(w_pp, io["w_ple_proj"].rearrange("(k p) n -> p k n", p=P), "wpp_in")
            load(pT, io["pT"].rearrange("(k p) t -> p k t", p=P), "pT_in")
            sp.wait_ge(S["s_read"], HEADS)
            load(xh, io["x"].rearrange("(t p) d -> p t d", p=P), "xh_in")
            sp.wait_ge(S["pe_pv"], HEADS)
            sp.wait_ge(S["ssm_done"], 3)

            def load_expert(b, e, first=False):
                sp.dma_start(ebuf[b][:, 0:2048], eg_v[e]).then_inc(S[f"e_in{b}"], 16)
                sp.dma_start(ebuf[b][:, 2048:4096], eu_v[e]).then_inc(S[f"e_in{b}"], 16)
                sp.dma_start(ebuf[b][:, 4096:6144], ed_v[e]).then_inc(S[f"e_in{b}"], 16)

            load_expert(0, 0)
            load_expert(1, 1)
            for t in range(NT):
                sp.wait_ge(S["h_ready"], t + 1)
                sp.dma_start(h_d[t * P:(t + 1) * P, :], xh[:, t, :]).then_inc(S[f"h_out{t}"], 16)
            load(lng, io["ln"][2:3, :].partition_broadcast(P), "ln2_in")
            load(lnb, io["ln"][3:4, :].partition_broadcast(P), "ln2_in")
            sp.wait_ge(S["pe_wo"], 2 * NT)
            load_expert(2, 2)
            sp.wait_ge(S["pe_pg"], 2 * NT)
            load_expert(3, 3)
            with sp.Fori(0, 3) as blk:
                for b in range(4):
                    sp.wait_ge(S["pe_dn"], 4 * blk + b + 1)
                    e = blk * 4 + (4 + b)
                    sp.dma_start(ebuf[b][:, 0:2048], eg_v[bass.ds(e, 1)].rearrange("o p n -> p (o n)")).then_inc(S[f"e_in{b}"], 16)
                    sp.dma_start(ebuf[b][:, 2048:4096], eu_v[bass.ds(e, 1)].rearrange("o p n -> p (o n)")).then_inc(S[f"e_in{b}"], 16)
                    sp.dma_start(ebuf[b][:, 4096:6144], ed_v[bass.ds(e, 1)].rearrange("o p n -> p (o n)")).then_inc(S[f"e_in{b}"], 16)
            sp.wait_ge(S["tok_ready"], 1)
            n_over = sp.value_load(over_i[0:1, 0:1], min_val=0, max_val=OVER)
            sp.wait_ge(S["pe_dn"], NE)
            with sp.If(n_over > 0):
                with sp.Fori(0, OVER) as o:
                    with sp.If(o < n_over):
                        e = sp.value_load(over_i[0:1, bass.ds(o + 1, 1)], min_val=0, max_val=NE - 1)
                        sp.wait_ge(S["o_col"], o + 1)
                        sp.dma_start(ebuf[0][:, 0:2048], eg_v[bass.ds(e, 1)].rearrange("o p n -> p (o n)")).then_inc(S["o_in"], 16)
                        sp.dma_start(ebuf[0][:, 2048:4096], eu_v[bass.ds(e, 1)].rearrange("o p n -> p (o n)")).then_inc(S["o_in"], 16)
                        sp.dma_start(ebuf[0][:, 4096:6144], ed_v[bass.ds(e, 1)].rearrange("o p n -> p (o n)")).then_inc(S["o_in"], 16)
                        sp.wait_ge(S["o_out"], 16 * (o + 1))
                        sp.sem_inc(S["o_round_sp"], 1)
            sp.wait_ge(S["moe_done"], 1)
            yv = ye_d.rearrange("(t p k) d -> t k p d", p=P, k=2)
            for t in range(NT):
                for k in range(2):
                    sp.dma_start(RA[:, (2 * t + k) * D:(2 * t + k + 1) * D], yv[t, k]).then_inc(S[f"yk{k}_in{t}"], 16)
            for t, signal, count in ((0, "o_pool", 1), (2, "o_dve", 1), (1, "o_pool", 2), (3, "o_dve", 2)):
                sp.wait_ge(S[signal], count)
                sp.dma_start(out[t * P:(t + 1) * P, :], xh[:, t, :]).then_inc(S["out_st"], 16)
            sp.wait_ge(S["out_st"], 16 * NT)

        @block.gpsimd
        def _(gp):
            n = [0]

            def link(ins):
                n[0] += 1
                ins.then_inc(S["gp_step"], 1)
                gp.wait_ge(S["gp_step"], n[0])

            g = nc.gpsimd
            link(g.memset(ident[:], 0.0))
            link(g.memset(ones[:], 1.0))
            link(g.affine_select(out=ident[:], in_=ident[:], compare_op=ALU.not_equal, fill=1.0, base=0,
                                 pattern=[[-1, P]], channel_multiplier=1))
            link(g.affine_select(out=tri[:], in_=ones[:], compare_op=ALU.is_gt, fill=0.0, base=0,
                                 pattern=[[1, P]], channel_multiplier=-1))
            link(g.memset(w_pl[:], 0.0))
            link(g.memset(m0, 0.0))
            link(g.iota(io_t[:].rearrange("p (t k) -> p t k", k=2), pattern=[[2 * P, NT], [1, 2]], base=0, channel_multiplier=2))
            link(g.iota(pad_t[:], pattern=[[0, SLOT_TILES]], base=PAD, channel_multiplier=0))
            link(g.iota(e_off[:], pattern=[[CAP, NE]], base=0, channel_multiplier=0, allow_small_or_imprecise_dtypes=True))
            g.iota(io_o[:], pattern=[[1, OVER]], base=0, channel_multiplier=0,
                   allow_small_or_imprecise_dtypes=True).then_inc(S["const_set"], 1)
            gp.wait_ge(S["const_set"], 1)
            for i in range(4):
                h, m = i % 2, i // 2
                gp.dma_start(w_pl[64 * h:64 * h + 64, m, 64 * h:64 * h + 64], io["w_pool"][i]).then_inc(S["wpl_in"], 16)
            gp.dma_start(inv_d.rearrange("(p c) o -> p (c o)", p=P), pad_t[:]).then_inc(S["inv_set"], 16)
            gp.wait_ge(S["rb_in"], 16)
            link(g.memset(rbias[0:64, :, 192:256], NEG))

            gp.wait_ge(S["bx_ready"], 1)
            tmp_g = decay
            link(g.memset(rot[:, 0, :, 0:1], 1.0))
            link(g.memset(rot[:, 1, :, 0:1], 0.0))
            link(g.tensor_copy(rot[:, 0, :, 1:2], u8[:, 0, :].unsqueeze(2)))
            link(g.tensor_copy(rot[:, 1, :, 1:2], u8[:, 1, :].unsqueeze(2)))
            m = 1
            while m < NC:
                shape = [P, Q, m]
                t = tmp_g[:, 0:Q * m].rearrange("p (q c) -> p q c", q=Q)
                ar, ai = rot[:, 0, :, 1:m + 1], rot[:, 1, :, 1:m + 1]
                br = rot[:, 0, :, m:m + 1].broadcast_to(shape)
                bi = rot[:, 1, :, m:m + 1].broadcast_to(shape)
                orr, oi = rot[:, 0, :, m + 1:2 * m + 1], rot[:, 1, :, m + 1:2 * m + 1]
                link(g.tensor_tensor(t, ai, bi, ALU.mult))
                link(g.tensor_tensor(orr, ar, br, ALU.mult))
                link(g.tensor_tensor(orr, orr, t, ALU.subtract))
                link(g.tensor_tensor(t, ar, bi, ALU.mult))
                link(g.tensor_tensor(oi, ai, br, ALU.mult))
                link(g.tensor_tensor(oi, oi, t, ALU.add))
                m *= 2
            dec = decay.rearrange("p (q c) -> p q c", q=Q)
            link(g.tensor_copy(dec, mag8[:].unsqueeze(2).broadcast_to([P, Q, NC])))
            g.memset(dec[:, :, 0:1], 0.0).then_inc(S["rot_ready"], 1)
            gp.wait_ge(S["rot_ready"], 1)

            gp.wait_ge(S["pool_in_done"], 2)
            gp.wait_ge(S["cp_ready"], 1)
            a, b2 = pl_s[:, 0], pl_s[:, 1]

            def add_shift(o, i, w, lo, ms):
                link(g.tensor_copy(o[lo:P, ms, 0:w], i[lo:P, ms, 0:w]))
                link(g.tensor_tensor(o[lo:P, ms, w:T], i[lo:P, ms, w:T], i[lo:P, ms, 0:T - w], ALU.add))

            both, second = slice(0, 2), slice(1, 2)
            add_shift(a, plT, 1, 0, both)
            add_shift(b2, a, 2, 0, second)
            add_shift(b2, a, 2, 64, slice(0, 1))
            link(g.tensor_copy(a[64:P, 0:1], b2[64:P, 0:1]))
            add_shift(a, b2, 4, 0, second)
            link(g.tensor_copy(b2[64:P, 1:2], a[64:P, 1:2]))
            add_shift(a, b2, 8, 64, second)
            gp.wait_ge(S["rc_in"], 16)
            link(g.tensor_tensor(a, a, rcnt, ALU.mult))
            g.tensor_tensor(a, a, plT, ALU.subtract).then_inc(S["pool_ready"], 1)

            gp.wait_ge(S["wo_in"], 16)
            gp.wait_ge(S["small_in"], 16)
            for k in (0, 1, 5, 6, 7, 2, 3, 4):
                g.tensor_scalar(w_o[:, k, :], w_o[:, k, :], vec[:, V_GAIN + k:V_GAIN + k + 1], None, ALU.mult).then_inc(S["wo_scaled"], 1)

            def add_squares(i, group, r):
                gp.wait_ge(S["sq_done"], (2, 4, 6, 7, 8)[i])
                g.tensor_tensor(ssum[:, group, :], ssum[:, group, :], sq2[:, r, :], ALU.add).then_inc(S["sq_added"], 1)
                gp.wait_ge(S["sq_added"], i + 1)

            def scale_x(t):
                g.tensor_scalar(xh[:, t, :], xh[:, t, :], ALPHA, None, ALU.mult).then_inc(S["x_scaled"], 1)

            add_squares(0, 0, 0)
            add_squares(1, 2, 1)
            gp.wait_ge(S["xh_in"], 16)
            scale_x(0)
            add_squares(2, 1, 0)
            add_squares(3, 1, 1)
            add_squares(4, 2, 0)
            for t in range(1, NT):
                scale_x(t)

            gp.wait_ge(S["pe_wo"], 2 * NT)
            link(g.memset(RE[:, :], 0.0))
            gp.wait_ge(S["slots_ready"], 1)
            gp.wait_ge(S["inv_set"], 16)
            for i in range(NT):
                for k in range(2):
                    gp.indirect_dma_start(
                        out=inv_d, out_offset=bass.IndirectOffsetOnAxis(ap=slot_i[:, 2 * i + k:2 * i + k + 1], axis=0),
                        in_=io_t[:, 2 * i + k:2 * i + k + 1], in_offset=None,
                        bounds_check=SLOT_TILES * P - 1, oob_is_err=False).then_inc(S["inv_put"], 16)
            gp.wait_ge(S["inv_put"], 16 * 2 * NT)
            gp.dma_start(inv_t[:], inv_d.rearrange("(c p) o -> p (c o)", p=P), allow_slow_non_contiguous=True).then_inc(S["inv_back"], 16)

            def gather(dst, idx, signal):
                gp.indirect_dma_start(out=dst, out_offset=None, in_=h_d,
                                      in_offset=bass.IndirectOffsetOnAxis(ap=idx, axis=0),
                                      bounds_check=T - 1, oob_is_err=False).then_inc(S[signal], 16)

            def scatter(idx, src, signal):
                gp.indirect_dma_start(out=ye_d, out_offset=bass.IndirectOffsetOnAxis(ap=idx, axis=0),
                                      in_=src, in_offset=None,
                                      bounds_check=2 * T - 1, oob_is_err=False).then_inc(S[signal], 16)

            gp.wait_ge(S["tok_ready"], 1)
            for t in range(NT):
                gp.wait_ge(S[f"h_out{t}"], 16)
            for e in range(4):
                gather(hg[:, e, :], tok_t[:, e:e + 1], f"hg_in{e}")
            for e in range(NE):
                if e + 4 < NE:
                    gp.wait_ge(S["pe_hgT"], e + 1)
                    gather(hg[:, e % 4, :], tok_t[:, e + 4:e + 5], f"hg_in{e % 4}")
                gp.wait_ge(S["ye_evac"], e + 1)
                scatter(inv_t[:, e:e + 1], y_e[e % 4], f"ye_out{e % 4}")
            n_over = gp.value_load(over_i[0:1, 0:1], min_val=0, max_val=OVER)
            for b in range(4):
                gp.wait_ge(S[f"ye_out{b}"], 16 * NE // 4)
            with gp.If(n_over > 0):
                with gp.Fori(0, OVER) as o:
                    with gp.If(o < n_over):
                        gp.wait_ge(S["o_col"], o + 1)
                        gp.sem_inc(S["o_round_gp"], 1)
                        gather(hg[:, 0, :], cur_t[:, 0:1], "o_hg")
                        gp.wait_ge(S["o_ye"], 2 * o + 2)
                        gp.sem_inc(S["o_round_gp"], 1)
                        scatter(cur_t[:, 1:2], y_e[0], "o_out")
                        gp.wait_ge(S["o_out"], 16 * (o + 1))
                        gp.sem_inc(S["o_round_gp"], 1)
            gp.sem_inc(S["moe_done"], 1)
            gp.wait_ge(S["ln2_in"], 32)
            for t in range(2):
                gp.wait_ge(S["xhat_done"], t + 1)
                link(g.tensor_tensor(xh[:, t, :], xh[:, t, :], lng, ALU.mult))
                g.tensor_tensor(xh[:, t, :], xh[:, t, :], lnb, ALU.add).then_inc(S["o_pool"], 1)

        @block.scalar
        def _(ac):
            a = nc.scalar
            n = [0]

            def link(ins):
                n[0] += 1
                ins.then_inc(S["act_step"], 1)
                ac.wait_ge(S["act_step"], n[0])

            ac.dma_start(vec[:], io["vec"]).then_inc(S["small_in"], 16)
            ac.dma_start(w_rt[:], io["w_router"].rearrange("(p k) n -> p k n", k=KD)).then_inc(S["wrt_in"], 16)

            ac.wait_ge(S["small_in"], 16)
            ac.wait_ge(S["par_in"], 16)
            link(a.activation(par[64:P, C_CA:C_CB], par[64:P, C_CA:C_CB], ACT.Copy, scale=-1.0))
            link(a.activation(par[:, C_CB:SSM_COLS], par[:, C_CB:SSM_COLS], ACT.Copy, scale=-1.0))
            link(a.activation(dt_[:], par[:, C_LDT:C_LDT + NG], ACT.Exp))
            ac.wait_ge(S["ang"], 1)
            link(a.activation(expo[:], expo[:], ACT.Exp))
            link(a.activation(sinf[:], angr[:], ACT.Sin))
            a.activation(sinh[:], angr[:], ACT.Sin, scale=0.5).then_inc(S["trig"], 1)
            for m in range(3):
                ac.wait_ge(S["pe_u"], m + 1)
                a.activation(uT[:, m, :].rearrange("p (j c) -> p j c", j=CH),
                             bank[m][:].rearrange("p (c j) -> p j c", j=CH), ACT.Copy).then_inc(S["uT_done"], 1)
                ac.wait_ge(S["uT_done"], m + 1)
                ac.dma_start(u_d[m * P:(m + 1) * P, :], uT[:, m, :]).then_inc(S["u_out"], 16)
            for m in range(6):
                ac.wait_ge(S["pe_qk"], m + 1)
                dst = (qT if m % 2 == 0 else kT)[:, m // 2, :]
                a.activation(dst, bank[(3 + m) % 8][:], ACT.Copy).then_inc(S["qk_done"], 1)
                if m == 0:
                    ac.wait_ge(S["u_out"], 48)
                    for j in range(CH):
                        ac.dma_start(uch[GD * j:GD * (j + 1), :, :],
                                     u_d.rearrange("(g h) (j c) -> j h g c", h=GD, j=CH)[j]).then_inc(S["u_back"], 16)
            for m in range(6):
                ac.wait_ge(S["pe_kern"], m + 1)
                a.activation(kern[:, 4 * m:4 * m + 4], bank[(7 + m) % 8][0:GD, :].rearrange("p (g l h) -> p g l h", g=4, l=CH),
                             ACT.Copy).then_inc(S["kern_done"], 1)
            for m in range(2):
                ac.wait_ge(S["pe_pool"], m + 1)
                a.activation(plT[:, m, :], bank[3 + m][:], ACT.Copy).then_inc(S["pool_in_done"], 1)

            def v_copy(t):
                ac.wait_ge(S["pe_v"], t + 1)
                a.activation(vN[:, t, :], bank[[5, 6, 7, 3][t]][:, 0:ATT_W], ACT.Copy).then_inc(S["v_done"], 1)

            def exps(h):
                ac.wait_ge(S["s_max"], h + 1)
                for i in range(NT):
                    o, w = SCORE_AT[i][2], (i + 1) * P
                    blk = prob[:, h % 3, o:o + w]
                    last = a.activation(blk, blk, ACT.Exp, bias=att_mx[:, h % 3, i:i + 1],
                                        accum_out=att_sm[:, h % 3, i:i + 1])
                    if i < NT - 1:
                        link(last)
                last.then_inc(S["p_exp"], 1)

            def pt_copy(h):
                for u, (_, o, w) in enumerate(PT_UNITS):
                    k = 3 * h + u
                    ac.wait_ge(S["pe_pt"], k + 1)
                    if u == 0 and h >= 2:
                        ac.wait_ge(S["pe_pv"], h - 1)
                    a.activation(probT[:, h % 2, o:o + w], bank[3 + k % 2][:, 0:w], ACT.Copy).then_inc(S["pt_evac"], 1)

            def pv_copy(pair):
                ac.wait_ge(S["pe_pv"], 2 * pair + 2)
                a.activation(hdT[:, 2 + pair, :], bank[5 + pair % 2][:], ACT.Copy).then_inc(S["pv_evac"], 1)

            def square(i, m, dst):
                a.activation(dst, hdT[:, m, :], ACT.Square).then_inc(S["sq_done"], 1)

            v_copy(0)
            exps(0)
            v_copy(1)
            v_copy(2)
            exps(1)
            v_copy(3)
            for m in range(2):
                ac.wait_ge(S["pe_pm"], m + 1)
                a.activation(hdT[:, m, :], bank[4 + m][:], ACT.Copy, scale=vec[:, V_PS + m:V_PS + m + 1]).then_inc(S["pool_mixed"], 1)
            for m in range(3):
                ac.wait_ge(S["pe_y"], m + 1)
                a.activation(y_ch[:, 8 * m:8 * m + 8, :], bank[(6, 7, 5)[m]][:].rearrange("p (g c) -> p g c", g=8),
                             ACT.Copy).then_inc(S["y_evac"], 1)
            pt_copy(0)
            exps(2)
            ac.wait_ge(S["pool_mixed"], 2)
            square(0, 0, ssum[:, 0, :])
            square(1, 1, sq2[:, 0, :])
            pt_copy(1)
            pv_copy(0)
            exps(3)
            pt_copy(2)
            exps(4)
            for m in range(3):
                ac.wait_ge(S["yin_ready"], m + 1)
                a.activation(hdT[:, 5 + m, :].rearrange("p (c j) -> p c j", j=CH),
                             yT[:, m, :].rearrange("p (j c) -> p c j", j=CH), ACT.Gelu_apprx_tanh).then_inc(S["gelu_done"], 1)
            pt_copy(3)
            exps(5)
            pv_copy(1)
            ac.wait_ge(S["pv_evac"], 2)
            square(2, 2, ssum[:, 2, :])
            square(3, 3, sq2[:, 1, :])
            pt_copy(4)
            for m in range(3):
                ac.wait_ge(S["pe_glu"], m + 1)
                a.activation(sgl[:, m, :], bank[(7, 0, 1)[m]][:], ACT.Sigmoid, bias=vec[:, V_BG + m:V_BG + m + 1]).then_inc(S["glu_sig"], 1)
            pt_copy(5)
            ac.wait_ge(S["ssm_done"], 1)
            square(4, 5, ssum[:, 1, :])
            ac.wait_ge(S["ssm_done"], 2)
            ac.wait_ge(S["sq_added"], 1)
            square(5, 6, sq2[:, 0, :])
            ac.wait_ge(S["ssm_done"], 3)
            ac.wait_ge(S["sq_added"], 2)
            square(6, 7, sq2[:, 1, :])
            pv_copy(2)
            ac.wait_ge(S["pv_evac"], 3)
            ac.wait_ge(S["sq_added"], 3)
            square(7, 4, sq2[:, 0, :])
            ac.wait_ge(S["pe_sq"], 1)
            for g in range(3):
                a.activation(rms_r[:, g, :], bank[4][:, g * NT:(g + 1) * NT], ACT.Sqrt, bias=eps_t[:],
                             scale=[1.0 / POOL_W, 1.0 / SSM_W, 1.0 / ATT_W][g]).then_inc(S["rms_sqrt"], 1)
            def hT_copy(t):
                for u in range(2):
                    ac.wait_ge(S["pe_hT"], 2 * t + u + 1)
                    a.activation(hT[:, 4 * u:4 * u + 4, t * P:(t + 1) * P], bank[4 + u][:].rearrange("p (k t) -> p k t", k=4),
                                 ACT.Copy).then_inc(S["hT_evac"], 1)

            def ple_gate(k):
                ac.wait_ge(S["pe_pg"], k + 1)
                if k >= 2:
                    ac.wait_ge(S["ple_done"], k - 1)
                elif k == 0:
                    ac.wait_ge(S["sq_added"], 5)
                a.activation(ple_t[:, (k % 2) * 512:(k % 2) * 512 + 512], bank[PG_AT[k % 2]][:], ACT.Sigmoid).then_inc(S["ple_sig"], 1)

            for t in range(NT):
                ac.wait_ge(S["z_ready"], t + 1)
                a.activation(ln_rs[:, t, 0:1], ln_mv[:, t, 1:2], ACT.Sqrt, bias=eps_t[:]).then_inc(S["ln_sqrt"], 1)
                if t >= 1:
                    hT_copy(t - 1)
            ple_gate(0)
            hT_copy(NT - 1)
            ac.wait_ge(S["pe_rt"], 1)
            a.activation(rtT, bank[B_ROUTER][0:NE, :], ACT.Sigmoid).then_inc(S["sig_rt"], 1)
            for k in range(1, 2 * NT):
                ple_gate(k)

            def hgT_copy(e, r):
                ac.wait_ge(S["pe_hgT"], e + 1)
                for u in range(2):
                    a.activation(hgT[:, r, 4 * u:4 * u + 4, :], bank[B_TOK[u]][:].rearrange("p (k s) -> p k s", k=4),
                                 ACT.Copy).then_inc(S["hgT_evac"], 1)

            def expert(e, r, last=False):
                ac.wait_ge(S["pe_gu"], e + 1)
                a.activation(act_e[:, r, 0, :], bank[B_GU[r]][:, 0:DE], ACT.Silu).then_inc(S["silu_done"], 1)
                if not last:
                    hgT_copy(e + 1, 1 - r)
                ac.wait_ge(S["pe_aT"], e + 1)
                a.activation(act_e[:, r, 2, :], bank[B_ACT[r]][:, 0:DE], ACT.Copy).then_inc(S["aT_evac"], 1)

            ac.wait_ge(S["pe_pg"], 2 * NT)
            hgT_copy(0, 0)
            with ac.Fori(0, NE // 2 - 1) as blk:
                for r in range(2):
                    expert(2 * blk + r, r)
            expert(NE - 2, 0)
            expert(NE - 1, 1, last=True)
            n_over = ac.value_load(over_i[0:1, 0:1], min_val=0, max_val=OVER)
            with ac.If(n_over > 0):
                with ac.Fori(0, OVER) as o:
                    with ac.If(o < n_over):
                        ac.wait_ge(S["o_t"], o + 1)
                        for u in range(2):
                            a.activation(hgT[:, 0, 4 * u:4 * u + 4, :], bank[B_TOK[u]][:].rearrange("p (k s) -> p k s", k=4),
                                         ACT.Copy).then_inc(S["o_te"], 1)
                        ac.wait_ge(S["o_gu"], o + 1)
                        a.activation(act_e[:, 0, 0, :], bank[B_GU[0]][:, 0:DE], ACT.Silu).then_inc(S["o_si"], 1)
                        ac.wait_ge(S["o_at"], o + 1)
                        a.activation(act_e[:, 0, 2, :], bank[B_ACT[0]][:, 0:DE], ACT.Copy).then_inc(S["o_ae"], 1)
            def deviation(t):
                ac.wait_ge(S["z2_ready"], t + 1)
                a.activation(RA[:, (8 + t) * D:(9 + t) * D], xh[:, t, :], ACT.Square, bias=ln_mv[:, t, 0:1],
                             accum_out=ln_mv[:, t, 1:2]).then_inc(S["var2_done"], 1)
                ac.wait_ge(S["var2_done"], t + 1)
                a.activation(ln_rs[:, t, 0:1], ln_mv[:, t, 1:2], ACT.Sqrt, bias=eps_t[:], scale=1.0 / D).then_inc(S["ln2_sqrt"], 1)

            def x_hat(t):
                ac.wait_ge(S["rs2_ready"], t + 1)
                a.activation(xh[:, t, :], xh[:, t, :], ACT.Identity, bias=ln_mv[:, t, 0:1], scale=ln_rs[:, t, 1:2]).then_inc(S["xhat_done"], 1)

            deviation(0)
            for t in range(1, NT):
                deviation(t)
                x_hat(t - 1)
            x_hat(NT - 1)

        @block.tensor
        def _(pe):
            mm = nc.tensor.matmul

            def project(bank_i, w, m, signal):
                for k in range(KD):
                    last = mm(bank[bank_i][:], w[:, k, m * P:(m + 1) * P], xT[:, k, :], start=(k == 0), stop=(k == KD - 1))
                last.then_inc(S[signal], 1)

            for k in range(KD):
                if k in FIRST_K:
                    pe.wait_ge(S[f"x_in{FIRST_K.index(k)}"], 32)
                for m in range(3):
                    last = mm(bank[m][:], w_ssm[:, k, m * P:(m + 1) * P], xT[:, k, :], start=(k == 0), stop=(k == KD - 1))
                    if k == KD - 1:
                        last.then_inc(S["pe_u"], 1)
            pe.wait_ge(S["wqk_in"], 32)
            for m in range(6):
                if m == 5:
                    pe.wait_ge(S["uT_done"], 1)
                project((3 + m) % 8, w_q if m % 2 == 0 else w_k, m // 2, "pe_qk")
            def v_tile(t, bank_i):
                for k in range(KD):
                    last = mm(bank[bank_i][:, 0:ATT_W], xT[:, k, t * P:(t + 1) * P], w_v[:, k, :], start=(k == 0), stop=(k == KD - 1))
                last.then_inc(S["pe_v"], 1)

            def bx_turn(n, bank_i):
                for i in range(4):
                    r, q = n // 3, 4 * (n % 3) + i
                    last = nc.tensor.transpose(bank[bank_i][:, i * P:(i + 1) * P], bx[:, r, q].rearrange("p j h -> p (j h)"), ident[:])
                last.then_inc(S["pe_bxT"], 1)

            pe.wait_ge(S["const_set"], 1)
            pe.wait_ge(S["bx_ready"], 2)
            for n, (signal, count) in enumerate([("uT_done", 2), ("uT_done", 3), ("qk_done", 1), ("qk_done", 2), ("qk_done", 3), ("qk_done", 4)]):
                pe.wait_ge(S[signal], count)
                bx_turn(n, 1 + n)

            pe.wait_ge(S["cp_ready"], 1)
            for n, (signal, count) in enumerate([("qk_done", 5), ("qk_done", 6), ("bxT_done", 1), ("bxT_done", 2), ("bxT_done", 3), ("bxT_done", 4)]):
                pe.wait_ge(S[signal], count)
                for i in range(4):
                    g = 4 * n + i
                    last = mm(bank[(7 + n) % 8][0:GD, i * P:(i + 1) * P], b_st[:, g, :],
                              cp[:, g, 0:CH, :].rearrange("p l h -> p (l h)"), start=True, stop=True)
                last.then_inc(S["pe_kern"], 1)

            pe.wait_ge(S["bxT_done"], 6)
            pe.wait_ge(S["kern_done"], 2)
            pe.wait_ge(S["u_back"], 16 * CH)
            for r in range(2):
                for q in range(Q):
                    for h in range(2):
                        b = (5 + 2 * r + q // 6) % 8
                        last = mm(bank[b][64 * h:64 * h + 64, (q % 6) * NC:(q % 6 + 1) * NC], bxT[:, r, q, 64 * h:64 * h + 64],
                                  uch[:, 2 * q + h, :], start=True, stop=True)
            last.then_inc(S["pe_x"], 1)

            def scores(h):
                if h == 0:
                    pe.wait_ge(S["xrot_done"], 1)
                else:
                    pe.wait_ge(S["s_read"], h)
                rows = slice(64 * (h % 2), 64 * (h % 2) + 64)
                for i in (0, 2, 3, 1):
                    b, c, _ = SCORE_AT[i]
                    w = (i + 1) * P
                    last = mm(bank[b][:, c:c + w], qT[rows, h // 2, i * P:(i + 1) * P], kT[rows, h // 2, 0:w], start=True, stop=True)
                last.then_inc(S["pe_s"], 1)

            def turn_probs(h):
                pe.wait_ge(S["p_norm"], h + 1)
                for u, (tiles, _, _) in enumerate(PT_UNITS):
                    k = 3 * h + u
                    if k >= 2:
                        pe.wait_ge(S["pt_evac"], k - 1)
                    elif k == 0:
                        pe.wait_ge(S["v_done"], 4)
                    c = 0
                    for j in tiles:
                        for i in range(j, NT):
                            o = SCORE_AT[i][2] + j * P
                            last = nc.tensor.transpose(bank[3 + k % 2][:, c:c + P], prob[:, h % 3, o:o + P], ident[:])
                            c += P
                    last.then_inc(S["pe_pt"], 1)

            def weigh_values(h):
                pair = h // 2
                pe.wait_ge(S["pt_evac"], 3 * h + 3)
                if h == 4:
                    pe.wait_ge(S["pv_evac"], 1)
                if h == 0:
                    pe.wait_ge(S["y_evac"], 3)
                rows = slice(64 * (h % 2), 64 * (h % 2) + 64)
                for j in range(NT):
                    o = PT_AT[j]
                    last = mm(bank[5 + pair % 2][rows, j * P:T], vN[:, j, h * HD:(h + 1) * HD],
                              probT[:, h % 2, o:o + T - j * P], start=(j == 0), stop=(j == NT - 1))
                last.then_inc(S["pe_pv"], 1)

            pe.wait_ge(S["wup_in"], 16)
            for m in range(2):
                pe.wait_ge(S["kern_done"], m + 5)
                project(3 + m, w_up, m, "pe_pool")
            scores(0)
            pe.wait_ge(S["wv_in"], 16)
            v_tile(0, 5)
            v_tile(1, 6)
            scores(1)
            v_tile(2, 7)
            pe.wait_ge(S["pool_in_done"], 1)
            v_tile(3, 3)
            scores(2)
            pe.wait_ge(S["pool_ready"], 1)
            pe.wait_ge(S["wpl_in"], 64)
            for m, (signal, count) in enumerate([("pool_in_done", 2), ("v_done", 1)]):
                pe.wait_ge(S[signal], count)
                mm(bank[4 + m][:], w_pl[:, m, :], pl_s[:, 0, m, :], start=True, stop=True).then_inc(S["pe_pm"], 1)
            pe.wait_ge(S["s_moved"], 64)
            pe.wait_ge(S["m0_in"], 16 * CH)
            for m, (signal, count) in enumerate([("v_done", 2), ("v_done", 3), ("pool_mixed", 2)]):
                pe.wait_ge(S[signal], count)
                for i in range(8):
                    g = 8 * m + i
                    dst = bank[(6, 7, 5)[m]][:, i * NC:(i + 1) * NC]
                    mm(dst, m0[:, g].rearrange("p l h -> p (l h)"), uch[:, g, :], start=True, stop=False)
                    last = mm(dst, cp[:, g, 1:CH + 1, :].rearrange("p l h -> p (l h)"), s_in[:, g, :], start=False, stop=True)
                last.then_inc(S["pe_y"], 1)

            def glu(m, bank_i):
                for k in range(3):
                    last = mm(bank[bank_i][:], w_glu[:, k, m * P:(m + 1) * P], hdT[:, 5 + k, :], start=(k == 0), stop=(k == 2))
                last.then_inc(S["pe_glu"], 1)

            def mix_part(t, half, group):
                for i, k in enumerate(MIX_AT[group]):
                    last = mm(bank[WO_AT[half][group]][:], hdT[:, k, t * P:(t + 1) * P], w_o[:, k, half * 512:half * 512 + 512],
                              start=(i == 0), stop=(i == len(MIX_AT[group]) - 1))
                return last

            for h in range(4):
                turn_probs(h)
                if h + 3 < HEADS:
                    scores(h + 3)
                if h == 3:
                    pe.wait_ge(S["gelu_done"], 3)
                    pe.wait_ge(S["wglu_in"], 16)
                    glu(0, 7)
                weigh_values(h)
            turn_probs(4)
            pe.wait_ge(S["s_read"], HEADS)
            glu(1, 0)
            glu(2, 1)
            weigh_values(4)
            turn_probs(5)
            pe.wait_ge(S["wo_scaled"], KD)
            mix_part(0, 0, 0)
            pe.wait_ge(S["glu_sig"], 1)
            mix_part(0, 1, 0)
            weigh_values(5)
            pe.wait_ge(S["ssm_done"], 3)
            pe.wait_ge(S["pv_evac"], 2)
            mix_part(0, 0, 1)
            pe.wait_ge(S["glu_sig"], 3)
            mix_part(0, 1, 1)
            pe.wait_ge(S["pv_evac"], 3)
            mix_part(0, 0, 2).then_inc(S["pe_wo"], 1)
            pe.wait_ge(S["pt_evac"], 3 * HEADS)
            pe.wait_ge(S["sq_added"], 5)
            for g in range(3):
                for t in range(NT):
                    last = mm(bank[4][:, g * NT + t:g * NT + t + 1], ssum[:, g, t * P:(t + 1) * P], ones[:, 0:1], start=True, stop=True)
            last.then_inc(S["pe_sq"], 1)
            mix_part(0, 1, 2).then_inc(S["pe_wo"], 1)

            def out_proj(t):
                for half in range(2):
                    pe.wait_ge(S["wo_read"], 2 * t + half - 1)
                    for group in range(3):
                        last = mix_part(t, half, group)
                    last.then_inc(S["pe_wo"], 1)

            def turn_h(t):
                pe.wait_ge(S["h_ready"], t + 1)
                for u in range(2):
                    if t:
                        pe.wait_ge(S["hT_evac"], 2 * t - 1 + u)
                    elif u == 0:
                        pe.wait_ge(S["rms_sqrt"], 3)
                    for i in range(4):
                        last = nc.tensor.transpose(bank[4 + u][:, i * P:(i + 1) * P], xh[:, t, 4 * u + i:D:KD], ident[:])
                    last.then_inc(S["pe_hT"], 1)

            def ple(k):
                t, half = k // 2, k % 2
                if k >= 2:
                    pe.wait_ge(S["ple_done"], k - 1)
                else:
                    pe.wait_ge(S["wo_read"], 2 * NT - 1 + k)
                cols = slice(half * 512, half * 512 + 512)
                for c in range(KD):
                    last = mm(bank[PG_AT[k % 2]][:], hT[:, c, t * P:(t + 1) * P], w_pg[:, c, cols], start=(c == 0), stop=(c == KD - 1))
                last.then_inc(S["pe_pg"], 1)
                for c in range(2):
                    last = mm(bank[PP_AT[k % 2]][:], pT[:, c, t * P:(t + 1) * P], w_pp[:, c, cols], start=(c == 0), stop=(c == 1))
                last.then_inc(S["pe_pp"], 1)

            for t in range(1, NT):
                out_proj(t)
                turn_h(t - 1)
            pe.wait_ge(S["wpg_in"], 16)
            pe.wait_ge(S["wpp_in"], 16)
            pe.wait_ge(S["pT_in"], 16)
            pe.wait_ge(S["hT_evac"], 2)
            ple(0)
            turn_h(NT - 1)
            pe.wait_ge(S["hT_evac"], 2 * NT)
            pe.wait_ge(S["wrt_in"], 16)
            for k in range(KD):
                last = mm(bank[B_ROUTER][0:NE, :], w_rt[:, k, :], hT[:, k, :], start=(k == 0), stop=(k == KD - 1))
            last.then_inc(S["pe_rt"], 1)
            ple(1)
            pe.wait_ge(S["sig_rt"], 1)
            for t in range(NT):
                last = nc.tensor.transpose(bank[B_COUNT][:, t * NE:(t + 1) * NE], rtT[:, t * P:(t + 1) * P], ident[0:NE, 0:NE])
            last.then_inc(S["rt_by_token"], 1)
            ple(2)
            ple(3)
            pe.wait_ge(S["sel_ready"], 1)
            for t in range(NT):
                for s in range(t + 1):
                    mm(bank[B_COUNT][:, t * NE:(t + 1) * NE], (tri if s == t else ones)[:], r_sel[:, s, :], start=(s == 0), stop=(s == t))
            for s in range(NT):
                last = mm(bank[B_COUNT][:, NT * NE:(NT + 1) * NE], ones[:], r_sel[:, s, :], start=(s == 0), stop=(s == NT - 1))
            last.then_inc(S["pe_cnt"], 1)
            for k in range(4, 2 * NT):
                ple(k)

            def turn_tokens(r):
                for k in range(KD):
                    last = nc.tensor.transpose(bank[B_TOK[k // 4]][:, (k % 4) * P:(k % 4 + 1) * P], hg[:, r, k:D:KD], ident[:])
                return last

            def gate_up(b, r):
                w = ebuf[b][:, 0:4096].rearrange("p (u k n) -> p k u n", u=2, k=KD)
                for k in range(KD):
                    last = mm(bank[B_GU[r]][:].rearrange("p (u n) -> p u n", u=2), hgT[:, r, k, :], w[:, k], start=(k == 0), stop=(k == KD - 1))
                return last

            def turn_act(r):
                for k in range(2):
                    last = nc.tensor.transpose(bank[B_ACT[r]][:, k * P:(k + 1) * P], act_e[:, r, 1, k:DE:2], ident[:])
                return last

            def down(b, r):
                w = ebuf[b][:, 4096:6144].rearrange("p (k n) -> p k n", k=2)
                for half in range(2):
                    for k in range(2):
                        last = mm(bank[B_DN[half]][:], act_e[:, r, 2, k * P:(k + 1) * P], w[:, k, half * 512:half * 512 + 512],
                                  start=(k == 0), stop=(k == 1))
                return last

            def tokens_of(r, uses):
                pe.wait_ge(S[f"hg_in{r}"], 16 * uses)
                turn_tokens(r).then_inc(S["pe_hgT"], 1)

            def expert(e, b, loads, first=False, last=False):
                r = b % 2
                pe.wait_ge(S[f"e_in{b}"], 48 * loads)
                pe.wait_ge(S["hgT_evac"], 2 * e + 2)
                if not first:
                    pe.wait_ge(S["a_ready"], e)
                gate_up(b, r).then_inc(S["pe_gu"], 1)
                if not last:
                    tokens_of((b + 1) % 4, loads if b < 3 else loads + 1)
                if not first:
                    pe.wait_ge(S["aT_evac"], e)
                    if isinstance(e, int) and e == 1:
                        pe.wait_ge(S["ple_done"], 2 * NT)
                    else:
                        pe.wait_ge(S["ye_evac"], e - 1)
                    down((b + 3) % 4, 1 - r).then_inc(S["pe_dn"], 1)
                pe.wait_ge(S["a_ready"], e + 1)
                turn_act(r).then_inc(S["pe_aT"], 1)

            pe.wait_ge(S["pe_pg"], 2 * NT)
            tokens_of(0, 1)
            pe.wait_ge(S["ple_done"], 2 * NT)
            for e in range(4):
                expert(e, e, 1, first=(e == 0))
            with pe.Fori(1, NE // 4 - 1) as blk:
                for b in range(4):
                    expert(4 * blk + b, b, blk + 1)
            for e in range(NE - 4, NE):
                expert(e, e % 4, NE // 4, last=(e == NE - 1))
            pe.wait_ge(S["aT_evac"], NE)
            pe.wait_ge(S["ye_evac"], NE - 1)
            down(3, 1).then_inc(S["pe_dn"], 1)
            n_over = pe.value_load(over_i[0:1, 0:1], min_val=0, max_val=OVER)
            pe.wait_ge(S["ye_evac"], NE)
            with pe.If(n_over > 0):
                with pe.Fori(0, OVER) as o:
                    with pe.If(o < n_over):
                        pe.wait_ge(S["o_hg"], 16 * (o + 1))
                        turn_tokens(0).then_inc(S["o_t"], 1)
                        pe.wait_ge(S["o_te"], 2 * (o + 1))
                        pe.wait_ge(S["o_in"], 48 * (o + 1))
                        gate_up(0, 0).then_inc(S["o_gu"], 1)
                        pe.wait_ge(S["o_a"], o + 1)
                        turn_act(0).then_inc(S["o_at"], 1)
                        pe.wait_ge(S["o_ae"], o + 1)
                        down(0, 0).then_inc(S["o_dn"], 1)

        @block.vector
        def _(dv):
            v = nc.vector
            tt, ts, stt = v.tensor_tensor, v.tensor_scalar, v.scalar_tensor_tensor
            n = [0]

            def link(ins):
                n[0] += 1
                ins.then_inc(S["dve_step"], 1)
                dv.wait_ge(S["dve_step"], n[0])

            def cmul(o_r, o_i, a_r, a_i, b_r, b_i, t):
                link(tt(t, a_i, b_i, ALU.mult))
                link(tt(o_r, a_r, b_r, ALU.mult))
                link(tt(o_r, o_r, t, ALU.subtract))
                link(tt(t, a_r, b_i, ALU.mult))
                link(tt(o_i, a_i, b_r, ALU.mult))
                link(tt(o_i, o_i, t, ALU.add))

            link(v.memset(eps_t[:], EPS))
            dv.wait_ge(S["par_in"], 16)
            dv.wait_ge(S["act_step"], 3)
            are, aim = par[:, C_ARE:C_ARE + NG], par[:, C_AIM:C_AIM + NG]
            link(tt(expo[:, 0:NG], are, dt_[:], ALU.mult))
            link(tt(ang[:, 0:NG], aim, dt_[:], ALU.mult))
            link(ts(expo[:, NG:NG + Q], expo[:, 0:Q], float(CH), None, ALU.mult))
            link(ts(ang[:, NG:NG + Q], ang[:, 0:Q], float(CH), None, ALU.mult))
            link(ts(turns[:], ang[:], 1.0 / (2 * np.pi), ROUND, ALU.mult, ALU.add))
            link(ts(turns[:], turns[:], -ROUND, None, ALU.add))
            for part in (PI2_A, PI2_B, PI2_C):
                link(stt(ang[:], turns[:], -part, ang[:], ALU.mult, ALU.add))
            ts(angr[:], ang[:], PI_SAFE, -PI_SAFE, ALU.min, ALU.max).then_inc(S["ang"], 1)
            dv.wait_ge(S["trig"], 1)
            link(tt(sinh[:], sinh[:], sinh[:], ALU.mult))
            link(ts(sinh[:], sinh[:], -2.0, 1.0, ALU.mult, ALU.add))
            link(v.tensor_copy(u8[:, 0, :], sinh[:, NG:NG + Q]))
            link(v.tensor_copy(u8[:, 1, :], sinf[:, NG:NG + Q]))
            v.tensor_copy(mag8[:], expo[:, NG:NG + Q]).then_inc(S["bx_ready"], 1)
            dv.wait_ge(S["bx_ready"], 1)
            pr, pi = pw[:, 0], pw[:, 1]
            link(v.memset(pr[:, :, 0:1], 1.0))
            link(v.memset(pi[:, :, 0:1], 0.0))
            link(tt(pr[:, :, 1], expo[:, 0:NG], sinh[:, 0:NG], ALU.mult))
            link(tt(pi[:, :, 1], expo[:, 0:NG], sinf[:, 0:NG], ALU.mult))
            nr, c1, c2, c3 = (sm[:, k * NG:(k + 1) * NG] for k in range(10, 14))
            link(ts(nr, pr[:, :, 1], -1.0, None, ALU.add))
            link(tt(c1, are, are, ALU.mult))
            link(tt(c2, aim, aim, ALU.mult))
            link(tt(c1, c1, c2, ALU.add))
            link(v.reciprocal(c1, c1))
            link(tt(c2, nr, are, ALU.mult))
            link(tt(c3, pi[:, :, 1], aim, ALU.mult))
            link(tt(c2, c2, c3, ALU.add))
            link(tt(c2, c2, c1, ALU.mult))
            link(tt(c3, pi[:, :, 1], are, ALU.mult))
            link(tt(nr, nr, aim, ALU.mult))
            link(tt(c3, c3, nr, ALU.subtract))
            link(tt(c3, c3, c1, ALU.mult))
            wide = [P, NG, GD]
            b_re = par[:, C_BRE:C_BIM].rearrange("p (g h) -> p g h", g=NG)
            b_im = par[:, C_BIM:C_CA].rearrange("p (g h) -> p g h", g=NG)
            t3 = tmp[:, 0:NG * GD].rearrange("p (g h) -> p g h", g=NG)
            cmul(bb[:, 0], bb[:, 1], b_re, b_im, c2.unsqueeze(2).broadcast_to(wide), c3.unsqueeze(2).broadcast_to(wide), t3)
            link(v.tensor_copy(b_st[0:64], bb[0:64, 0, Q:NG, :]))
            link(v.tensor_copy(b_st[64:P], bb[64:P, 1, Q:NG, :]))
            for lo, hi, by in ((2, 3, 1), (3, 5, 2), (5, 9, 4)):
                w = hi - lo
                t2 = tmp[:, 0:NG * w].rearrange("p (g l) -> p g l", g=NG)
                a_r, a_i = pr[:, :, lo - by:hi - by], pi[:, :, lo - by:hi - by]
                s_ = [P, NG, w]
                cmul(pr[:, :, lo:hi], pi[:, :, lo:hi], a_r, a_i,
                     pr[:, :, by:by + 1].broadcast_to(s_), pi[:, :, by:by + 1].broadcast_to(s_), t2)
            t4 = tmp[:, 0:Q * GD].rearrange("p (q h) -> p q h", q=Q)
            for j in range(CH):
                s_ = [P, Q, GD]
                l = CH - 1 - j
                cmul(bx[:, 0, :, j, :], bx[:, 1, :, j, :], bb[:, 0, 0:Q, :], bb[:, 1, 0:Q, :],
                     pr[:, 0:Q, l:l + 1].broadcast_to(s_), pi[:, 0:Q, l:l + 1].broadcast_to(s_), t4)
            v.engine_nop().then_inc(S["bx_ready"], 1)
            t5 = tmp[:, 0:3456].rearrange("p (g l h) -> p g l h", g=G, l=CH + 1)
            s_ = [P, G, CH + 1, GD]
            d1 = par[:, C_CA:C_CB].rearrange("p (g h) -> p g h", g=G).unsqueeze(2).broadcast_to(s_)
            d2 = par[:, C_CB:SSM_COLS].rearrange("p (g h) -> p g h", g=G).unsqueeze(2).broadcast_to(s_)
            link(tt(cp, d1, pr[:, Q:NG, :].unsqueeze(3).broadcast_to(s_), ALU.mult))
            link(tt(t5, d2, pi[:, Q:NG, :].unsqueeze(3).broadcast_to(s_), ALU.mult))
            tt(cp, cp, t5, ALU.add).then_inc(S["cp_ready"], 1)
            for k in range(6):
                dv.wait_ge(S["pe_bxT"], k + 1)
                r, q = k // 3, 4 * (k % 3)
                v.tensor_copy(bxT[:, r, q:q + 4, :], bank[1 + k][:].rearrange("p (q s) -> p q s", q=4)).then_inc(S["bxT_done"], 1)

            dv.wait_ge(S["pe_x"], 1)
            dv.wait_ge(S["rot_ready"], 1)
            half = Q // 2 * NC
            cosv, sinv = rot[:, 0, :, 0:NC], rot[:, 1, :, 0:NC]

            def qc(ap):
                return ap.rearrange("p (q c) -> p q c", c=NC)
            for u in range(2):
                xr, xi = qc(bank[5 + u][:, 0:half]), qc(bank[(7 + u) % 8][:, 0:half])
                cs, sn = cosv[:, 6 * u:6 * u + 6], sinv[:, 6 * u:6 * u + 6]
                cols = slice(u * half, (u + 1) * half)
                o_r, o_i = qc(x_rot[:, 0, cols]), qc(x_rot[:, 1, cols])
                t_r, t_i = qc(x_tmp[:, 0, cols]), qc(x_tmp[:, 1, cols])
                link(tt(o_r, xr, cs, ALU.mult))
                link(tt(t_r, xi, sn, ALU.mult))
                link(tt(o_i, xi, cs, ALU.mult))
                last = tt(t_i, xr, sn, ALU.mult)
                if u == 0:
                    link(last)
            last.then_inc(S["xrot_done"], 1)
            dv.wait_ge(S["xrot_done"], 1)
            link(tt(x_rot[:, 0, :], x_rot[:, 0, :], x_tmp[:, 0, :], ALU.add))
            link(tt(x_rot[:, 1, :], x_rot[:, 1, :], x_tmp[:, 1, :], ALU.subtract))
            for r in range(2):
                link(v.tensor_tensor_scan(x_rot[:, r, :], decay, x_rot[:, r, :], 0.0, ALU.mult, ALU.add))
            c0, c1_ = slice(0, NC - 1), slice(1, NC)
            s_r, s_i = qc(x_tmp[:, 0, :]), qc(x_tmp[:, 1, :])
            r_r, r_i = qc(x_rot[:, 0, :]), qc(x_rot[:, 1, :])
            tq = s_in.rearrange("p g c -> p (g c)")[:, 0:Q * NC].rearrange("p (q c) -> p q c", c=NC)
            link(v.memset(s_r[:, :, 0:1], 0.0))
            link(v.memset(s_i[:, :, 0:1], 0.0))
            link(tt(s_r[:, :, c1_], r_r[:, :, c0], cosv[:, :, c0], ALU.mult))
            link(tt(tq[:, :, c1_], r_i[:, :, c0], sinv[:, :, c0], ALU.mult))
            link(tt(s_r[:, :, c1_], s_r[:, :, c1_], tq[:, :, c1_], ALU.subtract))
            link(tt(s_i[:, :, c1_], r_i[:, :, c0], cosv[:, :, c0], ALU.mult))
            link(tt(tq[:, :, c1_], r_r[:, :, c0], sinv[:, :, c0], ALU.mult))
            tt(s_i[:, :, c1_], s_i[:, :, c1_], tq[:, :, c1_], ALU.add).then_inc(S["s_ready"], 1)

            def bias_max(h):
                dv.wait_ge(S["pe_s"], h + 1)
                if h == 0:
                    dv.wait_ge(S["rb_in"], 16)
                    dv.wait_ge(S["rot_ready"], 1)
                    dv.wait_ge(S["small_in"], 16)
                    dv.wait_ge(S["s_ready"], 1)
                if h >= 3:
                    dv.wait_ge(S["pe_pt"], 3 * h - 6)
                r = h % 3
                for i in range(NT):
                    b, c, o = SCORE_AT[i]
                    old = max(i - 1, 0) * P
                    near = (i + 1) * P - old
                    if old:
                        link(ts(prob[:, r, o:o + old], bank[b][:, c:c + old], HD ** -0.5,
                                vec[:, V_RC + h:V_RC + h + 1], ALU.mult, ALU.add))
                    last = stt(prob[:, r, o + old:o + old + near], bank[b][:, c + old:c + old + near], HD ** -0.5,
                               rbias[:, h, 256 - near:256], ALU.mult, ALU.add)
                    if i < NT - 1:
                        link(last)
                last.then_inc(S["s_read"], 1)
                dv.wait_ge(S["s_read"], h + 1)
                for i in range(NT):
                    o, w = SCORE_AT[i][2], (i + 1) * P
                    last = v.tensor_reduce(att_mx[:, r, i:i + 1], prob[:, r, o:o + w], AX.X, ALU.max, negate=True)
                    if i < NT - 1:
                        link(last)
                last.then_inc(S["s_max"], 1)

            def normalise(h):
                dv.wait_ge(S["p_exp"], h + 1)
                r = h % 3
                link(v.reciprocal(att_sm[:, r, :], att_sm[:, r, :]))
                for i in range(NT):
                    o, w = SCORE_AT[i][2], (i + 1) * P
                    last = ts(prob[:, r, o:o + w], prob[:, r, o:o + w], att_sm[:, r, i:i + 1], None, ALU.mult)
                    if i < NT - 1:
                        link(last)
                last.then_inc(S["p_norm"], 1)

            bias_max(0)
            for h in range(HEADS):
                if h + 1 < HEADS:
                    bias_max(h + 1)
                normalise(h)
                if h == 3:
                    dv.wait_ge(S["y_back"], 16)
                    for m in range(3):
                        stt(yT[:, m, :], uT[:, m, :], vec[:, V_D + m:V_D + m + 1], yT[:, m, :], ALU.mult, ALU.add).then_inc(S["yin_ready"], 1)
            for m in range(3):
                dv.wait_ge(S["glu_sig"], m + 1)
                dv.wait_ge(S["pe_glu"], 3)
                tt(hdT[:, 5 + m, :], hdT[:, 5 + m, :], sgl[:, m, :], ALU.mult).then_inc(S["ssm_done"], 1)
            dv.wait_ge(S["rms_sqrt"], 3)
            link(v.reciprocal(rms_r[:], rms_r[:]))
            dv.wait_ge(S["ln_in"], 32)

            def normalise_rows(t, signal, sqrt_signal, count):
                link(v.reciprocal(ln_rs[:, t, 1:2], ln_rs[:, t, 0:1]))
                link(ts(xh[:, t, :], xh[:, t, :], ln_mv[:, t, 0:1], ln_rs[:, t, 1:2], ALU.subtract, ALU.mult))
                link(tt(xh[:, t, :], xh[:, t, :], lng, ALU.mult))
                tt(xh[:, t, :], xh[:, t, :], lnb, ALU.add).then_inc(S[signal], 1)

            for t in range(NT):
                dv.wait_ge(S["x_scaled"], t + 1)
                for half_ in range(2):
                    dv.wait_ge(S["pe_wo"], 2 * t + half_ + 1)
                    cols = slice(half_ * 512, half_ * 512 + 512)
                    for group in range(3):
                        last = stt(xh[:, t, cols], bank[WO_AT[half_][group]][:], rms_r[:, group, t:t + 1], xh[:, t, cols], ALU.mult, ALU.add)
                        if group < 2:
                            link(last)
                    last.then_inc(S["wo_read"], 1)
                    dv.wait_ge(S["wo_read"], 2 * t + half_ + 1)
                    link(v.bn_stats(ln_st[:, t, 6 * half_:6 * half_ + 6], xh[:, t, cols]))
                v.bn_aggr(ln_mv[:, t, :], ln_st[:, t, :]).then_inc(S["z_ready"], 1)
                dv.wait_ge(S["ln_sqrt"], t + 1)
                normalise_rows(t, "h_ready", "ln_sqrt", t + 1)

            def ple_sum(k):
                t, half_ = k // 2, k % 2
                dv.wait_ge(S["ple_sig"], k + 1)
                dv.wait_ge(S["pe_pp"], k + 1)
                if half_ == 0:
                    dv.wait_ge(S["pe_hT"], 2 * t + 2)
                    dv.wait_ge(S[f"h_out{t}"], 16)
                cols = slice(half_ * 512, half_ * 512 + 512)
                link(tt(ple_t[:, cols], ple_t[:, cols], bank[PP_AT[k % 2]][:], ALU.mult))
                stt(xh[:, t, cols], xh[:, t, cols], ALPHA, ple_t[:, cols], ALU.mult, ALU.add).then_inc(S["ple_done"], 1)
            ple_sum(0)
            ple_sum(1)

            W3 = [P, NT, NE]

            def view(k, n_=NT * NE):
                return rt[:, 64 * k:64 * k + n_]
            b_s = view(1).rearrange("p (t e) -> p t e", t=NT)
            pairs = rt[:, 128:128 + NT * EG * 6].rearrange("p (t g c) -> p t g c", t=NT, g=EG)
            gs = rt[:, 224:240].rearrange("p (t g) -> p t g", t=NT)
            key = rt[:, 240:256].rearrange("p (t g) -> p t g", t=NT)
            ingr = rt[:, 256:272].rearrange("p (t g) -> p t g", t=NT)
            m4 = rt[:, 272:276]
            m4b = rt[:, 276:280]
            wsum = rt[:, 280:284]
            msk = view(5).rearrange("p (t e) -> p t e", t=NT)
            tie = view(6).rearrange("p (t e) -> p t e", t=NT)
            sel = [view(7).rearrange("p (t e) -> p t e", t=NT), view(8).rearrange("p (t e) -> p t e", t=NT)]
            slot = view(9).rearrange("p (t e) -> p t e", t=NT)
            low = view(10).rearrange("p (t e) -> p t e", t=NT)
            tc = view(11).rearrange("p (t e) -> p t e", t=NT)
            dv.wait_ge(S["rt_by_token"], 1)
            link(v.tensor_copy(r_s, bank[B_COUNT][:, 0:NT * NE]))
            s_v = r_s.rearrange("p (t e) -> p t e", t=NT)
            link(tt(b_s, s_v, vec[:, V_RB:V_RB + NE].unsqueeze(1).broadcast_to(W3), ALU.add))
            bg = view(1).rearrange("p (t g c) -> p t g c", t=NT, g=EG)
            link(tt(pairs[:, :, :, 0:3], bg[:, :, :, 0:3], bg[:, :, :, 1:4], ALU.add))
            link(tt(pairs[:, :, :, 3:5], bg[:, :, :, 0:2], bg[:, :, :, 2:4], ALU.add))
            link(tt(pairs[:, :, :, 5:6], bg[:, :, :, 0:1], bg[:, :, :, 3:4], ALU.add))
            link(v.tensor_reduce(gs, pairs, AX.X, ALU.max))

            def first_max(out_, in_, mx, keyb, order, width):
                s__ = [P, NT, width]
                link(v.tensor_reduce(mx, in_, AX.X, ALU.max))
                link(tt(keyb, in_, mx.unsqueeze(2).broadcast_to(s__), ALU.is_equal))
                link(tt(keyb, keyb, order, ALU.mult))
                link(v.tensor_reduce(mx, keyb, AX.X, ALU.max))
                link(tt(out_, keyb, mx.unsqueeze(2).broadcast_to(s__), ALU.is_equal))

            link(ts(tc[:, 0, :], e_off[:], -1.0, float(NE * CAP), ALU.mult, ALU.add))
            link(v.tensor_copy(low, tc[:, 0:1, :].broadcast_to(W3)))
            first_max(ingr, gs, m4, key, low[:, :, 0:EG], EG)
            ig4 = ingr.unsqueeze(3).broadcast_to([P, NT, EG, EPG])
            mk4 = view(5).rearrange("p (t g c) -> p t g c", t=NT, g=EG)
            link(tt(mk4, bg, ig4, ALU.mult))
            link(ts(ingr, ingr, BIG, -BIG, ALU.mult, ALU.add))
            link(tt(mk4, mk4, ig4, ALU.add))
            for k in range(2):
                first_max(sel[k], msk, m4, tie, low, NE)
                link(tt(tie, s_v, sel[k], ALU.mult))
                link(v.tensor_reduce(wgt[:, k, :], tie, AX.X, ALU.add))
                if k == 0:
                    link(ts(tie, sel[0], -BIG, None, ALU.mult))
                    link(tt(msk, msk, tie, ALU.add))
            link(tt(wsum, wgt[:, 0, :], wgt[:, 1, :], ALU.add))
            link(v.reciprocal(wsum, wsum))
            for k in range(2):
                link(tt(wgt[:, k, :], wgt[:, k, :], wsum, ALU.mult))
            tt(r_sel, sel[0], sel[1], ALU.add).then_inc(S["sel_ready"], 1)
            ple_sum(2)
            dv.wait_ge(S["pe_cnt"], 1)
            cnt, more, cum, base = (rt[:, 768 + 16 * k:784 + 16 * k] for k in range(4))
            link(v.tensor_copy(cnt, bank[B_COUNT][:, NT * NE:(NT + 1) * NE]))
            link(ts(more, cnt, float(CAP), None, ALU.is_gt))
            for k in (2, 3):
                link(stt(more, cnt, float(CAP * k), more, ALU.is_gt, ALU.add))
            link(v.tensor_tensor_scan(cum, ones[:, 0:NE], more, 0.0, ALU.mult, ALU.add))
            link(tt(base, cum, more, ALU.subtract))
            link(ts(base, base, float(CAP), float((NE - 1) * CAP), ALU.mult, ALU.add))
            link(v.tensor_copy(slot, bank[B_COUNT][:, 0:NT * NE].rearrange("p (t e) -> p t e", t=NT)))
            link(ts(low, slot, float(CAP), None, ALU.is_lt))
            link(tt(cnt, e_off[:], base, ALU.subtract))
            link(tt(low, low, cnt.unsqueeze(1).broadcast_to(W3), ALU.mult))
            link(tt(slot, slot, low, ALU.add))
            link(tt(slot, slot, base.unsqueeze(1).broadcast_to(W3), ALU.add))
            for k in range(2):
                link(tt(tie, slot, sel[k], ALU.mult))
                link(v.tensor_reduce(m4b, tie, AX.X, ALU.add))
                last = v.tensor_copy(slot_i[:].rearrange("p (t k) -> p t k", k=2)[:, :, k], m4b)
                if k == 0:
                    link(last)
            last.then_inc(S["slots_ready"], 1)
            dv.wait_ge(S["slots_ready"], 1)
            le = rt[:, 832:832 + OVER * NE].rearrange("p (o e) -> p o e", o=OVER)
            ov = rt[:, 960:968]
            link(tt(le, cum.unsqueeze(1).broadcast_to([P, OVER, NE]), io_o[:].unsqueeze(2).broadcast_to([P, OVER, NE]), ALU.is_le))
            link(v.tensor_reduce(ov[:, 1:8], le, AX.X, ALU.add))
            link(v.tensor_copy(ov[:, 0:1], cum[:, NE - 1:NE]))
            link(ts(ov[:, 1:8], ov[:, 1:8], float(NE - 1), None, ALU.min))
            link(v.tensor_copy(over_i[:], ov[0:1, :]))

            ple_sum(3)
            dv.wait_ge(S["inv_back"], 16)
            ts(tok_t[:], inv_t[:], 1, None, ALU.arith_shift_right).then_inc(S["tok_ready"], 1)
            for k in range(4, 2 * NT):
                ple_sum(k)

            def y_copy(e, b, uses):
                dv.wait_ge(S["pe_dn"], e + 1)
                if not isinstance(uses, int) or uses > 1:
                    dv.wait_ge(S[f"ye_out{b}"], 16 * (uses - 1))
                v.tensor_copy(y_e[b][:, 0:512], bank[B_DN[0]][:])
                v.tensor_copy(y_e[b][:, 512:1024], bank[B_DN[1]][:]).then_inc(S["ye_evac"], 1)

            def gate_times_up(e, r):
                dv.wait_ge(S["silu_done"], e + 1)
                if not isinstance(e, int) or e >= 2:
                    dv.wait_ge(S["pe_aT"], e - 1)
                tt(act_e[:, r, 1, :], act_e[:, r, 0, :], bank[B_GU[r]][:, DE:2 * DE], ALU.mult).then_inc(S["a_ready"], 1)

            gate_times_up(0, 0)
            for e in range(4):
                gate_times_up(e + 1, (e + 1) % 2)
                y_copy(e, e, 1)
            with dv.Fori(1, NE // 4 - 1) as blk:
                for b in range(4):
                    gate_times_up(4 * blk + (b + 1), (b + 1) % 2)
                    y_copy(4 * blk + b, b, blk + 1)
            for e in range(NE - 4, NE):
                if e + 1 < NE:
                    gate_times_up(e + 1, (e + 1) % 2)
                y_copy(e, e % 4, NE // 4)
            n_over = dv.value_load(over_i[0:1, 0:1], min_val=0, max_val=OVER)
            dv.wait_ge(S["ye_out0"], 16 * NE // 4)
            with dv.If(n_over > 0):
                with dv.Fori(0, OVER) as o:
                    with dv.If(o < n_over):
                        v.tensor_copy(cur_t[:, 0:1], tok_t[:, bass.ds(o + NE, 1)]).then_inc(S["o_c1"], 1)
                        v.tensor_copy(cur_t[:, 1:2], inv_t[:, bass.ds(o + NE, 1)]).then_inc(S["o_col"], 1)
                        dv.wait_ge(S["o_si"], o + 1)
                        tt(act_e[:, 0, 1, :], act_e[:, 0, 0, :], bank[B_GU[0]][:, DE:2 * DE], ALU.mult).then_inc(S["o_a"], 1)
                        dv.wait_ge(S["o_dn"], o + 1)
                        v.tensor_copy(y_e[0][:, 0:512], bank[B_DN[0]][:]).then_inc(S["o_ye"], 1)
                        v.tensor_copy(y_e[0][:, 512:1024], bank[B_DN[1]][:]).then_inc(S["o_ye"], 1)
                        dv.wait_ge(S["o_out"], 16 * (o + 1))
                        dv.sem_inc(S["o_round_dv"], 1)

            dv.wait_ge(S["ln2_in"], 32)

            def combine(t):
                for k in range(2):
                    dv.wait_ge(S[f"yk{k}_in{t}"], 16)
                    yk = RA[:, (2 * t + k) * D:(2 * t + k + 1) * D]
                    link(stt(xh[:, t, :], yk, wgt[:, k, t:t + 1], xh[:, t, :], ALU.mult, ALU.add,
                             accum_out=ln_st[:, t, 0:1] if k == 1 else None))
                ts(ln_mv[:, t, 0:1], ln_st[:, t, 0:1], -1.0 / D, None, ALU.mult).then_inc(S["z2_ready"], 1)

            def scale_rows(t):
                dv.wait_ge(S["ln2_sqrt"], t + 1)
                link(v.reciprocal(ln_rs[:, t, 1:2], ln_rs[:, t, 0:1]))
                tt(ln_mv[:, t, 0:1], ln_mv[:, t, 0:1], ln_rs[:, t, 1:2], ALU.mult).then_inc(S["rs2_ready"], 1)

            combine(0)
            for t in range(1, NT):
                combine(t)
                scale_rows(t - 1)
            scale_rows(NT - 1)
            for t in range(2, NT):
                dv.wait_ge(S["xhat_done"], t + 1)
                link(tt(xh[:, t, :], xh[:, t, :], lng, ALU.mult))
                tt(xh[:, t, :], xh[:, t, :], lnb, ALU.add).then_inc(S["o_dve"], 1)


def _lay_out(inputs):
    a = {k: np.asarray(v) for k, v in inputs.items()}

    def pair(v):
        w = v.reshape(Q, 2, NS, -1).transpose(1, 2, 0, 3)
        return w.reshape(P, Q, -1)

    def stacked(re, im):
        w = np.stack([re, im]).reshape(2, G, NS, -1).transpose(0, 2, 1, 3)
        return w.reshape(P, G, -1)

    def both(v):
        return np.concatenate([pair(v), stacked(v, v)], axis=1).reshape(P, -1)

    ldt = np.repeat(a["ssm_log_dt"][0][:, None], NS, axis=1)
    c_re, c_im = (a[k][0].transpose(0, 2, 1) for k in ("ssm_c_re", "ssm_c_im"))
    par = np.concatenate([both(a["ssm_a_re"][0]), both(a["ssm_a_im"][0]), both(ldt), both(a["ssm_b_re"][0]), both(a["ssm_b_im"][0]),
                          stacked(c_re, c_im).reshape(P, -1), stacked(c_im, c_re).reshape(P, -1)], axis=1)

    def cols(v):
        return v.reshape(-1, P).T

    gains = np.concatenate([a["g_pool"][0], a["g_attn"][0], a["g_ssm"][0]])
    vec = np.concatenate([cols(a["ssm_d"][0]), cols(a["b_glu"][0]), cols(gains), cols(a["pool_scale"][0]),
                          np.repeat(a["router_bias"][None], P, axis=0), np.repeat(a["rel_bias"][0][:, -1][None], P, axis=0)], axis=1)
    rel = np.arange(P)[:, None] + P - np.arange(2 * P)[None, :]
    tab = a["rel_bias"][0][:, np.clip(rel, -REL, REL) + REL]
    windows = np.repeat([2, 4, 8, 16], 64).reshape(2, P).T[:, :, None]
    rcnt = (1.0 / np.minimum(np.arange(T) + 1, windows)).astype(np.float32)
    return {
        "xT": a["x"][0].T, "x": a["x"][0], "pT": a["p"][0, 0].T, "w_in": a["w_in"][0], "w_out": a["w_out"][0],
        "w_pool": a["w_pool"][0], "rel_tab": tab.transpose(1, 0, 2), "ssm_par": par, "vec": vec, "rcnt": rcnt,
        "w_glu": a["w_glu"][0], "w_router": a["w_router"],
        "ln": np.stack([a["ln1_g"][0], a["ln1_b"][0], a["ln2_g"][0], a["ln2_b"][0]]),
        "w_exp_gate": a["w_exp_gate"][0], "w_exp_up": a["w_exp_up"][0], "w_exp_down": a["w_exp_down"][0],
        "w_ple_gate": a["w_ple_gate"][0], "w_ple_proj": a["w_ple_proj"][0],
    }


def kernel(**inputs):
    import concourse.bacc as bacc
    from concourse.bass_utils import run_bass_kernel_spmd

    nc = bacc.Bacc("TRN2", target_bir_lowering=False, num_devices=1)
    arrays = {k: np.ascontiguousarray(v) for k, v in _lay_out(inputs).items()}
    io = {k: nc.dram_tensor("in_" + k, v.shape, mybir.dt.from_np(v.dtype), kind="ExternalInput").ap() for k, v in arrays.items()}
    out = nc.dram_tensor("out", (T, D), F32, kind="ExternalOutput").ap()
    trunk(nc, io, out)
    r = run_bass_kernel_spmd(nc, [{"in_" + k: v for k, v in arrays.items()}], core_ids=[0])
    return r.results[0]["out"].reshape(1, T, D)
```

```python
from contextlib import ExitStack

import numpy as np

import concourse.bass as bass
from concourse import mybir

F32 = mybir.dt.float32
F32R = mybir.dt.float32r
I32 = mybir.dt.int32
ALU = mybir.AluOpType
ACT = mybir.ActivationFunctionType
AX = mybir.AxisListType

P = 128
D = 1024
T = 512
NT = T // P
KD = D // P
POOL_W, ATT_W, SSM_W = 256, 384, 384
IN_W = POOL_W + 3 * ATT_W + SSM_W
HEADS, HD = 6, 64
REL = 128
G, GD, NS = 24, 16, 64
CH = 8
NC = T // CH
Q = G // 2
NE, DE = 16, 256
EG, EPG = 4, 4
PLE = 256
ALPHA = 2.0 ** 0.25
EPS = 1e-5
NEG = -1.0e30
BIG = 3.0e38
KS = 4
CAP = P
OVER = 7
SLOT_TILES = NE + OVER
PAD = 4096
ROUND = 1.5 * 2.0 ** 23
PI2_A = 6.28125
PI2_B = 0.00193500518798828125
PI2_C = float(2 * np.pi - PI2_A - PI2_B)
PI_SAFE = 3.1415925

NG = Q + G
C_ARE, C_AIM, C_LDT = 0, NG, 2 * NG
C_BRE = 3 * NG
C_BIM = C_BRE + NG * GD
C_CA = C_BIM + NG * GD
C_CB = C_CA + G * GD
SSM_COLS = C_CB + G * GD
V_D, V_BG, V_GAIN, V_PS, V_RB, V_RC = 0, 3, 6, 14, 16, 32
VEC_COLS = 38

FIRST_K = (0, 1, 2, 4, KD)
SCORE_AT = {0: (0, 0, 0), 2: (0, 128, 128), 3: (1, 0, 512), 1: (2, 0, 1024)}
MIX_AT = ((0, 1), (5, 6, 7), (2, 3, 4))
WO_AT = ((2, 6, 1), (7, 0, 3))
PG_AT, PP_AT = (2, 7), (1, 0)
B_ROUTER, B_COUNT = 6, 3
B_TOK, B_GU, B_ACT, B_DN = (4, 5), (3, 6), (7, 0), (1, 2)
PT_AT = {0: 0, 1: 512, 3: 896, 2: 1024}
PT_BANKS = (3, 4, 7)
PT_UNITS = [((0,), 0, 512), ((1, 3), 512, 512), ((2,), 1024, 256)]


def trunk(nc, io, out):
    with ExitStack() as ctx:
        def sb(name, shape, dt=F32):
            return ctx.enter_context(nc.sbuf_tensor(name, shape, dt))

        def sem(name):
            return ctx.enter_context(nc.semaphore(name))

        start = -(-nc.sbuf_base // 32) * 32
        RA = sb("region_a", [P, 14336])
        RB = sb("region_b", [P, 8192])
        RC = sb("region_c", [P, 9600])
        RE = sb("region_e", [P, 4096])
        RF = sb("region_f", [P, 4096])
        RG = sb("region_g", [P, 4096])
        RH = sb("region_h", [P, 7680])
        ident = sb("ident", [P, P])
        ones = sb("ones", [P, P])
        tri = sb("tri", [P, P])
        vec = sb("vec", [P, VEC_COLS])
        w_rt = sb("w_rt", [P, KD, NE])
        w_pl = sb("w_pl", [P, 2, P])
        ln_st = sb("ln_st", [P, NT, 12])
        ln_mv = sb("ln_mv", [P, NT, 2])
        ln_rs = sb("ln_rs", [P, NT, 2])
        att_mx = sb("att_mx", [P, 4, 4])
        att_sm = sb("att_sm", [P, 4, 4])
        rms_r = sb("rms_r", [P, 3, NT])

        O_SSM, O_Q, O_K, O_V, O_PL = 0, KD * 384, KD * 768, KD * 1152, KD * 1536
        w_ssm = RA[:, O_SSM:O_SSM + KD * 384].rearrange("p (k n) -> p k n", k=KD)
        w_q = RA[:, O_Q:O_Q + KD * 384].rearrange("p (k n) -> p k n", k=KD)
        w_k = RA[:, O_K:O_K + KD * 384].rearrange("p (k n) -> p k n", k=KD)
        w_v = RA[:, O_V:O_V + KD * 384].rearrange("p (k n) -> p k n", k=KD)
        w_up = RA[:, O_PL:O_PL + KD * 256].rearrange("p (k n) -> p k n", k=KD)
        prob = RA[:, 0:5120].rearrange("p (r n) -> p r n", r=4)
        probT = RA[:, 5120:7680].rearrange("p (r n) -> p r n", r=2)
        x_rot = RA[:, 2304:3840].rearrange("p (r n) -> p r n", r=2)
        x_tmp = RA[:, 3840:5376].rearrange("p (r n) -> p r n", r=2)
        s_in = RA[:, 7680:9216].rearrange("p (g c) -> p g c", g=G)
        y_ch = RA[:, 9216:10752].rearrange("p (g c) -> p g c", g=G)
        sgl = RA[:, 9216:10752].rearrange("p (m t) -> p m t", m=3)
        yT = RA[:, 10752:12288].rearrange("p (m t) -> p m t", m=3)
        w_glu = RA[:, 12288:13440].rearrange("p (k n) -> p k n", k=3)
        par = RB[:, 0:SSM_COLS]
        bb = RB[:, 2028:3180].rearrange("p (r g h) -> p r g h", r=2, g=NG)
        b_st = RB[:, 3180:3564].rearrange("p (g h) -> p g h", g=G)
        tmp = RB[:, 3564:7020]
        pw = RB[:, 7020:7668].rearrange("p (r g l) -> p r g l", r=2, g=NG)
        sm = RB[:, 7668:8192]
        pl_s = RB[:, 3564:5612].rearrange("p (r m t) -> p r m t", r=2, m=2)
        rcnt = RB[:, 5612:6636].rearrange("p (k n) -> p k n", k=2)
        w_o = RB[:, :].rearrange("p (k n) -> p k n", k=KD)
        bx = RC[:, 0:3072].rearrange("p (r q j h) -> p r q j h", r=2, q=Q, j=CH)
        kern = RC[0:GD, 0:3072].rearrange("p (g l h) -> p g l h", g=G, l=CH)
        bxT = RC[:, 3072:6144].rearrange("p (r q s) -> p r q s", r=2, q=Q)
        cp = RC[:, 6144:9600].rearrange("p (g l h) -> p g l h", g=G, l=CH + 1)
        w_pg = RC[:, 0:8192].rearrange("p (k n) -> p k n", k=KD)
        rt = RC[:, 8192:9600]
        act_e = RC[:, 6144:7680].rearrange("p (r s n) -> p r s n", r=2, s=3)
        xT = RE[:, :].rearrange("p (k t) -> p k t", k=KD)
        hdT = RE[:, :].rearrange("p (k t) -> p k t", k=KD)
        hg = RE[:, :].rearrange("p (r n) -> p r n", r=4)
        rbias = RF[:, 0:1536].rearrange("p (h n) -> p h n", h=HEADS)
        rot = RF[:, 1536:3096].rearrange("p (r q c) -> p r q c", r=2, q=Q)
        decay = RF[:, 3096:3864]
        xh = RF[:, :].rearrange("p (t d) -> p t d", t=NT)
        qT = RG[:, 0:1536].rearrange("p (m t) -> p m t", m=3)
        kT = RG[:, 1536:3072].rearrange("p (m t) -> p m t", m=3)
        plT = RG[:, 3072:4096].rearrange("p (m t) -> p m t", m=2)
        ssum = [RG[:, 3072:3584], RG[:, 3584:4096], RA[:, 13440:13952]]
        hT = RG[:, :].rearrange("p (k t) -> p k t", k=KD)
        hgT = RG[:, 0:2048].rearrange("p (r k s) -> p r k s", r=2, k=KD)
        y_e = [RG[:, 2048:3072], RG[:, 3072:4096], RB[:, 6144:7168], RB[:, 7168:8192]]
        uT = RH[:, 0:1536].rearrange("p (m t) -> p m t", m=3)
        uch = RH[:, 1536:3072].rearrange("p (g c) -> p g c", g=G)
        m0 = RH[:, 3072:6144].rearrange("p (g l h) -> p g l h", g=G, l=CH)
        vN = RH[:, 6144:7680].rearrange("p (t n) -> p t n", t=NT)
        w_pp = RH[:, 0:2048].rearrange("p (k n) -> p k n", k=2)
        pT = RH[:, 2048:3072].rearrange("p (k t) -> p k t", k=2)
        lng = RH[:, 3072:4096]
        lnb = RH[:, 4096:5120]
        ple_t = RH[:, 5120:6144]
        rtT = RH[0:NE, 6144:6144 + T]
        sq2 = RH[:, 5120:6144].rearrange("p (r n) -> p r n", r=2)
        ebuf = [RA[:, 0:6144], RA[:, 6144:12288], RB[:, 0:6144], RC[:, 0:6144]]

        A0, C0, H0 = start, start + 4 * (14336 + 8192), start + 4 * (14336 + 8192 + 9600 + 3 * 4096)

        G0 = H0 - 4 * 4096

        def over(name, cols, at):
            return nc.alloc_sbuf_tensor_at(name, [P, cols], F32R, offset=at)
        dn_hi = over("down_upper", 2048, A0 + 4 * 12288)
        dn_lo = over("down_lower", 2048, H0)
        gu_hi = over("gate_up_upper", KS * 2 * DE, H0 + 4 * 5120)
        gu_lo = [over("gate_up_lower0", KS * DE, H0 + 4 * 2048),
                 over("gate_up_lower1", KS * DE, C0 + 4 * 8192)]
        x_hi = [over(f"tokens_upper{r}", KS * P, G0 + 4 * (1024 * r + 512)) for r in range(2)]
        x_lo = over("tokens_lower", KS * P, H0 + 4 * 7168)
        act_hi = [over(f"act_upper{r}", DE, C0 + 4 * (6144 + 768 * r + 512)) for r in range(2)]
        act_lo = [over(f"act_lower{r}", DE, C0 + 4 * (7680 + DE * r)) for r in range(2)]

        bank = [ctx.enter_context(nc.psum_tensor(f"bank{i}", [P, 512], F32)) for i in range(8)]

        def dram(name, shape, dt=F32):
            return nc.dram_tensor(name, shape, dt, kind="Internal").ap()
        u_d = dram("u_scratch", (SSM_W, T))
        y_d = dram("y_scratch", (SSM_W, T))
        h_d = dram("h_scratch", (T, D))
        inv_d = dram("slot_scratch", (SLOT_TILES * P, 1), I32)
        ye_d = dram("expert_scratch", (2 * T, D))

        dt_, expo, ang, turns, angr, sinf, sinh = (
            sm[:, lo:lo + w] for lo, w in ((0, 36), (36, 48), (84, 48), (132, 48), (180, 48), (228, 48), (276, 48)))
        u8 = sm[:, 324:348].rearrange("p (r q) -> p r q", r=2)
        mag8 = sm[:, 348:360]
        r_s = rt[:, 0:NT * NE]
        r_sel = rt[:, 1024:1024 + NT * NE].rearrange("p (t e) -> p t e", t=NT)
        eps_t = sb("eps_t", [P, 1])

        io_t = sb("io_t", [P, 2 * NT], I32)
        pad_t = sb("pad_t", [P, SLOT_TILES], I32)
        slot_i = sb("slot_i", [P, 2 * NT], I32)
        inv_t = sb("inv_t", [P, SLOT_TILES], I32)
        tok_t = sb("tok_t", [P, SLOT_TILES], I32)
        cur_t = sb("cur_t", [P, 2], I32)
        over_i = sb("over_i", [1, 8], I32)
        e_off = sb("e_off", [P, NE])
        io_o = sb("io_o", [P, OVER])
        wgt = sb("wgt", [P, 2, NT])

        S = {n: sem(n) for n in (
            "x_in0 x_in1 x_in2 x_in3 wqk_in wv_in wup_in small_in par_in rb_in wpl_in wglu_in rc_in "
            "wo_in wpg_in wpp_in ln_in xh_in "
            "const_set dve_step act_step gp_step uT_done qk_done pool_in_done v_done bx_ready bxT_done "
            "cp_ready kern_done rot_ready xrot_done "
            "u_out u_back m0_in s_ready s_moved y_evac y_out y_back yin_ready gelu_done glu_sig ssm_done "
            "pool_ready pool_mixed pe_u pe_qk pe_pool pe_v pe_bxT pe_kern pe_x pe_s pe_pt pe_pv pe_pm pe_y "
            "pe_glu s_read s_max p_exp p_norm pt_evac pv_evac sq_done sq_added pe_sq rms_sqrt wo_scaled x_scaled wo_read pe_wo "
            "ang trig rt_by_token sel_ready gu_hi_set gu_lo_set z_ready ln_sqrt h_ready pe_hT hT_evac h_out0 h_out1 h_out2 h_out3 pe_rt sig_rt pe_cnt slots_ready inv_set inv_put "
            "inv_back tok_ready pe_pg pe_pp ple_sig ple_done "
            "e_in0 e_in1 e_in2 e_in3 hg_in0 hg_in1 hg_in2 hg_in3 ye_out0 ye_out1 ye_out2 ye_out3 pe_hgT hgT_evac pe_gu silu_done a_ready "
            "pe_aT aT_evac pe_dn ye_evac moe_done "
            "o_col o_in o_hg o_t o_te o_gu o_si o_a o_at o_ae o_dn o_ye o_out o_round aT_hi dn_hi_set dn_lo_set "
            "yk0_in0 yk0_in1 yk0_in2 yk0_in3 yk1_in0 yk1_in1 yk1_in2 yk1_in3 z2_ready ln2_sqrt ln2_in rs2_ready var2_done xhat_done gain_done o_pool o_dve out_st").split()}

        block = ctx.enter_context(nc.Block())

        w_in_v = io["w_in"].rearrange("(p k) n -> p k n", k=KD)
        eg_v = io["w_exp_gate"].rearrange("e (p k) n -> e p (k n)", k=KD)
        eu_v = io["w_exp_up"].rearrange("e (p k) n -> e p (k n)", k=KD)
        ed_v = io["w_exp_down"].rearrange("e (p k) n -> e p (k n)", k=2)

        @block.sync
        def _(sp):
            def load(dst, src, signal):
                sp.dma_start(dst, src).then_inc(S[signal], 16)

            xv = io["xT"].rearrange("(p k) t -> p k t", k=KD)
            for i in range(4):
                ks = slice(FIRST_K[i], FIRST_K[i + 1])
                load(xT[:, ks, :], xv[:, ks, :], f"x_in{i}")
                load(w_ssm[:, ks, :], w_in_v[:, ks, POOL_W + 3 * ATT_W:IN_W], f"x_in{i}")
            load(par, io["ssm_par"], "par_in")
            load(w_q, w_in_v[:, :, POOL_W:POOL_W + ATT_W], "wqk_in")
            load(w_k, w_in_v[:, :, POOL_W + ATT_W:POOL_W + 2 * ATT_W], "wqk_in")
            load(w_up, w_in_v[:, :, 0:POOL_W], "wup_in")
            load(w_v, w_in_v[:, :, POOL_W + 2 * ATT_W:POOL_W + 3 * ATT_W], "wv_in")
            load(rbias, io["rel_tab"], "rb_in")
            sp.wait_ge(S["cp_ready"], 1)
            load(rcnt, io["rcnt"], "rc_in")
            sp.wait_ge(S["const_set"], 1)
            sp.wait_ge(S["kern_done"], 6)
            for j in range(CH):
                sp.dma_start(m0[GD * j:GD * (j + 1), :, j:CH, :], kern[:, :, 0:CH - j, :]).then_inc(S["m0_in"], 16)
            sp.wait_ge(S["s_ready"], 1)
            sv = s_in.rearrange("p (q r) c -> p q r c", r=2)
            for r in range(2):
                for par_ in range(2):
                    sp.dma_start(sv[64 * r:64 * r + 64, :, par_, :],
                                 x_tmp[64 * par_:64 * par_ + 64, r, :].rearrange("p (q c) -> p q c", q=Q)).then_inc(S["s_moved"], 16)
            sp.wait_ge(S["pe_v"], NT)
            load(w_glu, io["w_glu"].rearrange("(k p) n -> p k n", p=P), "wglu_in")
            sp.wait_ge(S["rot_ready"], 1)
            sp.wait_ge(S["pe_pm"], 2)
            load(w_o, io["w_out"].rearrange("(k p) n -> p k n", p=P), "wo_in")
            sp.wait_ge(S["y_evac"], 3)
            for j in range(CH):
                sp.dma_start(y_d.rearrange("(g h) (j c) -> j h g c", h=GD, j=CH)[j],
                             y_ch[GD * j:GD * (j + 1), :, :]).then_inc(S["y_out"], 16)
            sp.wait_ge(S["y_out"], 16 * CH)
            load(yT, y_d.rearrange("(m p) t -> p m t", p=P), "y_back")
            load(w_pg, io["w_ple_gate"].rearrange("(p k) n -> p k n", k=KD), "wpg_in")
            load(lng, io["ln"][0:1, :].partition_broadcast(P), "ln_in")
            load(lnb, io["ln"][1:2, :].partition_broadcast(P), "ln_in")
            sp.wait_ge(S["yin_ready"], 3)
            load(w_pp, io["w_ple_proj"].rearrange("(k p) n -> p k n", p=P), "wpp_in")
            load(pT, io["pT"].rearrange("(k p) t -> p k t", p=P), "wpp_in")
            sp.wait_ge(S["s_read"], HEADS)
            load(xh, io["x"].rearrange("(t p) d -> p t d", p=P), "xh_in")
            sp.wait_ge(S["pe_pv"], HEADS)
            sp.wait_ge(S["ssm_done"], 3)

            def load_expert(b, e, first=False):
                sp.dma_start(ebuf[b][:, 0:2048], eg_v[e]).then_inc(S[f"e_in{b}"], 16)
                sp.dma_start(ebuf[b][:, 2048:4096], eu_v[e]).then_inc(S[f"e_in{b}"], 16)
                sp.dma_start(ebuf[b][:, 4096:6144], ed_v[e]).then_inc(S[f"e_in{b}"], 16)

            load_expert(0, 0)
            load_expert(1, 1)
            for t in range(NT):
                sp.wait_ge(S["h_ready"], t + 1)
                sp.dma_start(h_d[t * P:(t + 1) * P, :], xh[:, t, :]).then_inc(S[f"h_out{t}"], 16)
            load(lng, io["ln"][2:3, :].partition_broadcast(P), "ln2_in")
            load(lnb, io["ln"][3:4, :].partition_broadcast(P), "ln2_in")
            sp.wait_ge(S["pe_wo"], 2 * NT)
            load_expert(2, 2)
            sp.wait_ge(S["pe_pg"], 2 * NT)
            load_expert(3, 3)
            with sp.Fori(0, 3) as blk:
                for b in range(4):
                    e = blk * 4 + (4 + b)
                    sp.wait_ge(S["pe_gu"], 4 * blk + b + 1)
                    sp.dma_start(ebuf[b][:, 0:2048], eg_v[bass.ds(e, 1)].rearrange("o p n -> p (o n)")).then_inc(S[f"e_in{b}"], 16)
                    sp.dma_start(ebuf[b][:, 2048:4096], eu_v[bass.ds(e, 1)].rearrange("o p n -> p (o n)")).then_inc(S[f"e_in{b}"], 16)
                    sp.wait_ge(S["dn_lo_set"], 4 * blk + b + 1)
                    sp.dma_start(ebuf[b][:, 4096:6144], ed_v[bass.ds(e, 1)].rearrange("o p n -> p (o n)")).then_inc(S[f"e_in{b}"], 16)
            sp.wait_ge(S["tok_ready"], 1)
            n_over = sp.value_load(over_i[0:1, 0:1], min_val=0, max_val=OVER)
            sp.wait_ge(S["pe_dn"], NE)
            with sp.If(n_over > 0):
                with sp.Fori(0, OVER) as o:
                    with sp.If(o < n_over):
                        e = sp.value_load(over_i[0:1, bass.ds(o + 1, 1)], min_val=0, max_val=NE - 1)
                        sp.wait_ge(S["o_col"], o + 1)
                        sp.dma_start(ebuf[0][:, 0:2048], eg_v[bass.ds(e, 1)].rearrange("o p n -> p (o n)")).then_inc(S["o_in"], 16)
                        sp.dma_start(ebuf[0][:, 2048:4096], eu_v[bass.ds(e, 1)].rearrange("o p n -> p (o n)")).then_inc(S["o_in"], 16)
                        sp.dma_start(ebuf[0][:, 4096:6144], ed_v[bass.ds(e, 1)].rearrange("o p n -> p (o n)")).then_inc(S["o_in"], 16)
                        sp.wait_ge(S["o_out"], 16 * (o + 1))
                        sp.sem_inc(S["o_round"], 1)
            sp.wait_ge(S["moe_done"], 1)
            yv = ye_d.rearrange("(t p k) d -> t k p d", p=P, k=2)
            for t in range(NT):
                for k in range(2):
                    sp.dma_start(RA[:, (2 * t + k) * D:(2 * t + k + 1) * D], yv[t, k]).then_inc(S[f"yk{k}_in{t}"], 16)
            for t, signal, count in ((0, "o_pool", 1), (2, "o_dve", 1), (3, "o_dve", 2), (1, "o_dve", 3)):
                sp.wait_ge(S[signal], count)
                sp.dma_start(out[t * P:(t + 1) * P, :], xh[:, t, :]).then_inc(S["out_st"], 16)
            sp.wait_ge(S["out_st"], 16 * NT)

        @block.gpsimd
        def _(gp):
            n = [0]

            def link(ins):
                n[0] += 1
                ins.then_inc(S["gp_step"], 1)
                gp.wait_ge(S["gp_step"], n[0])

            g = nc.gpsimd
            link(g.memset(ident[:], 0.0))
            link(g.memset(ones[:], 1.0))
            link(g.affine_select(out=ident[:], in_=ident[:], compare_op=ALU.not_equal, fill=1.0, base=0,
                                 pattern=[[-1, P]], channel_multiplier=1))
            link(g.affine_select(out=tri[:], in_=ones[:], compare_op=ALU.is_gt, fill=0.0, base=0,
                                 pattern=[[1, P]], channel_multiplier=-1))
            link(g.memset(w_pl[:], 0.0))
            link(g.memset(m0, 0.0))
            link(g.iota(io_t[:].rearrange("p (t k) -> p t k", k=2), pattern=[[2 * P, NT], [1, 2]], base=0, channel_multiplier=2))
            link(g.iota(pad_t[:], pattern=[[0, SLOT_TILES]], base=PAD, channel_multiplier=0))
            link(g.iota(e_off[:], pattern=[[CAP, NE]], base=0, channel_multiplier=0, allow_small_or_imprecise_dtypes=True))
            g.iota(io_o[:], pattern=[[1, OVER]], base=0, channel_multiplier=0,
                   allow_small_or_imprecise_dtypes=True).then_inc(S["const_set"], 1)
            gp.wait_ge(S["const_set"], 1)
            for i in range(4):
                h, m = i % 2, i // 2
                gp.dma_start(w_pl[64 * h:64 * h + 64, m, 64 * h:64 * h + 64], io["w_pool"][i]).then_inc(S["wpl_in"], 16)
            gp.dma_start(inv_d.rearrange("(p c) o -> p (c o)", p=P), pad_t[:]).then_inc(S["inv_set"], 16)
            gp.wait_ge(S["rb_in"], 16)
            link(g.memset(rbias[0:64, :, 192:256], NEG))

            gp.wait_ge(S["bx_ready"], 1)
            tmp_g = decay
            link(g.memset(rot[:, 0, :, 0:1], 1.0))
            link(g.memset(rot[:, 1, :, 0:1], 0.0))
            link(g.tensor_copy(rot[:, 0, :, 1:2], u8[:, 0, :].unsqueeze(2)))
            link(g.tensor_copy(rot[:, 1, :, 1:2], u8[:, 1, :].unsqueeze(2)))
            m = 1
            while m < NC:
                shape = [P, Q, m]
                t = tmp_g[:, 0:Q * m].rearrange("p (q c) -> p q c", q=Q)
                ar, ai = rot[:, 0, :, 1:m + 1], rot[:, 1, :, 1:m + 1]
                br = rot[:, 0, :, m:m + 1].broadcast_to(shape)
                bi = rot[:, 1, :, m:m + 1].broadcast_to(shape)
                orr, oi = rot[:, 0, :, m + 1:2 * m + 1], rot[:, 1, :, m + 1:2 * m + 1]
                link(g.tensor_tensor(t, ai, bi, ALU.mult))
                link(g.tensor_tensor(orr, ar, br, ALU.mult))
                link(g.tensor_tensor(orr, orr, t, ALU.subtract))
                link(g.tensor_tensor(t, ar, bi, ALU.mult))
                link(g.tensor_tensor(oi, ai, br, ALU.mult))
                link(g.tensor_tensor(oi, oi, t, ALU.add))
                m *= 2
            dec = decay.rearrange("p (q c) -> p q c", q=Q)
            link(g.tensor_copy(dec, mag8[:].unsqueeze(2).broadcast_to([P, Q, NC])))
            g.memset(dec[:, :, 0:1], 0.0).then_inc(S["rot_ready"], 1)
            gp.wait_ge(S["rot_ready"], 1)

            gp.wait_ge(S["pool_in_done"], 2)
            gp.wait_ge(S["cp_ready"], 1)
            a, b2 = pl_s[:, 0], pl_s[:, 1]

            def add_shift(o, i, w, lo, ms):
                link(g.tensor_copy(o[lo:P, ms, 0:w], i[lo:P, ms, 0:w]))
                link(g.tensor_tensor(o[lo:P, ms, w:T], i[lo:P, ms, w:T], i[lo:P, ms, 0:T - w], ALU.add))

            both, second = slice(0, 2), slice(1, 2)
            add_shift(a, plT, 1, 0, both)
            add_shift(b2, a, 2, 0, second)
            add_shift(b2, a, 2, 64, slice(0, 1))
            link(g.tensor_copy(a[64:P, 0:1], b2[64:P, 0:1]))
            add_shift(a, b2, 4, 0, second)
            link(g.tensor_copy(b2[64:P, 1:2], a[64:P, 1:2]))
            add_shift(a, b2, 8, 64, second)
            gp.wait_ge(S["rc_in"], 16)
            link(g.tensor_tensor(a, a, rcnt, ALU.mult))
            g.tensor_tensor(a, a, plT, ALU.subtract).then_inc(S["pool_ready"], 1)

            gp.wait_ge(S["wo_in"], 16)
            gp.wait_ge(S["small_in"], 32)
            for k in (0, 1, 5, 6, 7, 2, 3, 4):
                g.tensor_scalar(w_o[:, k, :], w_o[:, k, :], vec[:, V_GAIN + k:V_GAIN + k + 1], None, ALU.mult).then_inc(S["wo_scaled"], 1)

            def add_squares(i, group, r):
                gp.wait_ge(S["sq_done"], (2, 4, 6, 7, 8)[i])
                g.tensor_tensor(ssum[group], ssum[group], sq2[:, r, :], ALU.add).then_inc(S["sq_added"], 1)
                gp.wait_ge(S["sq_added"], i + 1)

            def scale_x(t):
                g.tensor_scalar(xh[:, t, :], xh[:, t, :], ALPHA, None, ALU.mult).then_inc(S["x_scaled"], 1)

            add_squares(0, 0, 0)
            add_squares(1, 2, 1)
            gp.wait_ge(S["xh_in"], 16)
            scale_x(0)
            add_squares(2, 1, 0)
            add_squares(3, 1, 1)
            add_squares(4, 2, 0)
            for t in range(1, NT):
                scale_x(t)

            gp.wait_ge(S["pe_wo"], 2 * NT)
            link(g.memset(RE[:, :], 0.0))
            gp.wait_ge(S["slots_ready"], 1)
            gp.wait_ge(S["inv_set"], 16)
            for i in range(NT):
                for k in range(2):
                    gp.indirect_dma_start(
                        out=inv_d, out_offset=bass.IndirectOffsetOnAxis(ap=slot_i[:, 2 * i + k:2 * i + k + 1], axis=0),
                        in_=io_t[:, 2 * i + k:2 * i + k + 1], in_offset=None,
                        bounds_check=SLOT_TILES * P - 1, oob_is_err=False).then_inc(S["inv_put"], 16)
            gp.wait_ge(S["inv_put"], 16 * 2 * NT)
            gp.dma_start(inv_t[:], inv_d.rearrange("(c p) o -> p (c o)", p=P), allow_slow_non_contiguous=True).then_inc(S["inv_back"], 16)

            def gather(dst, idx, signal):
                gp.indirect_dma_start(out=dst, out_offset=None, in_=h_d,
                                      in_offset=bass.IndirectOffsetOnAxis(ap=idx, axis=0),
                                      bounds_check=T - 1, oob_is_err=False).then_inc(S[signal], 16)

            def scatter(idx, src, signal):
                gp.indirect_dma_start(out=ye_d, out_offset=bass.IndirectOffsetOnAxis(ap=idx, axis=0),
                                      in_=src, in_offset=None,
                                      bounds_check=2 * T - 1, oob_is_err=False).then_inc(S[signal], 16)

            gp.wait_ge(S["tok_ready"], 1)
            for t in range(NT):
                gp.wait_ge(S[f"h_out{t}"], 16)
            for e in range(4):
                gather(hg[:, e, :], tok_t[:, e:e + 1], f"hg_in{e}")
            for e in range(NE):
                if e + 4 < NE:
                    gp.wait_ge(S["pe_hgT"], e + 1)
                    gather(hg[:, e % 4, :], tok_t[:, e + 4:e + 5], f"hg_in{e % 4}")
                gp.wait_ge(S["ye_evac"], e + 1)
                scatter(inv_t[:, e:e + 1], y_e[e % 4], f"ye_out{e % 4}")
            n_over = gp.value_load(over_i[0:1, 0:1], min_val=0, max_val=OVER)
            for b in range(4):
                gp.wait_ge(S[f"ye_out{b}"], 16 * NE // 4)
            with gp.If(n_over > 0):
                with gp.Fori(0, OVER) as o:
                    with gp.If(o < n_over):
                        gp.wait_ge(S["o_col"], o + 1)
                        gp.sem_inc(S["o_round"], 1)
                        gather(hg[:, 0, :], cur_t[:, 0:1], "o_hg")
                        gp.wait_ge(S["o_ye"], 2 * o + 2)
                        gp.sem_inc(S["o_round"], 1)
                        scatter(cur_t[:, 1:2], y_e[0], "o_out")
                        gp.wait_ge(S["o_out"], 16 * (o + 1))
                        gp.sem_inc(S["o_round"], 1)
            gp.sem_inc(S["moe_done"], 1)
            gp.wait_ge(S["ln2_in"], 32)
            gp.wait_ge(S["xhat_done"], 1)
            link(g.tensor_tensor(xh[:, 0, :], xh[:, 0, :], lng, ALU.mult))
            g.tensor_tensor(xh[:, 0, :], xh[:, 0, :], lnb, ALU.add).then_inc(S["o_pool"], 1)
            gp.wait_ge(S["xhat_done"], 2)
            g.tensor_tensor(xh[:, 1, :], xh[:, 1, :], lng, ALU.mult).then_inc(S["gain_done"], 1)

        @block.scalar
        def _(ac):
            a = nc.scalar
            n = [0]

            def link(ins):
                n[0] += 1
                ins.then_inc(S["act_step"], 1)
                ac.wait_ge(S["act_step"], n[0])

            ac.dma_start(vec[:], io["vec"]).then_inc(S["small_in"], 16)
            ac.dma_start(w_rt[:], io["w_router"].rearrange("(p k) n -> p k n", k=KD)).then_inc(S["small_in"], 16)

            ac.wait_ge(S["small_in"], 32)
            ac.wait_ge(S["par_in"], 16)
            link(a.activation(par[64:P, C_CA:C_CB], par[64:P, C_CA:C_CB], ACT.Copy, scale=-1.0))
            link(a.activation(par[:, C_CB:SSM_COLS], par[:, C_CB:SSM_COLS], ACT.Copy, scale=-1.0))
            link(a.activation(dt_[:], par[:, C_LDT:C_LDT + NG], ACT.Exp))
            ac.wait_ge(S["ang"], 1)
            link(a.activation(expo[:], expo[:], ACT.Exp))
            link(a.activation(sinf[:], angr[:], ACT.Sin))
            a.activation(sinh[:], angr[:], ACT.Sin, scale=0.5).then_inc(S["trig"], 1)
            for m in range(3):
                ac.wait_ge(S["pe_u"], m + 1)
                a.activation(uT[:, m, :].rearrange("p (j c) -> p j c", j=CH),
                             bank[m][:].rearrange("p (c j) -> p j c", j=CH), ACT.Copy).then_inc(S["uT_done"], 1)
                ac.wait_ge(S["uT_done"], m + 1)
                ac.dma_start(u_d[m * P:(m + 1) * P, :], uT[:, m, :]).then_inc(S["u_out"], 16)
            for m in range(6):
                ac.wait_ge(S["pe_qk"], m + 1)
                dst = (qT if m % 2 == 0 else kT)[:, m // 2, :]
                a.activation(dst, bank[(3 + m) % 8][:], ACT.Copy).then_inc(S["qk_done"], 1)
                if m == 0:
                    ac.wait_ge(S["u_out"], 48)
                    for j in range(CH):
                        ac.dma_start(uch[GD * j:GD * (j + 1), :, :],
                                     u_d.rearrange("(g h) (j c) -> j h g c", h=GD, j=CH)[j]).then_inc(S["u_back"], 16)
            for m in range(6):
                ac.wait_ge(S["pe_kern"], m + 1)
                a.activation(kern[:, 4 * m:4 * m + 4], bank[(7 + m) % 8][0:GD, :].rearrange("p (g l h) -> p g l h", g=4, l=CH),
                             ACT.Copy).then_inc(S["kern_done"], 1)
            for m in range(2):
                ac.wait_ge(S["pe_pool"], m + 1)
                a.activation(plT[:, m, :], bank[3 + m][:], ACT.Copy).then_inc(S["pool_in_done"], 1)

            def v_copy(t):
                ac.wait_ge(S["pe_v"], t + 1)
                a.activation(vN[:, t, :], bank[[5, 6, 7, 3][t]][:, 0:ATT_W], ACT.Copy).then_inc(S["v_done"], 1)

            def exps(h):
                ac.wait_ge(S["s_max"], h + 1)
                for i in range(NT):
                    o, w = SCORE_AT[i][2], (i + 1) * P
                    blk = prob[:, h % 4, o:o + w]
                    last = a.activation(blk, blk, ACT.Exp, bias=att_mx[:, h % 4, i:i + 1],
                                        accum_out=att_sm[:, h % 4, i:i + 1])
                    if i < NT - 1:
                        link(last)
                last.then_inc(S["p_exp"], 1)

            def pt_copy(h):
                for u, (_, o, w) in enumerate(PT_UNITS):
                    k = 3 * h + u
                    ac.wait_ge(S["pe_pt"], k + 1)
                    if u == 0 and h >= 2:
                        ac.wait_ge(S["pe_pv"], h - 1)
                    a.activation(probT[:, h % 2, o:o + w], bank[PT_BANKS[u]][:, 0:w], ACT.Copy).then_inc(S["pt_evac"], 1)

            def pv_copy(pair):
                ac.wait_ge(S["pe_pv"], 2 * pair + 2)
                a.activation(hdT[:, 2 + pair, :], bank[5 + pair % 2][:], ACT.Copy).then_inc(S["pv_evac"], 1)

            def square(i, m, dst):
                a.activation(dst, hdT[:, m, :], ACT.Square).then_inc(S["sq_done"], 1)

            v_copy(0)
            exps(0)
            v_copy(1)
            v_copy(2)
            exps(1)
            v_copy(3)
            for m in range(2):
                ac.wait_ge(S["pe_pm"], m + 1)
                a.activation(hdT[:, m, :], bank[4 + m][:], ACT.Copy, scale=vec[:, V_PS + m:V_PS + m + 1]).then_inc(S["pool_mixed"], 1)
            for m in range(3):
                ac.wait_ge(S["pe_y"], m + 1)
                a.activation(y_ch[:, 8 * m:8 * m + 8, :], bank[(6, 7, 5)[m]][:].rearrange("p (g c) -> p g c", g=8),
                             ACT.Copy).then_inc(S["y_evac"], 1)
                if m == 0:
                    exps(2)
            pt_copy(0)
            exps(3)
            ac.wait_ge(S["pool_mixed"], 2)
            square(0, 0, ssum[0])
            square(1, 1, sq2[:, 0, :])
            pt_copy(1)
            pv_copy(0)
            pt_copy(2)
            exps(4)
            pt_copy(3)
            exps(5)
            pv_copy(1)
            pt_copy(4)
            for m in range(3):
                ac.wait_ge(S["yin_ready"], m + 1)
                a.activation(hdT[:, 5 + m, :].rearrange("p (c j) -> p c j", j=CH),
                             yT[:, m, :].rearrange("p (j c) -> p c j", j=CH), ACT.Gelu_apprx_tanh).then_inc(S["gelu_done"], 1)
            ac.wait_ge(S["pv_evac"], 2)
            square(2, 2, ssum[2])
            square(3, 3, sq2[:, 1, :])
            for m in range(3):
                ac.wait_ge(S["pe_glu"], m + 1)
                a.activation(sgl[:, m, :], bank[(6, 0, 1)[m]][:], ACT.Sigmoid, bias=vec[:, V_BG + m:V_BG + m + 1]).then_inc(S["glu_sig"], 1)
            pt_copy(5)
            ac.wait_ge(S["ssm_done"], 1)
            square(4, 5, ssum[1])
            ac.wait_ge(S["ssm_done"], 2)
            ac.wait_ge(S["sq_added"], 1)
            square(5, 6, sq2[:, 0, :])
            ac.wait_ge(S["ssm_done"], 3)
            ac.wait_ge(S["sq_added"], 2)
            square(6, 7, sq2[:, 1, :])
            pv_copy(2)
            ac.wait_ge(S["pv_evac"], 3)
            ac.wait_ge(S["sq_added"], 3)
            square(7, 4, sq2[:, 0, :])
            ac.wait_ge(S["pe_sq"], 1)
            for g in range(3):
                a.activation(rms_r[:, g, :], bank[4][:, g * NT:(g + 1) * NT], ACT.Sqrt, bias=eps_t[:],
                             scale=[1.0 / POOL_W, 1.0 / SSM_W, 1.0 / ATT_W][g]).then_inc(S["rms_sqrt"], 1)
            def hT_copy(t):
                for u in range(2):
                    ac.wait_ge(S["pe_hT"], 2 * t + u + 1)
                    a.activation(hT[:, 4 * u:4 * u + 4, t * P:(t + 1) * P], bank[4 + u][:].rearrange("p (k t) -> p k t", k=4),
                                 ACT.Copy).then_inc(S["hT_evac"], 1)

            def ple_gate(k):
                ac.wait_ge(S["pe_pg"], k + 1)
                if k >= 2:
                    ac.wait_ge(S["ple_done"], k - 1)
                elif k == 0:
                    ac.wait_ge(S["sq_added"], 5)
                a.activation(ple_t[:, (k % 2) * 512:(k % 2) * 512 + 512], bank[PG_AT[k % 2]][:], ACT.Sigmoid).then_inc(S["ple_sig"], 1)

            for t in range(NT):
                ac.wait_ge(S["z_ready"], t + 1)
                a.activation(ln_rs[:, t, 0:1], ln_mv[:, t, 1:2], ACT.Sqrt, bias=eps_t[:]).then_inc(S["ln_sqrt"], 1)
                if t >= 1:
                    hT_copy(t - 1)
            ple_gate(0)
            hT_copy(NT - 1)
            ac.wait_ge(S["pe_rt"], 1)
            a.activation(rtT, bank[B_ROUTER][0:NE, :], ACT.Sigmoid).then_inc(S["sig_rt"], 1)
            for k in range(1, 2 * NT):
                ple_gate(k)

            def hgT_copy(e, r):
                ac.wait_ge(S["pe_hgT"], e + 1)
                a.activation(hgT[:, r, 0:4, :], bank[B_TOK[0]][:].rearrange("p (k s) -> p k s", k=4), ACT.Copy).then_inc(S["hgT_evac"], 1)
                a.activation(x_hi[r][:], bank[B_TOK[1]][:], ACT.Copy).then_inc(S["hgT_evac"], 1)

            def gate_up_upper(b, loads):
                ac.wait_ge(S[f"e_in{b}"], 48 * loads)
                a.activation(gu_hi[:].rearrange("p (u n) -> p u n", u=2),
                             ebuf[b][:, 0:4096].rearrange("p (u n) -> p u n", u=2)[:, :, (KD - KS) * DE:KD * DE], ACT.Copy).then_inc(S["gu_hi_set"], 1)

            def expert(e, b, loads, last=False):
                r = b % 2
                ac.wait_ge(S["pe_gu"], e + 1)
                a.activation(act_e[:, r, 0, :], bank[B_GU[r]][:, 0:DE], ACT.Silu).then_inc(S["silu_done"], 1)
                if not last:
                    hgT_copy(e + 1, 1 - r)
                    gate_up_upper((b + 1) % 4, loads if b < 3 else loads + 1)
                ac.wait_ge(S["pe_aT"], e + 1)
                if last:
                    a.activation(act_e[:, r, 2, :], bank[B_ACT[r]][:, 0:DE], ACT.Copy).then_inc(S["aT_hi"], 1)
                    return
                a.activation(act_hi[r][:], bank[B_ACT[r]][:, 0:DE], ACT.Copy).then_inc(S["aT_hi"], 1)
                ac.wait_ge(S[f"e_in{b}"], 48 * loads)
                a.activation(dn_hi[:], ebuf[b][:, 4096:6144], ACT.Copy).then_inc(S["dn_hi_set"], 1)

            ac.wait_ge(S["pe_pg"], 2 * NT)
            hgT_copy(0, 0)
            ac.wait_ge(S["ple_done"], 2 * NT)
            gate_up_upper(0, 1)
            with ac.Fori(0, NE // 4 - 1) as blk:
                for b in range(4):
                    expert(4 * blk + b, b, blk + 1)
            for e in range(NE - 4, NE):
                expert(e, e % 4, NE // 4, last=(e == NE - 1))
            n_over = ac.value_load(over_i[0:1, 0:1], min_val=0, max_val=OVER)
            with ac.If(n_over > 0):
                with ac.Fori(0, OVER) as o:
                    with ac.If(o < n_over):
                        ac.wait_ge(S["o_t"], o + 1)
                        for u in range(2):
                            a.activation(hgT[:, 0, 4 * u:4 * u + 4, :], bank[B_TOK[u]][:].rearrange("p (k s) -> p k s", k=4),
                                         ACT.Copy).then_inc(S["o_te"], 1)
                        ac.wait_ge(S["o_gu"], o + 1)
                        a.activation(act_e[:, 0, 0, :], bank[B_GU[0]][:, 0:DE], ACT.Silu).then_inc(S["o_si"], 1)
                        ac.wait_ge(S["o_at"], o + 1)
                        a.activation(act_e[:, 0, 2, :], bank[B_ACT[0]][:, 0:DE], ACT.Copy).then_inc(S["o_ae"], 1)
            def deviation(t):
                ac.wait_ge(S["z2_ready"], t + 1)
                a.activation(RA[:, (8 + t) * D:(9 + t) * D], xh[:, t, :], ACT.Square, bias=ln_mv[:, t, 0:1],
                             accum_out=ln_mv[:, t, 1:2]).then_inc(S["var2_done"], 1)
                ac.wait_ge(S["var2_done"], t + 1)
                a.activation(ln_rs[:, t, 0:1], ln_mv[:, t, 1:2], ACT.Sqrt, bias=eps_t[:], scale=1.0 / D).then_inc(S["ln2_sqrt"], 1)

            def x_hat(t):
                ac.wait_ge(S["rs2_ready"], t + 1)
                a.activation(xh[:, t, :], xh[:, t, :], ACT.Identity, bias=ln_mv[:, t, 0:1], scale=ln_rs[:, t, 1:2]).then_inc(S["xhat_done"], 1)

            deviation(0)
            deviation(1)
            x_hat(0)
            deviation(2)
            x_hat(1)
            deviation(3)

        @block.tensor
        def _(pe):
            mm = nc.tensor.matmul

            def project(bank_i, w, m, signal):
                for k in range(KD):
                    last = mm(bank[bank_i][:], w[:, k, m * P:(m + 1) * P], xT[:, k, :], start=(k == 0), stop=(k == KD - 1))
                last.then_inc(S[signal], 1)

            for k in range(KD):
                if k in FIRST_K:
                    pe.wait_ge(S[f"x_in{FIRST_K.index(k)}"], 32)
                for m in range(3):
                    last = mm(bank[m][:], w_ssm[:, k, m * P:(m + 1) * P], xT[:, k, :], start=(k == 0), stop=(k == KD - 1))
                    if k == KD - 1:
                        last.then_inc(S["pe_u"], 1)
            pe.wait_ge(S["wqk_in"], 32)
            for m in range(6):
                if m == 5:
                    pe.wait_ge(S["uT_done"], 1)
                project((3 + m) % 8, w_q if m % 2 == 0 else w_k, m // 2, "pe_qk")
            def v_tile(t, bank_i):
                for k in range(KD):
                    last = mm(bank[bank_i][:, 0:ATT_W], xT[:, k, t * P:(t + 1) * P], w_v[:, k, :], start=(k == 0), stop=(k == KD - 1))
                last.then_inc(S["pe_v"], 1)

            def bx_turn(n, bank_i):
                for i in range(4):
                    r, q = n // 3, 4 * (n % 3) + i
                    last = nc.tensor.transpose(bank[bank_i][:, i * P:(i + 1) * P], bx[:, r, q].rearrange("p j h -> p (j h)"), ident[:])
                last.then_inc(S["pe_bxT"], 1)

            pe.wait_ge(S["const_set"], 1)
            pe.wait_ge(S["bx_ready"], 2)
            for n, (signal, count) in enumerate([("uT_done", 2), ("uT_done", 3), ("qk_done", 1), ("qk_done", 2), ("qk_done", 3), ("qk_done", 4)]):
                pe.wait_ge(S[signal], count)
                bx_turn(n, 1 + n)

            pe.wait_ge(S["cp_ready"], 1)
            for n, (signal, count) in enumerate([("qk_done", 5), ("qk_done", 6), ("bxT_done", 1), ("bxT_done", 2), ("bxT_done", 3), ("bxT_done", 4)]):
                pe.wait_ge(S[signal], count)
                for i in range(4):
                    g = 4 * n + i
                    last = mm(bank[(7 + n) % 8][0:GD, i * P:(i + 1) * P], b_st[:, g, :],
                              cp[:, g, 0:CH, :].rearrange("p l h -> p (l h)"), start=True, stop=True)
                last.then_inc(S["pe_kern"], 1)

            pe.wait_ge(S["bxT_done"], 6)
            pe.wait_ge(S["kern_done"], 2)
            pe.wait_ge(S["u_back"], 16 * CH)
            for r in range(2):
                for q in range(Q):
                    for h in range(2):
                        b = (5 + 2 * r + q // 6) % 8
                        last = mm(bank[b][64 * h:64 * h + 64, (q % 6) * NC:(q % 6 + 1) * NC], bxT[:, r, q, 64 * h:64 * h + 64],
                                  uch[:, 2 * q + h, :], start=True, stop=True)
            last.then_inc(S["pe_x"], 1)

            def scores(h):
                if h == 0:
                    pe.wait_ge(S["xrot_done"], 1)
                else:
                    pe.wait_ge(S["s_read"], h)
                rows = slice(64 * (h % 2), 64 * (h % 2) + 64)
                for i in (0, 2, 3, 1):
                    b, c, _ = SCORE_AT[i]
                    w = (i + 1) * P
                    last = mm(bank[b][:, c:c + w], qT[rows, h // 2, i * P:(i + 1) * P], kT[rows, h // 2, 0:w], start=True, stop=True)
                last.then_inc(S["pe_s"], 1)

            def turn_probs(h):
                pe.wait_ge(S["p_norm"], h + 1)
                for u, (tiles, _, _) in enumerate(PT_UNITS):
                    k = 3 * h + u
                    if k >= 3:
                        pe.wait_ge(S["pt_evac"], k - 2)
                    elif k == 0:
                        pe.wait_ge(S["v_done"], 4)
                    elif k == 2:
                        pe.wait_ge(S["y_evac"], 2)
                    c = 0
                    for j in tiles:
                        for i in range(j, NT):
                            o = SCORE_AT[i][2] + j * P
                            last = nc.tensor.transpose(bank[PT_BANKS[u]][:, c:c + P], prob[:, h % 4, o:o + P], ident[:])
                            c += P
                    last.then_inc(S["pe_pt"], 1)

            def weigh_values(h):
                pair = h // 2
                pe.wait_ge(S["pt_evac"], 3 * h + 3)
                if h == 4:
                    pe.wait_ge(S["pv_evac"], 1)
                if h == 0:
                    pe.wait_ge(S["y_evac"], 3)
                rows = slice(64 * (h % 2), 64 * (h % 2) + 64)
                for j in range(NT):
                    o = PT_AT[j]
                    last = mm(bank[5 + pair % 2][rows, j * P:T], vN[:, j, h * HD:(h + 1) * HD],
                              probT[:, h % 2, o:o + T - j * P], start=(j == 0), stop=(j == NT - 1))
                last.then_inc(S["pe_pv"], 1)

            pe.wait_ge(S["wup_in"], 16)
            for m in range(2):
                pe.wait_ge(S["kern_done"], m + 5)
                project(3 + m, w_up, m, "pe_pool")
            scores(0)
            pe.wait_ge(S["wv_in"], 16)
            v_tile(0, 5)
            v_tile(1, 6)
            scores(1)
            v_tile(2, 7)
            pe.wait_ge(S["pool_in_done"], 1)
            v_tile(3, 3)
            scores(2)
            pe.wait_ge(S["pool_ready"], 1)
            pe.wait_ge(S["wpl_in"], 64)
            for m, (signal, count) in enumerate([("pool_in_done", 2), ("v_done", 1)]):
                pe.wait_ge(S[signal], count)
                mm(bank[4 + m][:], w_pl[:, m, :], pl_s[:, 0, m, :], start=True, stop=True).then_inc(S["pe_pm"], 1)
            pe.wait_ge(S["s_moved"], 64)
            pe.wait_ge(S["m0_in"], 16 * CH)
            for m, (signal, count) in enumerate([("v_done", 2), ("v_done", 3), ("pool_mixed", 2)]):
                pe.wait_ge(S[signal], count)
                for i in range(8):
                    g = 8 * m + i
                    dst = bank[(6, 7, 5)[m]][:, i * NC:(i + 1) * NC]
                    mm(dst, m0[:, g].rearrange("p l h -> p (l h)"), uch[:, g, :], start=True, stop=False)
                    last = mm(dst, cp[:, g, 1:CH + 1, :].rearrange("p l h -> p (l h)"), s_in[:, g, :], start=False, stop=True)
                last.then_inc(S["pe_y"], 1)
                if m == 0:
                    scores(3)

            def glu(m, bank_i):
                for k in range(3):
                    last = mm(bank[bank_i][:], w_glu[:, k, m * P:(m + 1) * P], hdT[:, 5 + k, :], start=(k == 0), stop=(k == 2))
                last.then_inc(S["pe_glu"], 1)

            def mix_part(t, half, group):
                for i, k in enumerate(MIX_AT[group]):
                    last = mm(bank[WO_AT[half][group]][:], hdT[:, k, t * P:(t + 1) * P], w_o[:, k, half * 512:half * 512 + 512],
                              start=(i == 0), stop=(i == len(MIX_AT[group]) - 1))
                return last

            for h in range(4):
                turn_probs(h)
                if h + 4 < HEADS:
                    scores(h + 4)
                weigh_values(h)
            turn_probs(4)
            weigh_values(4)
            pe.wait_ge(S["wo_scaled"], 2)
            pe.wait_ge(S["s_read"], HEADS)
            mix_part(0, 0, 0)
            pe.wait_ge(S["gelu_done"], 3)
            pe.wait_ge(S["wglu_in"], 16)
            pe.wait_ge(S["pv_evac"], 2)
            for m in range(3):
                glu(m, (6, 0, 1)[m])
            turn_probs(5)
            weigh_values(5)
            mix_part(0, 1, 0)
            pe.wait_ge(S["wo_scaled"], KD)
            pe.wait_ge(S["ssm_done"], 3)
            pe.wait_ge(S["glu_sig"], 3)
            mix_part(0, 0, 1)
            mix_part(0, 1, 1)
            pe.wait_ge(S["pv_evac"], 3)
            mix_part(0, 0, 2).then_inc(S["pe_wo"], 1)
            pe.wait_ge(S["pt_evac"], 3 * HEADS)
            pe.wait_ge(S["sq_added"], 5)
            for g in range(3):
                for t in range(NT):
                    last = mm(bank[4][:, g * NT + t:g * NT + t + 1], ssum[g][:, t * P:(t + 1) * P], ones[:, 0:1], start=True, stop=True)
            last.then_inc(S["pe_sq"], 1)
            mix_part(0, 1, 2).then_inc(S["pe_wo"], 1)

            def out_proj(t):
                for half in range(2):
                    pe.wait_ge(S["wo_read"], 2 * t + half - 1)
                    for group in range(3):
                        last = mix_part(t, half, group)
                    last.then_inc(S["pe_wo"], 1)

            def turn_h(t):
                pe.wait_ge(S["h_ready"], t + 1)
                for u in range(2):
                    if t:
                        pe.wait_ge(S["hT_evac"], 2 * t - 1 + u)
                    elif u == 0:
                        pe.wait_ge(S["rms_sqrt"], 3)
                    for i in range(4):
                        last = nc.tensor.transpose(bank[4 + u][:, i * P:(i + 1) * P], xh[:, t, 4 * u + i:D:KD], ident[:])
                    last.then_inc(S["pe_hT"], 1)

            def ple(k):
                t, half = k // 2, k % 2
                if k >= 2:
                    pe.wait_ge(S["ple_done"], k - 1)
                else:
                    pe.wait_ge(S["wo_read"], 2 * NT - 1 + k)
                cols = slice(half * 512, half * 512 + 512)
                for c in range(KD):
                    last = mm(bank[PG_AT[k % 2]][:], hT[:, c, t * P:(t + 1) * P], w_pg[:, c, cols], start=(c == 0), stop=(c == KD - 1))
                last.then_inc(S["pe_pg"], 1)
                for c in range(2):
                    last = mm(bank[PP_AT[k % 2]][:], pT[:, c, t * P:(t + 1) * P], w_pp[:, c, cols], start=(c == 0), stop=(c == 1))
                last.then_inc(S["pe_pp"], 1)

            for t in range(1, NT):
                out_proj(t)
                turn_h(t - 1)
            pe.wait_ge(S["wpg_in"], 16)
            pe.wait_ge(S["wpp_in"], 32)
            pe.wait_ge(S["hT_evac"], 2)
            ple(0)
            turn_h(NT - 1)
            pe.wait_ge(S["hT_evac"], 2 * NT)
            pe.wait_ge(S["small_in"], 32)
            for k in range(KD):
                last = mm(bank[B_ROUTER][0:NE, :], w_rt[:, k, :], hT[:, k, :], start=(k == 0), stop=(k == KD - 1))
            last.then_inc(S["pe_rt"], 1)
            ple(1)
            pe.wait_ge(S["sig_rt"], 1)
            for t in range(NT):
                last = nc.tensor.transpose(bank[B_COUNT][:, t * NE:(t + 1) * NE], rtT[:, t * P:(t + 1) * P], ident[0:NE, 0:NE])
            last.then_inc(S["rt_by_token"], 1)
            ple(2)
            ple(3)
            pe.wait_ge(S["sel_ready"], 1)
            for t in range(NT):
                for s in range(t + 1):
                    mm(bank[B_COUNT][:, t * NE:(t + 1) * NE], (tri if s == t else ones)[:], r_sel[:, s, :], start=(s == 0), stop=(s == t))
            for s in range(NT):
                last = mm(bank[B_COUNT][:, NT * NE:(NT + 1) * NE], ones[:], r_sel[:, s, :], start=(s == 0), stop=(s == NT - 1))
            last.then_inc(S["pe_cnt"], 1)
            for k in range(4, 2 * NT):
                ple(k)

            def turn_tokens(r):
                for k in range(KD):
                    last = nc.tensor.transpose(bank[B_TOK[k // 4]][:, (k % 4) * P:(k % 4 + 1) * P], hg[:, r, k:D:KD], ident[:])
                return last

            def gate_up(b, r):
                w = ebuf[b][:, 0:4096].rearrange("p (u k n) -> p k u n", u=2, k=KD)
                for k in range(KD):
                    last = mm(bank[B_GU[r]][:].rearrange("p (u n) -> p u n", u=2), hgT[:, r, k, :], w[:, k], start=(k == 0), stop=(k == KD - 1))
                return last

            def gate_up_split(e, b, r):
                out_ = bank[B_GU[r]][:].rearrange("p (u n) -> p u n", u=2)
                w = ebuf[b][:, 0:4096].rearrange("p (u k n) -> p k u n", u=2, k=KD)
                w_hi = gu_hi[:].rearrange("p (u k n) -> p k u n", u=2, k=KS)
                for k in range(KD - KS):
                    mm(out_, hgT[:, r, k, :], w[:, k], start=(k == 0), stop=False)
                pe.wait_ge(S["gu_hi_set"], e + 1)
                for k in range(KS):
                    mm(out_, x_hi[r][:, k * P:(k + 1) * P], w_hi[:, k], start=False, stop=False)
                pe.wait_ge(S["gu_lo_set"], e + 1)
                for k in range(KS):
                    mm(out_, x_lo[:, k * P:(k + 1) * P], w_hi[:, k], start=False, stop=False)
                    w_lo = gu_lo[k // 2][:].rearrange("p (u k n) -> p k u n", u=2, k=2)[:, k % 2]
                    last = mm(out_, x_hi[r][:, k * P:(k + 1) * P], w_lo, start=False, stop=(k == KS - 1))
                return last

            def turn_act(r):
                for k in range(2):
                    last = nc.tensor.transpose(bank[B_ACT[r]][:, k * P:(k + 1) * P], act_e[:, r, 1, k:DE:2], ident[:])
                return last

            def down_split(r):
                for half in range(2):
                    terms = [(k, x, w) for k in range(2) for x, w in ((act_hi, dn_hi), (act_hi, dn_lo), (act_lo, dn_hi))]
                    for i, (k, x, w) in enumerate(terms):
                        last = mm(bank[B_DN[half]][:], x[r][:, k * P:(k + 1) * P], w[:, k * D + half * 512:k * D + half * 512 + 512],
                                  start=(i == 0), stop=(i == len(terms) - 1))
                return last

            def down(b, r):
                w = ebuf[b][:, 4096:6144].rearrange("p (k n) -> p k n", k=2)
                for half in range(2):
                    for k in range(2):
                        last = mm(bank[B_DN[half]][:], act_e[:, r, 2, k * P:(k + 1) * P], w[:, k, half * 512:half * 512 + 512],
                                  start=(k == 0), stop=(k == 1))
                return last

            def tokens_of(r, uses):
                pe.wait_ge(S[f"hg_in{r}"], 16 * uses)
                turn_tokens(r).then_inc(S["pe_hgT"], 1)

            def expert(e, b, loads, first=False, last=False):
                r = b % 2
                pe.wait_ge(S[f"e_in{b}"], 48 * loads)
                pe.wait_ge(S["hgT_evac"], 2 * e + 2)
                if not first:
                    pe.wait_ge(S["a_ready"], e)
                gate_up_split(e, b, r).then_inc(S["pe_gu"], 1)
                if not last:
                    tokens_of((b + 1) % 4, loads if b < 3 else loads + 1)
                if not first:
                    pe.wait_ge(S["aT_evac"], e)
                    if isinstance(e, int) and e == 1:
                        pe.wait_ge(S["ple_done"], 2 * NT)
                    else:
                        pe.wait_ge(S["ye_evac"], e - 1)
                    pe.wait_ge(S["dn_lo_set"], e)
                    down_split(1 - r).then_inc(S["pe_dn"], 1)
                pe.wait_ge(S["a_ready"], e + 1)
                turn_act(r).then_inc(S["pe_aT"], 1)

            pe.wait_ge(S["pe_pg"], 2 * NT)
            tokens_of(0, 1)
            pe.wait_ge(S["ple_done"], 2 * NT)
            for e in range(4):
                expert(e, e, 1, first=(e == 0))
            with pe.Fori(1, NE // 4 - 1) as blk:
                for b in range(4):
                    expert(4 * blk + b, b, blk + 1)
            for e in range(NE - 4, NE):
                expert(e, e % 4, NE // 4, last=(e == NE - 1))
            pe.wait_ge(S["aT_hi"], NE)
            pe.wait_ge(S["ye_evac"], NE - 1)
            down(3, 1).then_inc(S["pe_dn"], 1)
            n_over = pe.value_load(over_i[0:1, 0:1], min_val=0, max_val=OVER)
            pe.wait_ge(S["ye_evac"], NE)
            with pe.If(n_over > 0):
                with pe.Fori(0, OVER) as o:
                    with pe.If(o < n_over):
                        pe.wait_ge(S["o_hg"], 16 * (o + 1))
                        turn_tokens(0).then_inc(S["o_t"], 1)
                        pe.wait_ge(S["o_te"], 2 * (o + 1))
                        pe.wait_ge(S["o_in"], 48 * (o + 1))
                        gate_up(0, 0).then_inc(S["o_gu"], 1)
                        pe.wait_ge(S["o_a"], o + 1)
                        turn_act(0).then_inc(S["o_at"], 1)
                        pe.wait_ge(S["o_ae"], o + 1)
                        down(0, 0).then_inc(S["o_dn"], 1)

        @block.vector
        def _(dv):
            v = nc.vector
            tt, ts, stt = v.tensor_tensor, v.tensor_scalar, v.scalar_tensor_tensor
            n = [0]

            def link(ins):
                n[0] += 1
                ins.then_inc(S["dve_step"], 1)
                dv.wait_ge(S["dve_step"], n[0])

            def cmul(o_r, o_i, a_r, a_i, b_r, b_i, t):
                link(tt(t, a_i, b_i, ALU.mult))
                link(tt(o_r, a_r, b_r, ALU.mult))
                link(tt(o_r, o_r, t, ALU.subtract))
                link(tt(t, a_r, b_i, ALU.mult))
                link(tt(o_i, a_i, b_r, ALU.mult))
                link(tt(o_i, o_i, t, ALU.add))

            link(v.memset(eps_t[:], EPS))
            dv.wait_ge(S["par_in"], 16)
            dv.wait_ge(S["act_step"], 3)
            are, aim = par[:, C_ARE:C_ARE + NG], par[:, C_AIM:C_AIM + NG]
            link(tt(expo[:, 0:NG], are, dt_[:], ALU.mult))
            link(tt(ang[:, 0:NG], aim, dt_[:], ALU.mult))
            link(ts(expo[:, NG:NG + Q], expo[:, 0:Q], float(CH), None, ALU.mult))
            link(ts(ang[:, NG:NG + Q], ang[:, 0:Q], float(CH), None, ALU.mult))
            link(ts(turns[:], ang[:], 1.0 / (2 * np.pi), ROUND, ALU.mult, ALU.add))
            link(ts(turns[:], turns[:], -ROUND, None, ALU.add))
            for part in (PI2_A, PI2_B, PI2_C):
                link(stt(ang[:], turns[:], -part, ang[:], ALU.mult, ALU.add))
            ts(angr[:], ang[:], PI_SAFE, -PI_SAFE, ALU.min, ALU.max).then_inc(S["ang"], 1)
            dv.wait_ge(S["trig"], 1)
            link(tt(sinh[:], sinh[:], sinh[:], ALU.mult))
            link(ts(sinh[:], sinh[:], -2.0, 1.0, ALU.mult, ALU.add))
            link(v.tensor_copy(u8[:, 0, :], sinh[:, NG:NG + Q]))
            link(v.tensor_copy(u8[:, 1, :], sinf[:, NG:NG + Q]))
            v.tensor_copy(mag8[:], expo[:, NG:NG + Q]).then_inc(S["bx_ready"], 1)
            dv.wait_ge(S["bx_ready"], 1)
            pr, pi = pw[:, 0], pw[:, 1]
            link(v.memset(pr[:, :, 0:1], 1.0))
            link(v.memset(pi[:, :, 0:1], 0.0))
            link(tt(pr[:, :, 1], expo[:, 0:NG], sinh[:, 0:NG], ALU.mult))
            link(tt(pi[:, :, 1], expo[:, 0:NG], sinf[:, 0:NG], ALU.mult))
            nr, c1, c2, c3 = (sm[:, k * NG:(k + 1) * NG] for k in range(10, 14))
            link(ts(nr, pr[:, :, 1], -1.0, None, ALU.add))
            link(tt(c1, are, are, ALU.mult))
            link(tt(c2, aim, aim, ALU.mult))
            link(tt(c1, c1, c2, ALU.add))
            link(v.reciprocal(c1, c1))
            link(tt(c2, nr, are, ALU.mult))
            link(tt(c3, pi[:, :, 1], aim, ALU.mult))
            link(tt(c2, c2, c3, ALU.add))
            link(tt(c2, c2, c1, ALU.mult))
            link(tt(c3, pi[:, :, 1], are, ALU.mult))
            link(tt(nr, nr, aim, ALU.mult))
            link(tt(c3, c3, nr, ALU.subtract))
            link(tt(c3, c3, c1, ALU.mult))
            wide = [P, NG, GD]
            b_re = par[:, C_BRE:C_BIM].rearrange("p (g h) -> p g h", g=NG)
            b_im = par[:, C_BIM:C_CA].rearrange("p (g h) -> p g h", g=NG)
            t3 = tmp[:, 0:NG * GD].rearrange("p (g h) -> p g h", g=NG)
            cmul(bb[:, 0], bb[:, 1], b_re, b_im, c2.unsqueeze(2).broadcast_to(wide), c3.unsqueeze(2).broadcast_to(wide), t3)
            link(v.tensor_copy(b_st[0:64], bb[0:64, 0, Q:NG, :]))
            link(v.tensor_copy(b_st[64:P], bb[64:P, 1, Q:NG, :]))
            for lo, hi, by in ((2, 3, 1), (3, 5, 2), (5, 9, 4)):
                w = hi - lo
                t2 = tmp[:, 0:NG * w].rearrange("p (g l) -> p g l", g=NG)
                a_r, a_i = pr[:, :, lo - by:hi - by], pi[:, :, lo - by:hi - by]
                s_ = [P, NG, w]
                cmul(pr[:, :, lo:hi], pi[:, :, lo:hi], a_r, a_i,
                     pr[:, :, by:by + 1].broadcast_to(s_), pi[:, :, by:by + 1].broadcast_to(s_), t2)
            t4 = tmp[:, 0:Q * GD].rearrange("p (q h) -> p q h", q=Q)
            for j in range(CH):
                s_ = [P, Q, GD]
                l = CH - 1 - j
                cmul(bx[:, 0, :, j, :], bx[:, 1, :, j, :], bb[:, 0, 0:Q, :], bb[:, 1, 0:Q, :],
                     pr[:, 0:Q, l:l + 1].broadcast_to(s_), pi[:, 0:Q, l:l + 1].broadcast_to(s_), t4)
            v.engine_nop().then_inc(S["bx_ready"], 1)
            t5 = tmp[:, 0:3456].rearrange("p (g l h) -> p g l h", g=G, l=CH + 1)
            s_ = [P, G, CH + 1, GD]
            d1 = par[:, C_CA:C_CB].rearrange("p (g h) -> p g h", g=G).unsqueeze(2).broadcast_to(s_)
            d2 = par[:, C_CB:SSM_COLS].rearrange("p (g h) -> p g h", g=G).unsqueeze(2).broadcast_to(s_)
            link(tt(cp, d1, pr[:, Q:NG, :].unsqueeze(3).broadcast_to(s_), ALU.mult))
            link(tt(t5, d2, pi[:, Q:NG, :].unsqueeze(3).broadcast_to(s_), ALU.mult))
            tt(cp, cp, t5, ALU.add).then_inc(S["cp_ready"], 1)
            for k in range(6):
                dv.wait_ge(S["pe_bxT"], k + 1)
                r, q = k // 3, 4 * (k % 3)
                v.tensor_copy(bxT[:, r, q:q + 4, :], bank[1 + k][:].rearrange("p (q s) -> p q s", q=4)).then_inc(S["bxT_done"], 1)

            dv.wait_ge(S["pe_x"], 1)
            dv.wait_ge(S["rot_ready"], 1)
            half = Q // 2 * NC
            cosv, sinv = rot[:, 0, :, 0:NC], rot[:, 1, :, 0:NC]

            def qc(ap):
                return ap.rearrange("p (q c) -> p q c", c=NC)
            for u in range(2):
                xr, xi = qc(bank[5 + u][:, 0:half]), qc(bank[(7 + u) % 8][:, 0:half])
                cs, sn = cosv[:, 6 * u:6 * u + 6], sinv[:, 6 * u:6 * u + 6]
                cols = slice(u * half, (u + 1) * half)
                o_r, o_i = qc(x_rot[:, 0, cols]), qc(x_rot[:, 1, cols])
                t_r, t_i = qc(x_tmp[:, 0, cols]), qc(x_tmp[:, 1, cols])
                link(tt(o_r, xr, cs, ALU.mult))
                link(tt(t_r, xi, sn, ALU.mult))
                link(tt(o_i, xi, cs, ALU.mult))
                last = tt(t_i, xr, sn, ALU.mult)
                if u == 0:
                    link(last)
            last.then_inc(S["xrot_done"], 1)
            dv.wait_ge(S["xrot_done"], 1)
            link(tt(x_rot[:, 0, :], x_rot[:, 0, :], x_tmp[:, 0, :], ALU.add))
            link(tt(x_rot[:, 1, :], x_rot[:, 1, :], x_tmp[:, 1, :], ALU.subtract))
            for r in range(2):
                link(v.tensor_tensor_scan(x_rot[:, r, :], decay, x_rot[:, r, :], 0.0, ALU.mult, ALU.add))
            c0, c1_ = slice(0, NC - 1), slice(1, NC)
            s_r, s_i = qc(x_tmp[:, 0, :]), qc(x_tmp[:, 1, :])
            r_r, r_i = qc(x_rot[:, 0, :]), qc(x_rot[:, 1, :])
            tq = s_in.rearrange("p g c -> p (g c)")[:, 0:Q * NC].rearrange("p (q c) -> p q c", c=NC)
            link(v.memset(s_r[:, :, 0:1], 0.0))
            link(v.memset(s_i[:, :, 0:1], 0.0))
            link(tt(s_r[:, :, c1_], r_r[:, :, c0], cosv[:, :, c0], ALU.mult))
            link(tt(tq[:, :, c1_], r_i[:, :, c0], sinv[:, :, c0], ALU.mult))
            link(tt(s_r[:, :, c1_], s_r[:, :, c1_], tq[:, :, c1_], ALU.subtract))
            link(tt(s_i[:, :, c1_], r_i[:, :, c0], cosv[:, :, c0], ALU.mult))
            link(tt(tq[:, :, c1_], r_r[:, :, c0], sinv[:, :, c0], ALU.mult))
            tt(s_i[:, :, c1_], s_i[:, :, c1_], tq[:, :, c1_], ALU.add).then_inc(S["s_ready"], 1)

            def bias_max(h):
                dv.wait_ge(S["pe_s"], h + 1)
                if h == 0:
                    dv.wait_ge(S["rb_in"], 16)
                    dv.wait_ge(S["rot_ready"], 1)
                    dv.wait_ge(S["small_in"], 32)
                    dv.wait_ge(S["s_ready"], 1)
                if h == 3:
                    dv.wait_ge(S["s_moved"], 64)
                if h >= 4:
                    dv.wait_ge(S["pe_pt"], 3 * h - 9)
                r = h % 4
                for i in range(NT):
                    b, c, o = SCORE_AT[i]
                    old = max(i - 1, 0) * P
                    near = (i + 1) * P - old
                    if old:
                        link(ts(prob[:, r, o:o + old], bank[b][:, c:c + old], HD ** -0.5,
                                vec[:, V_RC + h:V_RC + h + 1], ALU.mult, ALU.add))
                    last = stt(prob[:, r, o + old:o + old + near], bank[b][:, c + old:c + old + near], HD ** -0.5,
                               rbias[:, h, 256 - near:256], ALU.mult, ALU.add)
                    if i < NT - 1:
                        link(last)
                last.then_inc(S["s_read"], 1)
                dv.wait_ge(S["s_read"], h + 1)
                for i in range(NT):
                    o, w = SCORE_AT[i][2], (i + 1) * P
                    last = v.tensor_reduce(att_mx[:, r, i:i + 1], prob[:, r, o:o + w], AX.X, ALU.max, negate=True)
                    if i < NT - 1:
                        link(last)
                last.then_inc(S["s_max"], 1)

            def normalise(h):
                dv.wait_ge(S["p_exp"], h + 1)
                r = h % 4
                link(v.reciprocal(att_sm[:, r, :], att_sm[:, r, :]))
                for i in range(NT):
                    o, w = SCORE_AT[i][2], (i + 1) * P
                    last = ts(prob[:, r, o:o + w], prob[:, r, o:o + w], att_sm[:, r, i:i + 1], None, ALU.mult)
                    if i < NT - 1:
                        link(last)
                last.then_inc(S["p_norm"], 1)

            bias_max(0)
            for h in range(HEADS):
                if h + 1 < HEADS:
                    bias_max(h + 1)
                normalise(h)
                if h == 4:
                    dv.wait_ge(S["y_back"], 16)
                    for m in range(3):
                        stt(yT[:, m, :], uT[:, m, :], vec[:, V_D + m:V_D + m + 1], yT[:, m, :], ALU.mult, ALU.add).then_inc(S["yin_ready"], 1)
            for m in range(3):
                dv.wait_ge(S["glu_sig"], m + 1)
                dv.wait_ge(S["pe_glu"], 3)
                tt(hdT[:, 5 + m, :], hdT[:, 5 + m, :], sgl[:, m, :], ALU.mult).then_inc(S["ssm_done"], 1)
            dv.wait_ge(S["rms_sqrt"], 3)
            link(v.reciprocal(rms_r[:], rms_r[:]))
            dv.wait_ge(S["ln_in"], 32)

            def normalise_rows(t, signal, sqrt_signal, count):
                link(v.reciprocal(ln_rs[:, t, 1:2], ln_rs[:, t, 0:1]))
                link(ts(xh[:, t, :], xh[:, t, :], ln_mv[:, t, 0:1], ln_rs[:, t, 1:2], ALU.subtract, ALU.mult))
                link(tt(xh[:, t, :], xh[:, t, :], lng, ALU.mult))
                tt(xh[:, t, :], xh[:, t, :], lnb, ALU.add).then_inc(S[signal], 1)

            for t in range(NT):
                dv.wait_ge(S["x_scaled"], t + 1)
                for half_ in range(2):
                    dv.wait_ge(S["pe_wo"], 2 * t + half_ + 1)
                    cols = slice(half_ * 512, half_ * 512 + 512)
                    for group in range(3):
                        last = stt(xh[:, t, cols], bank[WO_AT[half_][group]][:], rms_r[:, group, t:t + 1], xh[:, t, cols], ALU.mult, ALU.add)
                        if group < 2:
                            link(last)
                    last.then_inc(S["wo_read"], 1)
                    dv.wait_ge(S["wo_read"], 2 * t + half_ + 1)
                    link(v.bn_stats(ln_st[:, t, 6 * half_:6 * half_ + 6], xh[:, t, cols]))
                v.bn_aggr(ln_mv[:, t, :], ln_st[:, t, :]).then_inc(S["z_ready"], 1)
                dv.wait_ge(S["ln_sqrt"], t + 1)
                normalise_rows(t, "h_ready", "ln_sqrt", t + 1)

            def ple_sum(k):
                t, half_ = k // 2, k % 2
                dv.wait_ge(S["ple_sig"], k + 1)
                dv.wait_ge(S["pe_pp"], k + 1)
                if half_ == 0:
                    dv.wait_ge(S["pe_hT"], 2 * t + 2)
                    dv.wait_ge(S[f"h_out{t}"], 16)
                cols = slice(half_ * 512, half_ * 512 + 512)
                link(tt(ple_t[:, cols], ple_t[:, cols], bank[PP_AT[k % 2]][:], ALU.mult))
                stt(xh[:, t, cols], xh[:, t, cols], ALPHA, ple_t[:, cols], ALU.mult, ALU.add).then_inc(S["ple_done"], 1)
            ple_sum(0)
            ple_sum(1)

            W3 = [P, NT, NE]

            def view(k, n_=NT * NE):
                return rt[:, 64 * k:64 * k + n_]
            b_s = view(1).rearrange("p (t e) -> p t e", t=NT)
            pairs = rt[:, 128:128 + NT * EG * 6].rearrange("p (t g c) -> p t g c", t=NT, g=EG)
            gs = rt[:, 224:240].rearrange("p (t g) -> p t g", t=NT)
            key = rt[:, 240:256].rearrange("p (t g) -> p t g", t=NT)
            ingr = rt[:, 256:272].rearrange("p (t g) -> p t g", t=NT)
            m4 = rt[:, 272:276]
            m4b = rt[:, 276:280]
            wsum = rt[:, 280:284]
            msk = view(5).rearrange("p (t e) -> p t e", t=NT)
            tie = view(6).rearrange("p (t e) -> p t e", t=NT)
            sel = [view(7).rearrange("p (t e) -> p t e", t=NT), view(8).rearrange("p (t e) -> p t e", t=NT)]
            slot = view(9).rearrange("p (t e) -> p t e", t=NT)
            low = view(10).rearrange("p (t e) -> p t e", t=NT)
            tc = view(11).rearrange("p (t e) -> p t e", t=NT)
            dv.wait_ge(S["rt_by_token"], 1)
            link(v.tensor_copy(r_s, bank[B_COUNT][:, 0:NT * NE]))
            s_v = r_s.rearrange("p (t e) -> p t e", t=NT)
            link(tt(b_s, s_v, vec[:, V_RB:V_RB + NE].unsqueeze(1).broadcast_to(W3), ALU.add))
            bg = view(1).rearrange("p (t g c) -> p t g c", t=NT, g=EG)
            link(tt(pairs[:, :, :, 0:3], bg[:, :, :, 0:3], bg[:, :, :, 1:4], ALU.add))
            link(tt(pairs[:, :, :, 3:5], bg[:, :, :, 0:2], bg[:, :, :, 2:4], ALU.add))
            link(tt(pairs[:, :, :, 5:6], bg[:, :, :, 0:1], bg[:, :, :, 3:4], ALU.add))
            link(v.tensor_reduce(gs, pairs, AX.X, ALU.max))

            def first_max(out_, in_, mx, keyb, order, width):
                s__ = [P, NT, width]
                link(v.tensor_reduce(mx, in_, AX.X, ALU.max))
                link(tt(keyb, in_, mx.unsqueeze(2).broadcast_to(s__), ALU.is_equal))
                link(tt(keyb, keyb, order, ALU.mult))
                link(v.tensor_reduce(mx, keyb, AX.X, ALU.max))
                link(tt(out_, keyb, mx.unsqueeze(2).broadcast_to(s__), ALU.is_equal))

            link(ts(tc[:, 0, :], e_off[:], -1.0, float(NE * CAP), ALU.mult, ALU.add))
            link(v.tensor_copy(low, tc[:, 0:1, :].broadcast_to(W3)))
            first_max(ingr, gs, m4, key, low[:, :, 0:EG], EG)
            ig4 = ingr.unsqueeze(3).broadcast_to([P, NT, EG, EPG])
            mk4 = view(5).rearrange("p (t g c) -> p t g c", t=NT, g=EG)
            link(tt(mk4, bg, ig4, ALU.mult))
            link(ts(ingr, ingr, BIG, -BIG, ALU.mult, ALU.add))
            link(tt(mk4, mk4, ig4, ALU.add))
            for k in range(2):
                first_max(sel[k], msk, m4, tie, low, NE)
                link(tt(tie, s_v, sel[k], ALU.mult))
                link(v.tensor_reduce(wgt[:, k, :], tie, AX.X, ALU.add))
                if k == 0:
                    link(ts(tie, sel[0], -BIG, None, ALU.mult))
                    link(tt(msk, msk, tie, ALU.add))
            link(tt(wsum, wgt[:, 0, :], wgt[:, 1, :], ALU.add))
            link(v.reciprocal(wsum, wsum))
            for k in range(2):
                link(tt(wgt[:, k, :], wgt[:, k, :], wsum, ALU.mult))
            tt(r_sel, sel[0], sel[1], ALU.add).then_inc(S["sel_ready"], 1)
            ple_sum(2)
            dv.wait_ge(S["pe_cnt"], 1)
            cnt, more, cum, base = (rt[:, 768 + 16 * k:784 + 16 * k] for k in range(4))
            link(v.tensor_copy(cnt, bank[B_COUNT][:, NT * NE:(NT + 1) * NE]))
            link(ts(more, cnt, float(CAP), None, ALU.is_gt))
            for k in (2, 3):
                link(stt(more, cnt, float(CAP * k), more, ALU.is_gt, ALU.add))
            link(v.tensor_tensor_scan(cum, ones[:, 0:NE], more, 0.0, ALU.mult, ALU.add))
            link(tt(base, cum, more, ALU.subtract))
            link(ts(base, base, float(CAP), float((NE - 1) * CAP), ALU.mult, ALU.add))
            link(v.tensor_copy(slot, bank[B_COUNT][:, 0:NT * NE].rearrange("p (t e) -> p t e", t=NT)))
            link(ts(low, slot, float(CAP), None, ALU.is_lt))
            link(tt(cnt, e_off[:], base, ALU.subtract))
            link(tt(low, low, cnt.unsqueeze(1).broadcast_to(W3), ALU.mult))
            link(tt(slot, slot, low, ALU.add))
            link(tt(slot, slot, base.unsqueeze(1).broadcast_to(W3), ALU.add))
            for k in range(2):
                link(tt(tie, slot, sel[k], ALU.mult))
                link(v.tensor_reduce(m4b, tie, AX.X, ALU.add))
                last = v.tensor_copy(slot_i[:].rearrange("p (t k) -> p t k", k=2)[:, :, k], m4b)
                if k == 0:
                    link(last)
            last.then_inc(S["slots_ready"], 1)
            dv.wait_ge(S["slots_ready"], 1)
            le = rt[:, 832:832 + OVER * NE].rearrange("p (o e) -> p o e", o=OVER)
            ov = rt[:, 960:968]
            link(tt(le, cum.unsqueeze(1).broadcast_to([P, OVER, NE]), io_o[:].unsqueeze(2).broadcast_to([P, OVER, NE]), ALU.is_le))
            link(v.tensor_reduce(ov[:, 1:8], le, AX.X, ALU.add))
            link(v.tensor_copy(ov[:, 0:1], cum[:, NE - 1:NE]))
            link(ts(ov[:, 1:8], ov[:, 1:8], float(NE - 1), None, ALU.min))
            link(v.tensor_copy(over_i[:], ov[0:1, :]))

            ple_sum(3)
            ple_sum(4)
            dv.wait_ge(S["inv_back"], 16)
            ts(tok_t[:], inv_t[:], 1, None, ALU.arith_shift_right).then_inc(S["tok_ready"], 1)
            for k in range(5, 2 * NT):
                ple_sum(k)

            def y_copy(e, b, uses):
                dv.wait_ge(S["pe_dn"], e + 1)
                if not isinstance(uses, int) or uses > 1:
                    dv.wait_ge(S[f"ye_out{b}"], 16 * (uses - 1))
                v.tensor_copy(y_e[b][:, 0:512], bank[B_DN[0]][:])
                v.tensor_copy(y_e[b][:, 512:1024], bank[B_DN[1]][:]).then_inc(S["ye_evac"], 1)

            def gate_times_up(e, r):
                dv.wait_ge(S["silu_done"], e + 1)
                if not isinstance(e, int) or e >= 2:
                    dv.wait_ge(S["pe_aT"], e - 1)
                tt(act_e[:, r, 1, :], act_e[:, r, 0, :], bank[B_GU[r]][:, DE:2 * DE], ALU.mult).then_inc(S["a_ready"], 1)

            def gate_up_lower(e, b):
                dv.wait_ge(S["hgT_evac"], 2 * e + 2)
                tt(x_lo[:], bank[B_TOK[1]][:], x_hi[b % 2][:], ALU.subtract)
                dv.wait_ge(S["gu_hi_set"], e + 1)
                w = ebuf[b][:, 0:4096].rearrange("p (u n) -> p u n", u=2)
                w_hi = gu_hi[:].rearrange("p (u n) -> p u n", u=2)
                for i in range(2):
                    at = (KD - KS + 2 * i) * DE
                    last = tt(gu_lo[i][:].rearrange("p (u n) -> p u n", u=2), w[:, :, at:at + 2 * DE], w_hi[:, :, 2 * i * DE:2 * (i + 1) * DE], ALU.subtract)
                last.then_inc(S["gu_lo_set"], 1)

            def lower_parts(e, b):
                dv.wait_ge(S["aT_hi"], e + 1)
                tt(act_lo[b % 2][:], bank[B_ACT[b % 2]][:, 0:DE], act_hi[b % 2][:], ALU.subtract).then_inc(S["aT_evac"], 1)
                gate_up_lower(e + 1, (b + 1) % 4)
                dv.wait_ge(S["dn_hi_set"], e + 1)
                tt(dn_lo[:], ebuf[b][:, 4096:6144], dn_hi[:], ALU.subtract).then_inc(S["dn_lo_set"], 1)

            def step(e, b, uses, last=False):
                gate_times_up(e, b % 2)
                if uses is not None:
                    y_copy(e - 1, (b - 1) % 4, uses)
                if not last:
                    lower_parts(e, b)

            gate_up_lower(0, 0)
            step(0, 0, None)
            for e in range(1, 5):
                step(e, e % 4, 1)
            with dv.Fori(1, NE // 4 - 1) as blk:
                for i in range(1, 5):
                    step(4 * blk + i, i % 4, blk + 1)
            for e in range(NE - 3, NE):
                step(e, e % 4, NE // 4, last=(e == NE - 1))
            y_copy(NE - 1, 3, NE // 4)
            n_over = dv.value_load(over_i[0:1, 0:1], min_val=0, max_val=OVER)
            dv.wait_ge(S["ye_out0"], 16 * NE // 4)
            with dv.If(n_over > 0):
                with dv.Fori(0, OVER) as o:
                    with dv.If(o < n_over):
                        v.tensor_copy(cur_t[:, 0:1], tok_t[:, bass.ds(o + NE, 1)])
                        v.tensor_copy(cur_t[:, 1:2], inv_t[:, bass.ds(o + NE, 1)]).then_inc(S["o_col"], 1)
                        dv.wait_ge(S["o_si"], o + 1)
                        tt(act_e[:, 0, 1, :], act_e[:, 0, 0, :], bank[B_GU[0]][:, DE:2 * DE], ALU.mult).then_inc(S["o_a"], 1)
                        dv.wait_ge(S["o_dn"], o + 1)
                        v.tensor_copy(y_e[0][:, 0:512], bank[B_DN[0]][:]).then_inc(S["o_ye"], 1)
                        v.tensor_copy(y_e[0][:, 512:1024], bank[B_DN[1]][:]).then_inc(S["o_ye"], 1)
                        dv.wait_ge(S["o_out"], 16 * (o + 1))
                        dv.sem_inc(S["o_round"], 1)

            dv.wait_ge(S["ln2_in"], 32)

            def combine(t):
                for k in range(2):
                    dv.wait_ge(S[f"yk{k}_in{t}"], 16)
                    yk = RA[:, (2 * t + k) * D:(2 * t + k + 1) * D]
                    link(stt(xh[:, t, :], yk, wgt[:, k, t:t + 1], xh[:, t, :], ALU.mult, ALU.add,
                             accum_out=ln_st[:, t, 0:1] if k == 1 else None))
                ts(ln_mv[:, t, 0:1], ln_st[:, t, 0:1], -1.0 / D, None, ALU.mult).then_inc(S["z2_ready"], 1)

            def scale_rows(t):
                dv.wait_ge(S["ln2_sqrt"], t + 1)
                link(v.reciprocal(ln_rs[:, t, 1:2], ln_rs[:, t, 0:1]))
                tt(ln_mv[:, t, 0:1], ln_mv[:, t, 0:1], ln_rs[:, t, 1:2], ALU.mult).then_inc(S["rs2_ready"], 1)

            combine(0)
            combine(1)
            scale_rows(0)
            combine(2)
            scale_rows(1)
            combine(3)
            for t in range(2, NT):
                xg = RE[:, (t - 2) * D:(t - 1) * D]
                link(stt(xg, xh[:, t, :], ln_mv[:, t, 0:1], lng, ALU.add, ALU.mult))
                dv.wait_ge(S["ln2_sqrt"], t + 1)
                link(v.reciprocal(ln_rs[:, t, 1:2], ln_rs[:, t, 0:1]))
                stt(xh[:, t, :], xg, ln_rs[:, t, 1:2], lnb, ALU.mult, ALU.add).then_inc(S["o_dve"], 1)
            dv.wait_ge(S["gain_done"], 1)
            tt(xh[:, 1, :], xh[:, 1, :], lnb, ALU.add).then_inc(S["o_dve"], 1)


def _lay_out(inputs):
    a = {k: np.asarray(v) for k, v in inputs.items()}

    def pair(v):
        w = v.reshape(Q, 2, NS, -1).transpose(1, 2, 0, 3)
        return w.reshape(P, Q, -1)

    def stacked(re, im):
        w = np.stack([re, im]).reshape(2, G, NS, -1).transpose(0, 2, 1, 3)
        return w.reshape(P, G, -1)

    def both(v):
        return np.concatenate([pair(v), stacked(v, v)], axis=1).reshape(P, -1)

    ldt = np.repeat(a["ssm_log_dt"][0][:, None], NS, axis=1)
    c_re, c_im = (a[k][0].transpose(0, 2, 1) for k in ("ssm_c_re", "ssm_c_im"))
    par = np.concatenate([both(a["ssm_a_re"][0]), both(a["ssm_a_im"][0]), both(ldt), both(a["ssm_b_re"][0]), both(a["ssm_b_im"][0]),
                          stacked(c_re, c_im).reshape(P, -1), stacked(c_im, c_re).reshape(P, -1)], axis=1)

    def cols(v):
        return v.reshape(-1, P).T

    gains = np.concatenate([a["g_pool"][0], a["g_attn"][0], a["g_ssm"][0]])
    vec = np.concatenate([cols(a["ssm_d"][0]), cols(a["b_glu"][0]), cols(gains), cols(a["pool_scale"][0]),
                          np.repeat(a["router_bias"][None], P, axis=0), np.repeat(a["rel_bias"][0][:, -1][None], P, axis=0)], axis=1)
    rel = np.arange(P)[:, None] + P - np.arange(2 * P)[None, :]
    tab = a["rel_bias"][0][:, np.clip(rel, -REL, REL) + REL]
    windows = np.repeat([2, 4, 8, 16], 64).reshape(2, P).T[:, :, None]
    rcnt = (1.0 / np.minimum(np.arange(T) + 1, windows)).astype(np.float32)
    return {
        "xT": a["x"][0].T, "x": a["x"][0], "pT": a["p"][0, 0].T, "w_in": a["w_in"][0], "w_out": a["w_out"][0],
        "w_pool": a["w_pool"][0], "rel_tab": tab.transpose(1, 0, 2), "ssm_par": par, "vec": vec, "rcnt": rcnt,
        "w_glu": a["w_glu"][0], "w_router": a["w_router"],
        "ln": np.stack([a["ln1_g"][0], a["ln1_b"][0], a["ln2_g"][0], a["ln2_b"][0]]),
        "w_exp_gate": a["w_exp_gate"][0], "w_exp_up": a["w_exp_up"][0], "w_exp_down": a["w_exp_down"][0],
        "w_ple_gate": a["w_ple_gate"][0], "w_ple_proj": a["w_ple_proj"][0],
    }


def kernel(**inputs):
    import concourse.bacc as bacc
    from concourse.bass_utils import run_bass_kernel_spmd

    nc = bacc.Bacc("TRN2", target_bir_lowering=False, num_devices=1)
    arrays = {k: np.ascontiguousarray(v) for k, v in _lay_out(inputs).items()}
    io = {k: nc.dram_tensor("in_" + k, v.shape, mybir.dt.from_np(v.dtype), kind="ExternalInput").ap() for k, v in arrays.items()}
    out = nc.dram_tensor("out", (T, D), F32, kind="ExternalOutput").ap()
    trunk(nc, io, out)
    r = run_bass_kernel_spmd(nc, [{"in_" + k: v for k, v in arrays.items()}], core_ids=[0])
    return r.results[0]["out"].reshape(1, T, D)
```
